# Optimizing a Trainium2 kernel written in Bass

```python
import math
import jax, jax.numpy as jnp
from jax import lax
import numpy as np

D_MODEL = 1024
BATCH = 1
SEQ = 256
DEPTH = 1

HEAD_DIM = 64
ATT_WIDTH = D_MODEL // 2
RWKV_WIDTH = D_MODEL - ATT_WIDTH
ATT_HEADS = ATT_WIDTH // HEAD_DIM
RWKV_HEADS = RWKV_WIDTH // HEAD_DIM
MIX_WIDTH = ATT_WIDTH + RWKV_WIDTH
DILATED_PATTERNS = ((128, 1), (512, 4), (2048, 16))
DECAY_LORA = 64
AAA_LORA = 64
GATE_LORA = 128
SHIFT_WIDTH = 3 * RWKV_WIDTH + DECAY_LORA + AAA_LORA + GATE_LORA
IN_WIDTH = 3 * ATT_WIDTH + SHIFT_WIDTH
PEER_N_KEYS = 128
PEER_N_EXPERTS = PEER_N_KEYS * PEER_N_KEYS
PEER_HEADS = 8
PEER_KEY_DIM = 256
PEER_TOPK = 16
PEER_TOKEN_BLOCK = 128
NORM_EPS = 1e-6
LNX_EPS = 64e-5
MASK_VALUE = -1e30


def rms_norm(x, g, eps=NORM_EPS):
    x32 = x.astype(jnp.float32)
    y = x32 * lax.rsqrt(jnp.mean(x32 * x32, axis=-1, keepdims=True) + eps)
    return y * g.astype(jnp.float32)

def alibi_slopes(n_heads):
    return jnp.exp2(-8.0 * (jnp.arange(n_heads, dtype=jnp.float32) + 1.0) / n_heads)

def dilated_window_attention(q, k, v, slopes, window, dilation):
    B, S, H, E = q.shape
    d = dilation
    n = window // (2 * d)
    L = S // d
    nb = -(-L // n)
    Lp = nb * n
    qs = jnp.pad(q.reshape(B, L, d, H, E), ((0, 0), (0, Lp - L), (0, 0), (0, 0), (0, 0)))
    qs = qs.reshape(B, nb, n, d, H, E)

    def neighbourhood(t):
        tp = jnp.pad(t.reshape(B, L, d, H, E), ((0, 0), (n, Lp - L + n), (0, 0), (0, 0), (0, 0)))
        tp = tp.reshape(B, nb + 2, n, d, H, E)
        return jnp.concatenate([tp[:, :-2], tp[:, 1:-1], tp[:, 2:]], axis=2)

    kb = neighbourhood(k)
    vb = neighbourhood(v)
    qi = jnp.arange(nb)[:, None] * n + jnp.arange(n)[None, :]
    kj = (jnp.arange(nb)[:, None] - 1) * n + jnp.arange(3 * n)[None, :]
    off = kj[:, None, :] - qi[:, :, None]
    valid = (jnp.abs(off) <= n) & (kj[:, None, :] >= 0) & (kj[:, None, :] < L)
    dist = (d * jnp.abs(off)).astype(jnp.float32)

    s = jnp.einsum('bnqrhe,bnkrhe->bhrnqk', qs, kb) * (E ** -0.5)
    s = s - slopes[None, :, None, None, None, None] * dist[None, None, None]
    s = jnp.where(valid[None, None, None], s, MASK_VALUE)
    m = jnp.max(s, axis=-1, keepdims=True)
    p = jnp.exp(s - m)
    den = jnp.sum(p, axis=-1)
    lse = m[..., 0] + jnp.log(den)
    out = jnp.einsum('bhrnqk,bnkrhe->bnqrhe', p, vb)
    out = out / jnp.transpose(den, (0, 3, 4, 2, 1))[..., None]
    out = out.reshape(B, Lp, d, H, E)[:, :L].reshape(B, S, H, E)
    lse = jnp.transpose(lse, (0, 3, 4, 2, 1)).reshape(B, Lp, d, H)[:, :L].reshape(B, S, H)
    return out, lse

def dilated_mixture_attention(q, k, v):
    slopes = alibi_slopes(q.shape[2])
    outs, lses = [], []
    for window, dilation in DILATED_PATTERNS:
        o, l = dilated_window_attention(q, k, v, slopes, window, dilation)
        outs.append(o)
        lses.append(l)
    wts = jax.nn.softmax(jnp.stack(lses, axis=0), axis=0)
    return jnp.einsum('pbsh,pbshe->bshe', wts, jnp.stack(outs, axis=0))

def token_shift(z, mu_prev, mu_next):
    z_prev = jnp.pad(z, ((0, 0), (1, 0), (0, 0)))[:, :-1]
    z_next = jnp.pad(z, ((0, 0), (0, 1), (0, 0)))[:, 1:]
    return z + mu_prev * (z_prev - z) + mu_next * (z_next - z)

def wkv7_scan(r, w, k, v, kk, a, reverse):
    B, S, H, N = r.shape
    xs = tuple(jnp.moveaxis(t, 1, 0) for t in (r, w, k, v, kk, a))
    state0 = jnp.zeros((B, H, N, N), jnp.float32)

    def step(state, inp):
        r_t, w_t, k_t, v_t, kk_t, a_t = inp
        sa = jnp.einsum('bhvk,bhk->bhv', state, -kk_t)
        state = (state * w_t[:, :, None, :]
                 + sa[..., :, None] * (kk_t * a_t)[..., None, :]
                 + v_t[..., :, None] * k_t[..., None, :])
        y = jnp.einsum('bhvk,bhk->bhv', state, r_t)
        return state, y

    _, ys = lax.scan(step, state0, xs, reverse=reverse)
    return jnp.moveaxis(ys, 0, 1)

def rwkv7_bidirectional(r, k, v, xw, xa, xg, w_decay0, w_decay_up, a_gate0, a_gate_up,
                        g_up, k_k, k_a, r_k, lnx_g, lnx_b):
    B, S, _ = r.shape

    def hs(t):
        return t.reshape(B, S, RWKV_HEADS, HEAD_DIM)

    g = jax.nn.sigmoid(xg) @ g_up
    kk = hs(k * k_k)
    kk = kk * lax.rsqrt(jnp.maximum(jnp.sum(kk * kk, axis=-1, keepdims=True), 1e-12))
    ys, a_dirs = [], []
    for direction in range(2):
        w = -jax.nn.softplus(-(w_decay0[direction] + jnp.tanh(xw) @ w_decay_up[direction])) - 0.5
        decay = jnp.exp(-jnp.exp(w))
        a = jax.nn.sigmoid(a_gate0[direction] + xa @ a_gate_up[direction])
        k_dir = k * (1.0 + (a - 1.0) * k_a)
        ys.append(wkv7_scan(hs(r), hs(decay), hs(k_dir), hs(v), kk, hs(a), reverse=(direction == 1)))
        a_dirs.append(a)
    y = ys[0] + ys[1]
    mean = jnp.mean(y, axis=-1, keepdims=True)
    var = jnp.mean(jnp.square(y - mean), axis=-1, keepdims=True)
    yn = ((y - mean) * lax.rsqrt(var + LNX_EPS)).reshape(B, S, RWKV_WIDTH) * lnx_g + lnx_b
    k_bonus = hs(k * (1.0 + (0.5 * (a_dirs[0] + a_dirs[1]) - 1.0) * k_a))
    bonus = jnp.sum(hs(r) * k_bonus * r_k, axis=-1, keepdims=True) * hs(v)
    return (yn + bonus.reshape(B, S, RWKV_WIDTH)) * g

def peer_ffn(h, w_query, sub_keys1, sub_keys2, expert_u, expert_v):
    B, S, D = h.shape
    T = B * S
    half = PEER_KEY_DIM // 2
    x = h.reshape(T, D)
    q = (x @ w_query).astype(jnp.float32).reshape(T, PEER_HEADS, PEER_KEY_DIM)
    s1 = jnp.einsum('thd,nd->thn', q[..., :half], sub_keys1.astype(jnp.float32))
    s2 = jnp.einsum('thd,nd->thn', q[..., half:], sub_keys2.astype(jnp.float32))
    v1, i1 = lax.top_k(s1, PEER_TOPK)
    v2, i2 = lax.top_k(s2, PEER_TOPK)
    cand = (v1[..., :, None] + v2[..., None, :]).reshape(T, PEER_HEADS, PEER_TOPK * PEER_TOPK)
    top_s, top_p = lax.top_k(cand, PEER_TOPK)
    e_idx = (jnp.take_along_axis(i1, top_p // PEER_TOPK, axis=-1) * PEER_N_KEYS
             + jnp.take_along_axis(i2, top_p % PEER_TOPK, axis=-1))
    gate = jax.nn.softmax(top_s, axis=-1)
    HK = PEER_HEADS * PEER_TOPK
    nblk = T // PEER_TOKEN_BLOCK
    xb = x.reshape(nblk, PEER_TOKEN_BLOCK, D)
    ib = e_idx.reshape(nblk, PEER_TOKEN_BLOCK, HK)
    gb = gate.reshape(nblk, PEER_TOKEN_BLOCK, HK)

    def block(args):
        xc, ic, gc = args
        u = jnp.take(expert_u, ic, axis=0)
        act = jax.nn.gelu(jnp.einsum('cd,ced->ce', xc, u).astype(jnp.float32), approximate=False)
        vv = jnp.take(expert_v, ic, axis=0)
        return jnp.einsum('ce,ced->cd', (gc * act).astype(vv.dtype), vv)

    y = lax.map(block, (xb, ib, gb))
    return y.reshape(B, S, D)

def first_inputs(seed: int = 0) -> dict:
    key = jax.random.key(seed)
    ks = jax.random.split(key, 32)
    f32 = jnp.float32
    nrm = lambda k, shape, s: jax.random.normal(k, shape, f32) * s
    RW = RWKV_WIDTH
    return {
        "x": nrm(ks[0], (BATCH, SEQ, D_MODEL), 1.0),
        "c": nrm(ks[1], (BATCH, D_MODEL), 1.0),
        "ada_w": nrm(ks[2], (DEPTH, D_MODEL, 6 * D_MODEL), 0.5 * D_MODEL ** -0.5),
        "ada_b": nrm(ks[3], (DEPTH, 6 * D_MODEL), 0.1),
        "norm1_g": 1.0 + nrm(ks[4], (DEPTH, D_MODEL), 0.05),
        "w_in": nrm(ks[5], (DEPTH, D_MODEL, IN_WIDTH), D_MODEL ** -0.5),
        "mu_prev": jax.random.uniform(ks[6], (DEPTH, SHIFT_WIDTH), f32, 0.0, 0.5),
        "mu_next": jax.random.uniform(ks[7], (DEPTH, SHIFT_WIDTH), f32, 0.0, 0.5),
        "q_norm_g": 1.0 + nrm(ks[8], (DEPTH, HEAD_DIM), 0.05),
        "k_norm_g": 1.0 + nrm(ks[9], (DEPTH, HEAD_DIM), 0.05),
        "w_decay0": jax.random.uniform(ks[10], (DEPTH, 2, RW), f32, -5.0, -1.0),
        "w_decay_up": nrm(ks[11], (DEPTH, 2, DECAY_LORA, RW), 0.5 * DECAY_LORA ** -0.5),
        "a_gate0": nrm(ks[12], (DEPTH, 2, RW), 0.5),
        "a_gate_up": nrm(ks[13], (DEPTH, 2, AAA_LORA, RW), AAA_LORA ** -0.5),
        "g_up": nrm(ks[14], (DEPTH, GATE_LORA, RW), GATE_LORA ** -0.5),
        "k_k": 0.85 + nrm(ks[15], (DEPTH, RW), 0.05),
        "k_a": 1.0 + nrm(ks[16], (DEPTH, RW), 0.05),
        "r_k": nrm(ks[17], (DEPTH, RWKV_HEADS, HEAD_DIM), 0.1),
        "lnx_g": 1.0 + nrm(ks[18], (DEPTH, RW), 0.05),
        "lnx_b": nrm(ks[19], (DEPTH, RW), 0.01),
        "w_out": nrm(ks[20], (DEPTH, MIX_WIDTH, D_MODEL), MIX_WIDTH ** -0.5),
        "norm2_g": 1.0 + nrm(ks[21], (DEPTH, D_MODEL), 0.05),
        "peer_w_query": nrm(ks[22], (DEPTH, D_MODEL, PEER_HEADS * PEER_KEY_DIM), D_MODEL ** -0.5),
        "peer_sub_keys1": nrm(ks[23], (DEPTH, PEER_N_KEYS, PEER_KEY_DIM // 2), (PEER_KEY_DIM // 2) ** -0.5),
        "peer_sub_keys2": nrm(ks[24], (DEPTH, PEER_N_KEYS, PEER_KEY_DIM // 2), (PEER_KEY_DIM // 2) ** -0.5),
        "peer_u": nrm(ks[25], (DEPTH, PEER_N_EXPERTS, D_MODEL), D_MODEL ** -0.5),
        "peer_v": nrm(ks[26], (DEPTH, PEER_N_EXPERTS, D_MODEL), (PEER_HEADS * PEER_TOPK) ** -0.5),
    }

def first_block(x, c, ada_w, ada_b, norm1_g, w_in, mu_prev, mu_next, q_norm_g, k_norm_g,
              w_decay0, w_decay_up, a_gate0, a_gate_up, g_up, k_k, k_a, r_k, lnx_g, lnx_b,
              w_out, norm2_g, peer_w_query, peer_sub_keys1, peer_sub_keys2, peer_u, peer_v):
    in_dtype = x.dtype
    B, S, _ = x.shape
    A = ATT_WIDTH
    RW = RWKV_WIDTH
    for l in range(DEPTH):
        mod = (jax.nn.silu(c.astype(jnp.float32)) @ ada_w[l].astype(jnp.float32)
               + ada_b[l].astype(jnp.float32))[:, None, :]
        shift1, scale1, gate1, shift2, scale2, gate2 = jnp.split(mod, 6, axis=-1)

        h = rms_norm(x, norm1_g[l]) * (1.0 + scale1) + shift1
        z = (h.astype(in_dtype) @ w_in[l]).astype(jnp.float32)
        qa = rms_norm(z[..., :A].reshape(B, S, ATT_HEADS, HEAD_DIM), q_norm_g[l])
        ka = rms_norm(z[..., A:2 * A].reshape(B, S, ATT_HEADS, HEAD_DIM), k_norm_g[l])
        va = z[..., 2 * A:3 * A].reshape(B, S, ATT_HEADS, HEAD_DIM)
        att = dilated_mixture_attention(qa, ka, va).reshape(B, S, A)

        zr = token_shift(z[..., 3 * A:], mu_prev[l].astype(jnp.float32), mu_next[l].astype(jnp.float32))
        o1, o2, o3 = RW, 2 * RW, 3 * RW
        o4, o5 = o3 + DECAY_LORA, o3 + DECAY_LORA + AAA_LORA
        rw = rwkv7_bidirectional(
            zr[..., :o1], zr[..., o1:o2], zr[..., o2:o3],
            zr[..., o3:o4], zr[..., o4:o5], zr[..., o5:],
            w_decay0[l].astype(jnp.float32), w_decay_up[l].astype(jnp.float32),
            a_gate0[l].astype(jnp.float32), a_gate_up[l].astype(jnp.float32),
            g_up[l].astype(jnp.float32), k_k[l].astype(jnp.float32), k_a[l].astype(jnp.float32),
            r_k[l].astype(jnp.float32), lnx_g[l].astype(jnp.float32), lnx_b[l].astype(jnp.float32))
        mixed = jnp.concatenate([att, rw], axis=-1).astype(in_dtype) @ w_out[l]
        x = (x.astype(jnp.float32) + gate1 * mixed.astype(jnp.float32)).astype(in_dtype)

        h2 = (rms_norm(x, norm2_g[l]) * (1.0 + scale2) + shift2).astype(in_dtype)
        ff = peer_ffn(h2, peer_w_query[l], peer_sub_keys1[l], peer_sub_keys2[l], peer_u[l], peer_v[l])
        x = (x.astype(jnp.float32) + gate2 * ff.astype(jnp.float32)).astype(in_dtype)
    return x


DEPTH_2 = 2

ROPE_THETA = 10000.0
GM_HEADS = D_MODEL // 2 // HEAD_DIM
GM_CHUNK = 128
NSA_HEADS = D_MODEL // 2 // HEAD_DIM
NSA_KV = NSA_HEADS // 4
NSA_HPG = NSA_HEADS // NSA_KV
CMP_LEN = 32
CMP_STRIDE = 16
SEL_BLOCK = 64
SEL_TOPN = 8
WINDOW = 512
Q_BLOCK = 128
POOL_WIDTH = D_MODEL // 2
POOL_WINDOWS = (2, 4, 8, 16)
POOL_GROUP = POOL_WIDTH // len(POOL_WINDOWS)
S5_WIDTH = D_MODEL // 2
S5_GROUP_CH = 16
S5_GROUPS = S5_WIDTH // S5_GROUP_CH
S5_STATE = 64
FFN_DIM = ((8 * D_MODEL // 3 + 255) // 256) * 256
N_EVEN = (DEPTH_2 + 1) // 2
N_ODD = DEPTH_2 // 2
GM_W = GM_HEADS * HEAD_DIM
NSA_W = NSA_HEADS * HEAD_DIM
KV_W = NSA_KV * HEAD_DIM
EVEN_SPLITS = (GM_W, GM_W, NSA_W, KV_W, KV_W, KV_W, KV_W, KV_W, KV_W, 3 * NSA_HEADS)
EVEN_IN = sum(EVEN_SPLITS)
EVEN_OUT = GM_W + NSA_W
ODD_IN = POOL_WIDTH + S5_WIDTH
ODD_OUT = POOL_WIDTH + S5_WIDTH
RMS_EPS = 1e-6
LN_EPS = 1e-5
NEG_INF = -1e30
SEL_FORCE = 1e4


def rmsnorm(x, g):
    xf = x.astype(jnp.float32)
    y = xf * lax.rsqrt(jnp.mean(xf * xf, axis=-1, keepdims=True) + RMS_EPS)
    return (y * g.astype(jnp.float32)).astype(x.dtype)

def swiglu(h, w_gate, w_up, w_down):
    return (jax.nn.silu(h @ w_gate) * (h @ w_up)) @ w_down

def rope(x, pos):
    half = HEAD_DIM // 2
    inv = ROPE_THETA ** (-jnp.arange(half, dtype=jnp.float32) / half)
    ang = pos[:, None] * inv[None, :]
    cos, sin = jnp.cos(ang)[:, None, :], jnp.sin(ang)[:, None, :]
    xf = x.astype(jnp.float32)
    x1, x2 = xf[..., :half], xf[..., half:]
    return jnp.concatenate([x1 * cos - x2 * sin, x2 * cos + x1 * sin], axis=-1).astype(x.dtype)

def gmlp_spatial_gate(u, v, w_s, b):
    B, S = u.shape[0], u.shape[1]
    u = jax.nn.gelu(u)
    v = jax.nn.gelu(v).astype(jnp.float32)
    mu = jnp.mean(v, axis=-1, keepdims=True)
    var = jnp.mean(jnp.square(v - mu), axis=-1, keepdims=True)
    v = ((v - mu) * lax.rsqrt(var + LN_EPS)).astype(u.dtype)
    causal = jnp.tril(jnp.ones((GM_CHUNK, GM_CHUNK), dtype=w_s.dtype))
    vc = v.reshape(B, S // GM_CHUNK, GM_CHUNK, GM_HEADS, HEAD_DIM)
    s = jnp.einsum('hts,bcshd->bcthd', w_s * causal, vc) + b.T[None, None, :, :, None]
    return u * s.reshape(B, S, GM_HEADS, HEAD_DIM)

def nsa_compress(t, pe, w1, w2, idx):
    B = t.shape[0]
    nc = idx.shape[0]
    blocks = t[:, idx] + pe[:, None, :]
    flat = blocks.transpose(0, 1, 3, 2, 4).reshape(B, nc, NSA_KV, CMP_LEN * HEAD_DIM)
    return jax.nn.gelu(flat @ w1) @ w2

def nsa_attention(q, k_c, v_c, k_s, v_s, k_w, v_w, gate_logits, pe, w1, w2):
    B, S = q.shape[0], q.shape[1]
    G, HPG = NSA_KV, NSA_HPG
    scale = HEAD_DIM ** -0.5
    t = jnp.arange(S, dtype=jnp.int32)
    qg = q.reshape(B, S, G, HPG, HEAD_DIM)

    nc = (S - CMP_LEN) // CMP_STRIDE + 1
    cmp_start = jnp.arange(nc, dtype=jnp.int32) * CMP_STRIDE
    cidx = cmp_start[:, None] + jnp.arange(CMP_LEN, dtype=jnp.int32)[None, :]
    kc = nsa_compress(k_c, pe[0], w1[0], w2[0], cidx)
    vc = nsa_compress(v_c, pe[1], w1[1], w2[1], cidx)
    end_pos = cmp_start + (CMP_LEN - 1)
    kc = rope(kc, end_pos.astype(jnp.float32))
    s_c = jnp.einsum('btgqd,bngd->bgqtn', qg, kc).astype(jnp.float32) * scale
    valid_c = end_pos[None, :] <= t[:, None]
    s_c = jnp.where(valid_c, s_c, NEG_INF)
    p_c = jax.nn.softmax(s_c, axis=-1) * jnp.any(valid_c, axis=-1)[:, None].astype(jnp.float32)
    o_c = jnp.einsum('bgqtn,bngd->btgqd', p_c.astype(vc.dtype), vc)

    nsel = S // SEL_BLOCK
    blk_start = jnp.arange(nsel, dtype=jnp.int32) * SEL_BLOCK
    overlap = ((cmp_start[:, None] < blk_start[None, :] + SEL_BLOCK)
               & (cmp_start[:, None] + CMP_LEN > blk_start[None, :])).astype(jnp.float32)
    imp = jnp.einsum('bgqtn,nj->btgj', p_c, overlap)
    cur = t // SEL_BLOCK
    j = jnp.arange(nsel, dtype=jnp.int32)
    forced = (j[None, :] == 0) | (j[None, :] == cur[:, None]) | (j[None, :] == cur[:, None] - 1)
    causal_blk = blk_start[None, :] <= t[:, None]
    imp = jnp.where(forced[:, None, :], SEL_FORCE,
                    jnp.where(causal_blk[:, None, :], imp, -SEL_FORCE))
    n_top = min(SEL_TOPN, nsel)
    _, sel_idx = lax.top_k(imp, n_top)

    kb = k_s.reshape(B, nsel, SEL_BLOCK, G, HEAD_DIM).transpose(0, 3, 1, 2, 4)
    vb = v_s.reshape(B, nsel, SEL_BLOCK, G, HEAD_DIM).transpose(0, 3, 1, 2, 4)
    nq = S // Q_BLOCK
    q_chunks = qg.reshape(B, nq, Q_BLOCK, G, HPG, HEAD_DIM).transpose(1, 0, 2, 3, 4, 5)
    i_chunks = sel_idx.reshape(B, nq, Q_BLOCK, G, n_top).transpose(1, 0, 2, 3, 4)
    t_chunks = t.reshape(nq, Q_BLOCK)
    bi = jnp.arange(B)[:, None, None, None]
    gi = jnp.arange(G)[None, None, :, None]
    in_blk = jnp.arange(SEL_BLOCK, dtype=jnp.int32)

    def selected_block(args):
        q_i, idx_i, t_i = args
        ks = kb[bi, gi, idx_i]
        vs = vb[bi, gi, idx_i]
        kpos = idx_i[..., None] * SEL_BLOCK + in_blk
        s = jnp.einsum('btgqd,btgnld->btgqnl', q_i, ks).astype(jnp.float32) * scale
        mask = kpos <= t_i[None, :, None, None, None]
        s = jnp.where(mask[:, :, :, None], s, NEG_INF)
        s = s.reshape(B, Q_BLOCK, G, HPG, n_top * SEL_BLOCK)
        p = jax.nn.softmax(s, axis=-1).astype(vs.dtype)
        return jnp.einsum('btgqk,btgkd->btgqd', p, vs.reshape(B, Q_BLOCK, G, n_top * SEL_BLOCK, HEAD_DIM))

    o_s = lax.map(selected_block, (q_chunks, i_chunks, t_chunks))
    o_s = o_s.transpose(1, 0, 2, 3, 4, 5).reshape(B, S, G, HPG, HEAD_DIM)

    span = WINDOW + Q_BLOCK
    kp = jnp.pad(k_w, ((0, 0), (WINDOW, 0), (0, 0), (0, 0)))
    vp = jnp.pad(v_w, ((0, 0), (WINDOW, 0), (0, 0), (0, 0)))
    widx = jnp.arange(nq, dtype=jnp.int32)[:, None] * Q_BLOCK + jnp.arange(span, dtype=jnp.int32)[None, :]
    kw = kp[:, widx]
    vw = vp[:, widx]
    kpos = widx - WINDOW
    qw = qg.reshape(B, nq, Q_BLOCK, G, HPG, HEAD_DIM)
    s_w = jnp.einsum('bitgqd,bikgd->bigqtk', qw, kw).astype(jnp.float32) * scale
    diff = t_chunks[:, :, None] - kpos[:, None, :]
    wmask = (kpos[:, None, :] >= 0) & (diff >= 0) & (diff < WINDOW)
    s_w = jnp.where(wmask[None, :, None, None], s_w, NEG_INF)
    p_w = jax.nn.softmax(s_w, axis=-1).astype(vw.dtype)
    o_w = jnp.einsum('bigqtk,bikgd->bitgqd', p_w, vw).reshape(B, S, G, HPG, HEAD_DIM)

    g = jax.nn.sigmoid(gate_logits.astype(jnp.float32)).reshape(B, S, G, HPG, 3)
    o = g[..., 0:1] * o_c + g[..., 1:2] * o_s + g[..., 2:3] * o_w
    return o.reshape(B, S, NSA_W).astype(q.dtype)

def even_mixer(h, w_in, w_out, gm_w_s, gm_b, cmp_pe, cmp_w1, cmp_w2):
    B, S = h.shape[0], h.shape[1]
    z = h @ w_in
    cuts = list(np.cumsum(EVEN_SPLITS)[:-1])
    u, v, q, kc, vc, ks, vs, kw, vw, gl = jnp.split(z, cuts, axis=-1)
    heads = lambda a, n: a.reshape(B, S, n, HEAD_DIM)
    pos = jnp.arange(S, dtype=jnp.float32)
    out_a = gmlp_spatial_gate(heads(u, GM_HEADS), heads(v, GM_HEADS), gm_w_s, gm_b).reshape(B, S, GM_W)
    out_b = nsa_attention(rope(heads(q, NSA_HEADS), pos),
                          heads(kc, NSA_KV), heads(vc, NSA_KV),
                          rope(heads(ks, NSA_KV), pos), heads(vs, NSA_KV),
                          rope(heads(kw, NSA_KV), pos), heads(vw, NSA_KV),
                          gl, cmp_pe, cmp_w1, cmp_w2)
    return jnp.concatenate([out_a, out_b.astype(out_a.dtype)], axis=-1) @ w_out

def odd_mixer(h, w_in, w_out, pool_w, pool_scale, lam_re, lam_im, b_re, b_im, c_re, c_im, d_skip, log_dt, w_glu):
    B, S = h.shape[0], h.shape[1]
    z = h @ w_in
    zc, zd = z[..., :POOL_WIDTH], z[..., POOL_WIDTH:]
    t = jnp.arange(S, dtype=jnp.int32)

    n_grp = len(POOL_WINDOWS)
    zg = zc.reshape(B, S, n_grp, POOL_GROUP).astype(jnp.float32)
    cs = jnp.concatenate([jnp.zeros((B, 1, n_grp, POOL_GROUP), jnp.float32), jnp.cumsum(zg, axis=1)], axis=1)
    win = jnp.array(POOL_WINDOWS, dtype=jnp.int32)
    lo = jnp.maximum(t[:, None] + 1 - win[None, :], 0)
    lower = cs[:, lo, jnp.arange(n_grp)[None, :]]
    cnt = (t[:, None] + 1 - lo).astype(jnp.float32)
    pooled = (cs[:, 1:] - lower) / cnt[..., None] - zg
    y_c = jnp.einsum('bsgc,gcd->bsgd', pooled, pool_w.astype(jnp.float32))
    y_c = (y_c.reshape(B, S, POOL_WIDTH) * pool_scale.astype(jnp.float32)).astype(h.dtype)

    u = zd.reshape(B, S, S5_GROUPS, S5_GROUP_CH).astype(jnp.float32)
    lam = lax.complex(lam_re.astype(jnp.float32), lam_im.astype(jnp.float32))
    dt = jnp.exp(log_dt.astype(jnp.float32))[:, None]
    lam_bar = jnp.exp(lam * dt)
    b_c = lax.complex(b_re.astype(jnp.float32), b_im.astype(jnp.float32))
    c_c = lax.complex(c_re.astype(jnp.float32), c_im.astype(jnp.float32))
    b_bar = ((lam_bar - 1.0) / lam)[..., None] * b_c
    bu = jnp.einsum('gpc,bsgc->sbgp', b_bar, u.astype(jnp.complex64))
    a = jnp.broadcast_to(lam_bar, (S, 1, S5_GROUPS, S5_STATE))

    def combine(e1, e2):
        a1, b1 = e1
        a2, b2 = e2
        return a2 * a1, a2 * b1 + b2

    _, states = lax.associative_scan(combine, (a, bu), axis=0)
    y = jnp.einsum('gcp,sbgp->bsgc', c_c, states).real + d_skip.astype(jnp.float32) * u
    y = jax.nn.gelu(y.reshape(B, S, S5_WIDTH))
    ab = y @ w_glu.astype(jnp.float32)
    y_d = (ab[..., :S5_WIDTH] * jax.nn.sigmoid(ab[..., S5_WIDTH:])).astype(h.dtype)

    return jnp.concatenate([y_c, y_d], axis=-1) @ w_out

def second_inputs(seed: int = 0) -> dict:
    key = jax.random.key(seed)
    k = jax.random.split(key, 26)
    f32 = jnp.float32
    nrm = lambda kk, shape, sc: jax.random.normal(kk, shape, f32) * sc
    lam_im = jnp.pi * jnp.broadcast_to(jnp.arange(S5_STATE, dtype=f32), (N_ODD, S5_GROUPS, S5_STATE))
    return {
        'x': nrm(k[0], (BATCH, SEQ, D_MODEL), 1.0),
        'norm_w': 1.0 + nrm(k[1], (DEPTH_2, 3, D_MODEL), 0.01),
        'ffn_w_gate': nrm(k[2], (DEPTH_2, 2, D_MODEL, FFN_DIM), D_MODEL ** -0.5),
        'ffn_w_up': nrm(k[3], (DEPTH_2, 2, D_MODEL, FFN_DIM), D_MODEL ** -0.5),
        'ffn_w_down': nrm(k[4], (DEPTH_2, 2, FFN_DIM, D_MODEL), FFN_DIM ** -0.5),
        'final_norm_w': 1.0 + nrm(k[5], (D_MODEL,), 0.01),
        'ev_w_in': nrm(k[6], (N_EVEN, D_MODEL, EVEN_IN), D_MODEL ** -0.5),
        'ev_w_out': nrm(k[7], (N_EVEN, EVEN_OUT, D_MODEL), EVEN_OUT ** -0.5),
        'gm_w_s': nrm(k[8], (N_EVEN, GM_HEADS, GM_CHUNK, GM_CHUNK), GM_CHUNK ** -0.5),
        'gm_b': 1.0 + nrm(k[9], (N_EVEN, GM_HEADS, GM_CHUNK), 0.01),
        'nsa_cmp_pe': nrm(k[10], (N_EVEN, 2, CMP_LEN, HEAD_DIM), 0.02),
        'nsa_cmp_w1': nrm(k[11], (N_EVEN, 2, CMP_LEN * HEAD_DIM, HEAD_DIM), (CMP_LEN * HEAD_DIM) ** -0.5),
        'nsa_cmp_w2': nrm(k[12], (N_EVEN, 2, HEAD_DIM, HEAD_DIM), HEAD_DIM ** -0.5),
        'od_w_in': nrm(k[13], (N_ODD, D_MODEL, ODD_IN), D_MODEL ** -0.5),
        'od_w_out': nrm(k[14], (N_ODD, ODD_OUT, D_MODEL), ODD_OUT ** -0.5),
        'pool_w': nrm(k[15], (N_ODD, len(POOL_WINDOWS), POOL_GROUP, POOL_GROUP), POOL_GROUP ** -0.5),
        'pool_scale': 1.0 + nrm(k[16], (N_ODD, POOL_WIDTH), 0.02),
        's5_lam_re': -0.5 + nrm(k[17], (N_ODD, S5_GROUPS, S5_STATE), 0.01),
        's5_lam_im': lam_im + nrm(k[18], (N_ODD, S5_GROUPS, S5_STATE), 0.01),
        's5_b_re': nrm(k[19], (N_ODD, S5_GROUPS, S5_STATE, S5_GROUP_CH), (2 * S5_GROUP_CH) ** -0.5),
        's5_b_im': nrm(k[20], (N_ODD, S5_GROUPS, S5_STATE, S5_GROUP_CH), (2 * S5_GROUP_CH) ** -0.5),
        's5_c_re': nrm(k[21], (N_ODD, S5_GROUPS, S5_GROUP_CH, S5_STATE), (2 * S5_STATE) ** -0.5),
        's5_c_im': nrm(k[22], (N_ODD, S5_GROUPS, S5_GROUP_CH, S5_STATE), (2 * S5_STATE) ** -0.5),
        's5_d': nrm(k[23], (N_ODD, S5_GROUPS, S5_GROUP_CH), 1.0),
        's5_log_dt': jax.random.uniform(k[24], (N_ODD, S5_GROUPS), f32, float(np.log(1e-3)), float(np.log(1e-1))),
        's5_w_glu': nrm(k[25], (N_ODD, S5_WIDTH, 2 * S5_WIDTH), S5_WIDTH ** -0.5),
    }

def second_block(x, norm_w, ffn_w_gate, ffn_w_up, ffn_w_down, final_norm_w, ev_w_in, ev_w_out,
              gm_w_s, gm_b, nsa_cmp_pe, nsa_cmp_w1, nsa_cmp_w2, od_w_in, od_w_out, pool_w, pool_scale,
              s5_lam_re, s5_lam_im, s5_b_re, s5_b_im, s5_c_re, s5_c_im, s5_d, s5_log_dt, s5_w_glu):
    for l in range(DEPTH_2):
        x = x + 0.5 * swiglu(rmsnorm(x, norm_w[l, 0]), ffn_w_gate[l, 0], ffn_w_up[l, 0], ffn_w_down[l, 0])
        h = rmsnorm(x, norm_w[l, 1])
        i = l // 2
        if l % 2 == 0:
            m = even_mixer(h, ev_w_in[i], ev_w_out[i], gm_w_s[i], gm_b[i],
                           nsa_cmp_pe[i], nsa_cmp_w1[i], nsa_cmp_w2[i])
        else:
            m = odd_mixer(h, od_w_in[i], od_w_out[i], pool_w[i], pool_scale[i],
                          s5_lam_re[i], s5_lam_im[i], s5_b_re[i], s5_b_im[i], s5_c_re[i], s5_c_im[i],
                          s5_d[i], s5_log_dt[i], s5_w_glu[i])
        x = x + m.astype(x.dtype)
        x = x + 0.5 * swiglu(rmsnorm(x, norm_w[l, 2]), ffn_w_gate[l, 1], ffn_w_up[l, 1], ffn_w_down[l, 1])
    return rmsnorm(x, final_norm_w)


_first_inputs = second_inputs


def second_inputs(seed=0):
    import zlib

    import numpy as np

    out = dict(_first_inputs(seed))
    spreads = {}
    factors = {'norm_w': 14.117,
     'final_norm_w': 156.403,
     'gm_b': 200.0,
     'nsa_cmp_pe': 200.0,
     'pool_scale': 145.979,
     's5_lam_re': 64.0,
     's5_lam_im': 39.656,
     's5_b_re': 54.808,
     's5_b_im': 54.752,
     's5_c_re': 55.736,
     's5_c_im': 55.088,
     's5_log_dt': 41.728,
     'gm_w_s': 3.254,
     'nsa_cmp_w1': 4.485,
     'nsa_cmp_w2': 3.747,
     's5_d': 5.232,
     's5_w_glu': 4.372}
    for name, (base, spread) in spreads.items():
        noise = np.random.default_rng([zlib.crc32(name.encode()), seed]).standard_normal(out[name].shape)
        drawn = base * np.exp(spread * noise) if base else spread * noise
        out[name] = __import__('jax').numpy.asarray(drawn.astype(out[name].dtype))
    for name, factor in factors.items():
        out[name] = (out[name] * factor).astype(out[name].dtype)
    return out


_narrow_inputs = second_inputs


def second_inputs(seed=0):
    out = dict(_narrow_inputs(seed))
    wider = {'final_norm_w': 6.06, 'gm_w_s': 5.01, 'gm_b': 6.04, 'pool_scale': 5.31}
    for name, times in wider.items():
        mean = out[name].mean()
        out[name] = (mean + times * (out[name] - mean)).astype(out[name].dtype)
    return out


def setup_inputs(seed=0):
    out = dict(first_inputs(seed))
    for name, value in second_inputs(seed + 1).items():
        if name != "x":
            out[name + "_2"] = value
    return out


def reference(
    x, c, ada_w, ada_b, norm1_g, w_in, mu_prev, mu_next, q_norm_g, k_norm_g, w_decay0,
    w_decay_up, a_gate0, a_gate_up, g_up, k_k, k_a, r_k, lnx_g, lnx_b, w_out, norm2_g,
    peer_w_query, peer_sub_keys1, peer_sub_keys2, peer_u, peer_v, norm_w_2, ffn_w_gate_2,
    ffn_w_up_2, ffn_w_down_2, final_norm_w_2, ev_w_in_2, ev_w_out_2, gm_w_s_2, gm_b_2,
    nsa_cmp_pe_2, nsa_cmp_w1_2, nsa_cmp_w2_2, od_w_in_2, od_w_out_2, pool_w_2, pool_scale_2,
    s5_lam_re_2, s5_lam_im_2, s5_b_re_2, s5_b_im_2, s5_c_re_2, s5_c_im_2, s5_d_2, s5_log_dt_2,
    s5_w_glu_2,
):
    x = first_block(
        x, c, ada_w, ada_b, norm1_g, w_in, mu_prev, mu_next, q_norm_g, k_norm_g, w_decay0,
        w_decay_up, a_gate0, a_gate_up, g_up, k_k, k_a, r_k, lnx_g, lnx_b, w_out, norm2_g,
        peer_w_query, peer_sub_keys1, peer_sub_keys2, peer_u, peer_v,
    )
    return second_block(
        x, norm_w_2, ffn_w_gate_2, ffn_w_up_2, ffn_w_down_2, final_norm_w_2, ev_w_in_2,
        ev_w_out_2, gm_w_s_2, gm_b_2, nsa_cmp_pe_2, nsa_cmp_w1_2, nsa_cmp_w2_2, od_w_in_2,
        od_w_out_2, pool_w_2, pool_scale_2, s5_lam_re_2, s5_lam_im_2, s5_b_re_2, s5_b_im_2,
        s5_c_re_2, s5_c_im_2, s5_d_2, s5_log_dt_2, s5_w_glu_2,
    )


_drawn_inputs = setup_inputs


def setup_inputs(seed=0):
    import zlib

    import numpy as np

    out = dict(_drawn_inputs(seed))
    spreads = {}
    factors = {'norm1_g': 2.911,
     'q_norm_g': 8.0,
     'k_norm_g': 8.0,
     'w_decay_up': 5.082,
     'k_k': 3.239,
     'lnx_g': 5.521,
     'lnx_b': 31.437,
     'norm2_g': 7.29}
    for name, (base, spread) in spreads.items():
        noise = np.random.default_rng([zlib.crc32(name.encode()), seed]).standard_normal(out[name].shape)
        drawn = base * np.exp(spread * noise) if base else spread * noise
        out[name] = __import__('jax').numpy.asarray(drawn.astype(out[name].dtype))
    for name, factor in factors.items():
        out[name] = (out[name] * factor).astype(out[name].dtype)
    return out
```

```python
from contextlib import ExitStack, contextmanager

import numpy as np

import concourse.bass as bass
from concourse import mybir

F32 = mybir.dt.float32
U32 = mybir.dt.uint32
ACT = mybir.ActivationFunctionType
ALU = mybir.AluOpType
AXX = mybir.AxisListType.X

P = 128
S = 256
TT = S // P
D = 1024
KT = D // P
HD = 64
NH = 8
RING = 6
FFN = 2816
FJ = FFN // P
NE = 128
TOPK = 16
SLOTS = NH * TOPK
NEG = -1e30
NC_CMP = (S - 32) // 16 + 1
S5T = 16
NORM_EPS = 1e-6

T_ADA, T_IN_TOK, T_IN, T_OUT, T_QUERY = 48, 4, 22, 8, 16
T_FFN = 3 * FJ
T_EV_TOK, T_EV, T_GLU = 7, 12, 4
TOTAL = (T_ADA + T_IN_TOK + T_IN + T_OUT + T_QUERY + 4 * T_FFN + T_EV_TOK + T_EV + T_OUT + KT + T_GLU + KT)

VEC = {}
_at = 0
for _name, _n in (("c", 8), ("ada_b", 48), ("norm1_g", 8), ("mu_prev", 14), ("mu_next", 14), ("w_decay0", 8), ("a_gate0", 8),
                  ("k_k", 4), ("k_a", 4), ("r_k", 4), ("lnx_g", 4), ("lnx_b", 4), ("norm2_g", 8), ("q_norm_g", 1),
                  ("k_norm_g", 1), ("norm_w", 48), ("final", 8), ("pool_scale", 4), ("s5_d", 4), ("lam_re", S5T),
                  ("lam_im", S5T), ("log_dt", S5T)):
    VEC[_name] = (_at, _at + _n)
    _at += _n
NVEC = _at

MATS = ["ident", "ones", "blockones", "rotate"]
for _d in range(2):
    MATS += [f"strict{_d}", f"upto{_d}"] + [f"level{_d}_{b}" for b in (1, 2, 4, 8, 16, 32, 64)]
MATS += ["level_row0", "level_row1"]
MAT = {n: i for i, n in enumerate(MATS)}


def constant_matrices():
    t = np.arange(P)
    a, b = t[:, None], t[None, :]
    out = np.zeros((len(MATS), P, P), np.float32)
    out[MAT["ident"]] = a == b
    out[MAT["ones"]] = 1
    out[MAT["blockones"]] = a // HD == b // HD
    half = HD // 2
    rot = np.zeros((P, P), np.float32)
    for m in range(P):
        rot[(m + half, m) if m % HD < half else (m - half, m)] = -1 if m % HD < half else 1
    out[MAT["rotate"]] = rot
    for d in range(2):
        later = (b > a) if d == 0 else (b < a)
        out[MAT[f"strict{d}"]] = later
        out[MAT[f"upto{d}"]] = later | (a == b)
        for n in (1, 2, 4, 8, 16, 32, 64):
            out[MAT[f"level{d}_{n}"]] = later & (a // (2 * n) == b // (2 * n)) & (a // n != b // n)
        out[MAT[f"level_row{d}"]] = out[MAT[f"level{d}_1"]].T
    return out


class counter:
    def __init__(self):
        self.now = 0

    def __call__(self):
        self.now += 1
        return self.now

    def one(self):
        self.now += 1
        return 1


def over_tiles(eng, first, count, body):
    turns = count // RING if count >= 2 * RING else 0
    if turns:
        with eng.Fori(0, turns) as g:
            for u in range(RING):
                body(g * RING + u, (first + u) % RING, g + (first + u) // RING)
    for i in range(turns * RING, count):
        body(i, (first + i) % RING, (first + i) // RING)


def build(nc, A):
    with ExitStack() as ctx:
        def sb(name, shape, dt=F32, where=ctx):
            return where.enter_context(nc.sbuf_tensor(name, shape, dt))

        def sem(name):
            return ctx.enter_context(nc.semaphore(name))

        ring = sb("ring", [P, RING, D])
        xT = sb("xT", [P, KT, S])
        hT = sb("hT", [P, KT, S])
        mix = sb("mix", [P, KT, S])
        sq = sb("sq", [P, KT, S])
        rstd = sb("rstd", [P, S])
        vecs = sb("vecs", [P, NVEC])
        mats = sb("mats", [P, len(MATS), P])
        mod = sb("mod", [P, 48])
        gs = sb("gs", [P, 2, KT])
        ps = ctx.enter_context(nc.psum_tensor("ps", [P, 8, 512], F32))

        loaded = [sem(f"tile_loaded{i}") for i in range(RING)]
        tiles_used = sem("tiles_used")
        consts_in = sem("consts_in")
        table_in = sem("table_in")
        stored = sem("stored")
        tables = counter()
        sets = [[sem(f"stage{j}_{i}") for i in range(14)] for j in range(2)]
        stages = [0]
        stream = [0]

        def vec(name, i=0):
            return vecs[:, VEC[name][0] + i:VEC[name][0] + i + 1]

        def vec_all(name):
            return vecs[:, VEC[name][0]:VEC[name][1]]

        def mat(name):
            return mats[:, MAT[name], :]

        @contextmanager
        def stage():
            mine, other = sets[stages[0] % 2], sets[1 - stages[0] % 2]
            again = stages[0] > 0
            stages[0] += 1
            with nc.Block() as block:
                if again:
                    @block.gpsimd
                    def _(pool):
                        pool.sem_clear(range(other[0].num, other[0].num + len(other)))
                yield block, mine

        def take(count):
            stream[0] += count
            return stream[0] - count

        def refill(sp, first, count):
            def load(i, slot, turn):
                sp.wait_ge(tiles_used, i + (first + 1))
                sp.dma_start(ring[:, slot, :], A["stream"][bass.ds(i + (first + RING), 1)]
                             .rearrange("a p n -> (a p) n")).then_inc(loaded[slot], 16)
            over_tiles(sp, first, min(count, TOTAL - RING - first), load)

        with stage() as (block, _):
            @block.sync
            def _(sp):
                for i in range(RING):
                    sp.dma_start(ring[:, i, :], A["stream"][i]).then_inc(loaded[i], 16)

            @block.scalar
            def _(act):
                act.dma_start(vecs[:, :], A["vecs"]).then_inc(consts_in, 16)
                act.dma_start(xT[:, :, :], A["xT"].rearrange("(k p) t -> p k t", p=P)).then_inc(consts_in, 16)
                act.dma_start(mats[:, :, :], A["mats"].rearrange("m p n -> p m n")).then_inc(consts_in, 16)
                act.wait_ge(consts_in, 48)

        with ExitStack() as tmp, stage() as (block, (c_ready, *_)):
            cs = sb("cs", [P, KT], where=tmp)
            first = take(T_ADA)

            @block.sync
            def _(sp):
                refill(sp, first, T_ADA)

            @block.scalar
            def _(act):
                nc.scalar.activation(cs[:, :], vec_all("c"), ACT.Silu).then_inc(c_ready, 1)

            @block.tensor
            def _(pe):
                pe.wait_ge(c_ready, 1)

                def tile(i, slot, turn):
                    pe.wait_ge(loaded[slot], turn * 16 + 16)
                    for k in range(KT):
                        last = nc.tensor.matmul(ps[:, 0, bass.ds(i, 1)], ring[:, slot, k * P:(k + 1) * P],
                                                cs[:, k:k + 1], start=(k == 0), stop=(k == KT - 1))
                    last.then_inc(tiles_used, 1)
                over_tiles(pe, first, T_ADA, tile)

            @block.vector
            def _(dve):
                dve.wait_ge(tiles_used, first + T_ADA)
                nc.vector.tensor_tensor(mod[:, :], ps[:, 0, 0:48], vec_all("ada_b"), ALU.add).then_inc(c_ready, 1)
                dve.wait_ge(c_ready, 2)
                for n, name in ((0, "norm1_g"), (1, "norm2_g")):
                    nc.vector.scalar_tensor_tensor(gs[:, n, :], mod[:, 24 * n + 8:24 * n + 16], 1.0, vec_all(name),
                                                   ALU.add, ALU.mult)

        def rms_norm(gain, shift):
            with stage() as (block, (squared, summed, scaled, root, v, *_)):
                @block.scalar
                def _(act):
                    nc.scalar.activation(sq[:, :, :], xT[:, :, :], ACT.Square).then_inc(squared, 1)
                    act.wait_ge(scaled, 1)
                    nc.scalar.activation(rstd[:, :], rstd[:, :], ACT.Sqrt).then_inc(root, 1)

                @block.tensor
                def _(pe):
                    pe.wait_ge(squared, 1)
                    for k in range(KT):
                        last = nc.tensor.matmul(ps[:, 0, 0:S], mat("ones"), sq[:, k, :], start=(k == 0),
                                                stop=(k == KT - 1))
                    last.then_inc(summed, 1)

                @block.vector
                def _(dve):
                    n = counter()
                    dve.wait_ge(summed, 1)
                    nc.vector.tensor_scalar(rstd[:, :], ps[:, 0, 0:S], 1.0 / D, NORM_EPS, ALU.mult,
                                            ALU.add).then_inc(scaled, 1)
                    dve.wait_ge(root, 1)
                    nc.vector.reciprocal(rstd[:, :], rstd[:, :]).then_inc(v, 1)
                    dve.wait_ge(v, n())
                    for k in range(KT):
                        nc.vector.scalar_tensor_tensor(hT[:, k, :], xT[:, k, :], gain(k), rstd[:, :], ALU.mult,
                                                       ALU.mult).then_inc(v, 1)
                        if shift:
                            dve.wait_ge(v, n())
                            nc.vector.tensor_scalar(hT[:, k, :], hT[:, k, :], shift(k), None, ALU.add)

        def project(count, src, evacuate, tok_count=0, tok_evacuate=None):
            with stage() as (block, (bank_free, *_)):
                first = take(tok_count + count)

                @block.sync
                def _(sp):
                    refill(sp, first, tok_count + count)

                @block.tensor
                def _(pe):
                    for i in range(tok_count):
                        slot, turn = (first + i) % RING, (first + i) // RING
                        pe.wait_ge(loaded[slot], turn * 16 + 16)
                        pe.wait_ge(bank_free, i + 1)
                        for t in range(TT):
                            for k in range(KT):
                                last = nc.tensor.matmul(ps[:, i % 2, t * P:(t + 1) * P], src[:, k, t * P:(t + 1) * P],
                                                        ring[:, slot, k * P:(k + 1) * P], start=(k == 0),
                                                        stop=(k == KT - 1))
                        last.then_inc(tiles_used, 1)

                    at = first + tok_count

                    def tile(i, slot, turn):
                        bank = 2 + (slot - at) % RING % 2
                        pe.wait_ge(loaded[slot], turn * 16 + 16)
                        pe.wait_ge(bank_free, i + (tok_count + 1))
                        for k in range(KT):
                            last = nc.tensor.matmul(ps[:, bank, 0:S], ring[:, slot, k * P:(k + 1) * P], src[:, k, :],
                                                    start=(k == 0), stop=(k == KT - 1))
                        last.then_inc(tiles_used, 1)
                    over_tiles(pe, at, count, tile)

                @block.vector
                def _(dve):
                    dve.sem_inc(bank_free, 2)
                    for i in range(tok_count):
                        dve.wait_ge(tiles_used, first + i + 1)
                        tok_evacuate(i, ps[:, i % 2, 0:S].rearrange("p (t f) -> p t f", t=TT)).then_inc(bank_free, 1)
                    at = first + tok_count

                    def tile(i, slot, turn):
                        dve.wait_ge(tiles_used, i + (at + 1))
                        evacuate(i, ps[:, 2 + (slot - at) % RING % 2, 0:S]).then_inc(bank_free, 1)
                    over_tiles(dve, at, count, tile)

        def one(tensor, i):
            return tensor[:, bass.ds(i, 1), :].rearrange("p a t -> p (a t)")

        def swiglu():
            with ExitStack() as tmp, stage() as (block, (silu_done, act_ready, *_)):
                sl = sb(f"sl{stream[0]}", [P, 2, S], where=tmp)
                hid = sb(f"hid{stream[0]}", [P, 2, S], where=tmp)
                first = take(T_FFN)
                ACC = 4

                @block.sync
                def _(sp):
                    refill(sp, first, T_FFN)

                @block.tensor
                def _(pe):
                    def use(at, turns):
                        slot = (first + at) % RING
                        pe.wait_ge(loaded[slot], turns * 16 + 16 * ((first + at) // RING + 1))
                        return slot

                    def gate_up(j, at, turns=0):
                        if j >= 2:
                            pe.wait_ge(act_ready, turns * 2 + (j - 1))
                        for q in range(2):
                            slot = use(at + q, turns)
                            for k in range(KT):
                                last = nc.tensor.matmul(ps[:, j % 2, q * S:(q + 1) * S],
                                                        ring[:, slot, k * P:(k + 1) * P], hT[:, k, :],
                                                        start=(k == 0), stop=(k == KT - 1))
                            last.then_inc(tiles_used, 1)

                    def down(j, at, turns=0, begin=False, end=False):
                        pe.wait_ge(act_ready, turns * 2 + (j + 1))
                        slot = use(at, turns)
                        for d in range(KT):
                            last = nc.tensor.matmul(ps[:, ACC + d // 2, d % 2 * S:(d % 2 + 1) * S],
                                                    ring[:, slot, d * P:(d + 1) * P], hid[:, j % 2, :],
                                                    start=(begin and d % 2 == 0), stop=end, skip_group_check=True)
                        last.then_inc(tiles_used, 1)

                    gate_up(0, 0)
                    gate_up(1, 2)
                    down(0, 4, begin=True)
                    gate_up(2, 5)
                    down(1, 7)
                    with pe.Fori(0, FJ // 2 - 2) as g:
                        gate_up(3, 8, g)
                        down(2, 10, g)
                        gate_up(4, 11, g)
                        down(3, 13, g)
                    gate_up(FJ - 1, T_FFN - 4)
                    down(FJ - 2, T_FFN - 2)
                    down(FJ - 1, T_FFN - 1, end=True)

                def gated(j):
                    return 2 if j == 0 else 3 * j + 1

                @block.scalar
                def _(act):
                    def silu(j, turns=0):
                        act.wait_ge(tiles_used, turns * RING + (first + gated(j)))
                        if j >= 2:
                            act.wait_ge(act_ready, turns * 2 + (j - 1))
                        nc.scalar.activation(sl[:, j % 2, :], ps[:, j % 2, 0:S], ACT.Silu).then_inc(silu_done, 1)
                    silu(0)
                    silu(1)
                    with act.Fori(0, FJ // 2 - 1) as g:
                        silu(2, g)
                        silu(3, g)

                @block.vector
                def _(dve):
                    def gate(j, turns=0):
                        dve.wait_ge(silu_done, turns * 2 + (j + 1))
                        if j >= 2:
                            dve.wait_ge(tiles_used, turns * RING + (first + 3 * (j - 2) + 5))
                        nc.vector.tensor_tensor(hid[:, j % 2, :], ps[:, j % 2, S:2 * S], sl[:, j % 2, :],
                                                ALU.mult).then_inc(act_ready, 1)
                    gate(0)
                    gate(1)
                    with dve.Fori(0, FJ // 2 - 1) as g:
                        gate(2, g)
                        gate(3, g)
                    dve.wait_ge(tiles_used, first + T_FFN)
                    for b in range(4):
                        nc.vector.scalar_tensor_tensor(xT[:, 2 * b:2 * b + 2, :].rearrange("p a t -> p (a t)"),
                                                       ps[:, ACC + b, :], 0.5,
                                                       xT[:, 2 * b:2 * b + 2, :].rearrange("p a t -> p (a t)"),
                                                       ALU.mult, ALU.add)

        def attention(units, out, tag):
            U = len(units)
            WIDE = max(u["n"] for u in units)
            with ExitStack() as tmp, stage() as (block, (scored, shifted, maxed, exped, probs_ready, turned, turned_back,
                                                         out_ready, out_copied, v, a, *_)):
                sc = sb(f"sc_{tag}", [P, 2, TT, WIDE], where=tmp)
                pT = sb(f"pT_{tag}", [P, 2, TT, S], where=tmp)
                stat = sb(f"stat_{tag}", [P, U, 6], where=tmp)

                done = [u for u in range(U) if u == U - 1 or units[u + 1]["j"] != units[u]["j"]]

                @block.tensor
                def _(pe):
                    for step in range(U + 2):
                        if step < U:
                            u = units[step]
                            if step >= 2:
                                pe.wait_ge(shifted, step - 1)
                            for t in range(TT):
                                last = nc.tensor.matmul(ps[:, step % 2, t * u["n"]:(t + 1) * u["n"]],
                                                        u["q"][:, t * P:(t + 1) * P], u["k"], start=True, stop=True)
                            last.then_inc(scored, 1)
                        if 1 <= step <= U:
                            i = step - 1
                            u = units[i]
                            pe.wait_ge(probs_ready, i + 1)
                            if i >= 2:
                                pe.wait_ge(turned_back, i - 1)
                            for kt in range(len(u["v"])):
                                n = min(P, u["n"] - kt * P)
                                for t in range(TT):
                                    dst = ps[0:n, 2 + i % 2, kt * S + t * P:kt * S + (t + 1) * P]
                                    src = sc[:, i % 2, t, kt * P:kt * P + n]
                                    if n == P:
                                        last = nc.tensor.transpose(dst, src, mat("ident"))
                                    else:
                                        last = nc.tensor.matmul(dst, src, mat("ident"), start=True, stop=True)
                            last.then_inc(turned, 1)
                        if step >= 2:
                            i = step - 2
                            u = units[i]
                            pe.wait_ge(turned_back, i + 1)
                            fresh = i == 0 or (units[i - 1]["j"], units[i - 1]["po"]) != (u["j"], u["po"])
                            ends = i == U - 1 or (units[i + 1]["j"], units[i + 1]["po"]) != (u["j"], u["po"])
                            tiles = sum(x < i for x in done)
                            if tiles >= 2:
                                pe.wait_ge(out_copied, tiles - 1)
                            for kt, vv in enumerate(u["v"]):
                                n = min(P, u["n"] - kt * P)
                                last = nc.tensor.matmul(ps[u["po"]:u["po"] + HD, 4 + tiles % 2, 0:S], vv,
                                                        pT[0:n, i % 2, kt, :], start=(fresh and kt == 0),
                                                        stop=(ends and kt == len(u["v"]) - 1), skip_group_check=True)
                            if i in done:
                                last.then_inc(out_ready, 1)
                            else:
                                last.then_inc(a, 1)

                @block.vector
                def _(dve):
                    n = counter()
                    for i in range(U + 1):
                        if i < U:
                            u = units[i]
                            dve.wait_ge(scored, i + 1)
                            if i >= 2:
                                dve.wait_ge(turned, i - 1)
                            w = u["n"]
                            nc.vector.scalar_tensor_tensor(sc[:, i % 2, :, 0:w],
                                                           ps[:, i % 2, 0:TT * w].rearrange("p (t n) -> p t n", t=TT),
                                                           HD ** -0.5, u["bias"], ALU.mult, ALU.add).then_inc(shifted, 1)
                            dve.wait_ge(shifted, i + 1)
                            nc.vector.tensor_reduce(stat[:, i, 0:2], sc[:, i % 2, :, 0:w], AXX, ALU.max,
                                                    negate=True).then_inc(maxed, 1)
                        if i >= 1:
                            g = i - 1
                            dve.wait_ge(exped, TT * (g + 1))
                            nc.vector.reciprocal(stat[:, g, 4:6], stat[:, g, 2:4]).then_inc(v, 1)
                            dve.wait_ge(v, n())
                            if units[g].get("gate") is not None:
                                nc.vector.tensor_tensor(stat[:, g, 4:6], stat[:, g, 4:6], units[g]["gate"],
                                                        ALU.mult).then_inc(v, 1)
                                dve.wait_ge(v, n())
                            w = units[g]["n"]
                            nc.vector.tensor_tensor(sc[:, g % 2, :, 0:w], sc[:, g % 2, :, 0:w],
                                                    stat[:, g, 4:6].unsqueeze(2).broadcast_to([P, TT, w]),
                                                    ALU.mult).then_inc(probs_ready, 1)

                @block.scalar
                def _(act):
                    outs = 0
                    for i in range(U + 2):
                        if i < U:
                            act.wait_ge(maxed, i + 1)
                            for t in range(TT):
                                x = sc[:, i % 2, t, 0:units[i]["n"]]
                                nc.scalar.activation(x, x, ACT.Exp, bias=stat[:, i, t:t + 1],
                                                     accum_out=stat[:, i, 2 + t:3 + t]).then_inc(exped, 1)
                        if 1 <= i <= U:
                            g = i - 1
                            act.wait_ge(turned, g + 1)
                            n = min(P, units[g]["n"])
                            w = len(units[g]["v"]) * S
                            if g >= 2:
                                ends = sum(x <= g - 2 for x in done)
                                act.wait_ge(out_ready, ends) if ends else None
                                act.wait_ge(a, g - 1 - ends) if g - 1 - ends else None
                            nc.scalar.activation(pT[0:n, g % 2, 0:len(units[g]["v"]), :].rearrange("p a b -> p (a b)"),
                                                 ps[0:n, 2 + g % 2, 0:w], ACT.Copy).then_inc(turned_back, 1)
                        if i >= 2 and i - 2 in done:
                            act.wait_ge(out_ready, outs + 1)
                            nc.scalar.activation(out[:, units[i - 2]["j"], :], ps[:, 4 + outs % 2, 0:S],
                                                 ACT.Copy).then_inc(out_copied, 1)
                            outs += 1

        mixer = ExitStack()
        zT = sb("zT", [P, T_IN, S], where=mixer)
        vtok = sb("vtok", [P, TT, 512], where=mixer)

        rms_norm(lambda k: gs[:, 0, k:k + 1], lambda k: mod[:, k:k + 1])

        def copy_in(i, src):
            return nc.vector.tensor_scalar(one(zT, i), src, 1.0, None, ALU.mult)

        project(T_IN, hT, copy_in, T_IN_TOK,
                lambda i, src: nc.vector.tensor_copy(vtok[:, :, i * P:(i + 1) * P], src))

        attn = ExitStack()
        bias = sb("bias", [P, NH, TT, S], where=attn)
        with ExitStack() as tmp, stage() as (block, (squared, summed, scaled, root, v, c0_ready, weighted, *_)):
            root_qk = sb("root_qk", [P, NH * S], where=tmp)
            c0 = sb("c0", [P, 14], where=tmp)
            shiftd = sb("shiftd", [P, 14, S], where=tmp)
            qk = zT[:, 0:8, :].rearrange("p a t -> p (a t)")
            zr = zT[:, 8:22, :]

            @block.sync
            def _(sp):
                for h in range(NH):
                    sp.dma_start(bias[:, h, :, :], A["attn_bias"][h].rearrange("(t p) k -> p t k", p=P)
                                 ).then_inc(table_in, 16)
                    tables()
                sp.wait_ge(table_in, 16 * NH)

            @block.scalar
            def _(act):
                nc.scalar.activation(sq[:, :, :].rearrange("p a t -> p (a t)"), qk, ACT.Square).then_inc(squared, 1)
                act.wait_ge(c0_ready, 2)
                for i in range(14):
                    nc.scalar.activation(shiftd[:, i, :], zr[:, i, :], ACT.Copy, scale=c0[:, i:i + 1]
                                         ).then_inc(weighted, 1)
                act.wait_ge(scaled, 4)
                nc.scalar.activation(root_qk[:, :], root_qk[:, :], ACT.Sqrt).then_inc(root, 1)

            @block.tensor
            def _(pe):
                pe.wait_ge(squared, 1)
                for b in range(4):
                    nc.tensor.matmul(ps[:, b, :], mat("blockones"),
                                     sq[:, 2 * b:2 * b + 2, :].rearrange("p a t -> p (a t)"),
                                     start=True, stop=True).then_inc(summed, 1)

            @block.vector
            def _(dve):
                n = counter()
                nc.vector.tensor_tensor(c0[:, :], vec_all("mu_prev"), vec_all("mu_next"), ALU.add).then_inc(c0_ready, 1)
                dve.wait_ge(c0_ready, 1)
                nc.vector.tensor_scalar(c0[:, :], c0[:, :], -1.0, 1.0, ALU.mult, ALU.add).then_inc(c0_ready, 1)
                for i in range(14):
                    dve.wait_ge(weighted, i + 1)
                    nc.vector.scalar_tensor_tensor(shiftd[:, i, 1:S], zr[:, i, 0:S - 1], vec("mu_prev", i),
                                                   shiftd[:, i, 1:S], ALU.mult, ALU.add).then_inc(v, 1)
                    dve.wait_ge(v, n())
                    nc.vector.scalar_tensor_tensor(shiftd[:, i, 0:S - 1], zr[:, i, 1:S], vec("mu_next", i),
                                                   shiftd[:, i, 0:S - 1], ALU.mult, ALU.add).then_inc(v, 1)
                    dve.wait_ge(v, n())
                for b in range(4):
                    dve.wait_ge(summed, b + 1)
                    nc.vector.tensor_scalar(root_qk[:, 512 * b:512 * b + 512], ps[:, b, :], 1.0 / HD, NORM_EPS,
                                            ALU.mult, ALU.add).then_inc(scaled, 1)
                dve.wait_ge(root, 1)
                nc.vector.reciprocal(root_qk[:, :], root_qk[:, :]).then_inc(v, 1)
                dve.wait_ge(v, n())
                for b, name in enumerate(("q_norm_g", "k_norm_g")):
                    cols = slice(1024 * b, 1024 * b + 1024)
                    nc.vector.scalar_tensor_tensor(qk[:, cols], qk[:, cols], vec(name), root_qk[:, cols], ALU.mult,
                                                   ALU.mult)
                nc.vector.tensor_copy(zr, shiftd[:, :, :])

        attention([dict(po=HD * (h % 2), j=h // 2, n=S, q=zT[HD * (h % 2):HD * (h % 2) + HD, h // 2, :],
                        k=zT[HD * (h % 2):HD * (h % 2) + HD, 4 + h // 2, :], bias=bias[:, h, :, :],
                        v=[vtok[:, t, h * HD:(h + 1) * HD] for t in range(TT)]) for h in range(NH)], mix, "dilated")
        attn.close()

        wkv = ExitStack()
        rT, kT, vT = zT[:, 8:12, :], zT[:, 12:16, :], zT[:, 16:20, :]
        flat = "p a t -> p (a t)"
        alpha, beta, kappa, rho = (sb(n, [P, 2, 4, S], where=wkv) for n in ("alpha", "beta", "kappa", "rho"))
        gT = sb("gT", [P, 4, S], where=wkv)
        bonus = sb("bonus", [P, 4, S], where=wkv)
        ysum = sb("ysum", [P, 2, 512], where=wkv)
        carry = sb("carry", [P, 2, 4], where=wkv)
        feat = ExitStack()
        lora = sb("lora", [P, 2, 512], where=feat)
        g_up = sb("g_up", [P, 512], where=feat)
        logw = sb("logw", [P, 2, 4, S], where=feat)
        aa = sb("aa", [P, 2, 4, S], where=feat)
        kk = sb("kk", [P, 4, S], where=feat)
        omka = sb("omka", [P, 4], where=feat)
        with stage() as (block, (ups_in, squashed, raised, sig_done, v, kk_scaled, summed, *_)):
            @block.sync
            def _(sp):
                sp.dma_start(lora[:, :, :], A["lora_up"]).then_inc(ups_in, 16)
                sp.dma_start(g_up[:, :], A["g_up"]).then_inc(ups_in, 16)

            @block.scalar
            def _(act):
                nc.scalar.activation(zT[0:64, 20, :], zT[0:64, 20, :], ACT.Tanh).then_inc(squashed, 1)
                nc.scalar.activation(zT[:, 21, :], zT[:, 21, :], ACT.Sigmoid).then_inc(squashed, 1)
                for d in range(2):
                    act.wait_ge(raised, 8 * d + 8)
                    for j in range(4):
                        bank, col = 4 * d + j // 2, j % 2 * S
                        nc.scalar.activation(logw[:, d, j, :], ps[:, bank, col:col + S], ACT.Sigmoid,
                                             bias=vec("w_decay0", 4 * d + j)).then_inc(sig_done, 1)
                        nc.scalar.activation(aa[:, d, j, :], ps[:, bank + 2, col:col + S], ACT.Sigmoid,
                                             bias=vec("a_gate0", 4 * d + j)).then_inc(sig_done, 1)

            @block.tensor
            def _(pe):
                pe.wait_ge(ups_in, 32)
                pe.wait_ge(squashed, 2)
                for d in range(2):
                    for j in range(4):
                        bank, col = 4 * d + j // 2, j % 2 * S
                        nc.tensor.matmul(ps[:, bank, col:col + S], lora[0:64, d, j * P:(j + 1) * P], zT[0:64, 20, :],
                                         start=True, stop=True).then_inc(raised, 1)
                        nc.tensor.matmul(ps[:, bank + 2, col:col + S], lora[64:128, d, j * P:(j + 1) * P],
                                         zT[64:128, 20, :], start=True, stop=True).then_inc(raised, 1)

            @block.vector
            def _(dve):
                for j in range(4):
                    nc.vector.tensor_scalar(kk[:, j, :], kT[:, j, :], vec("k_k", j), None, ALU.mult).then_inc(v, 1)
                nc.vector.tensor_scalar(omka[:, :], vec_all("k_a"), -1.0, 1.0, ALU.mult, ALU.add)
                dve.wait_ge(v, 4)
                nc.vector.tensor_tensor(sq[:, 0:4, :], kk[:, :, :], kk[:, :, :], ALU.mult)
                dve.wait_ge(sig_done, 16)
                nc.vector.tensor_scalar(logw[:, :, :, :].rearrange("p d a t -> p (d a t)"),
                                        logw[:, :, :, :].rearrange("p d a t -> p (d a t)"),
                                        -float(np.exp(-0.5)), None, ALU.mult)

        with ExitStack() as tmp, stage() as (block, (summed, gated, kk_ready, exp_in, exps, v, w, kb_ready, bonus_sum,
                                                     g_done, kk_root, carry_in, *_)):
            cum = sb("cum", [P, 2, 4, S], where=tmp)
            off = sb("off", [P, 2, 4, S], where=tmp)
            inv = sb("inv", [P, 4, S], where=tmp)
            inv2 = sb("inv2", [P, 2, 4, S], where=tmp)
            kd = sb("kd", [P, 4, S], where=tmp)

            @block.tensor
            def _(pe):
                for b in range(2):
                    nc.tensor.matmul(ps[:, b, :], mat("blockones"), sq[:, 2 * b:2 * b + 2, :].rearrange(flat),
                                     start=True, stop=True).then_inc(summed, 1)
                for j in range(4):
                    nc.tensor.matmul(ps[:, 2 + j // 2, j % 2 * S:j % 2 * S + S], g_up[:, j * P:(j + 1) * P],
                                     zT[:, 21, :], start=True, stop=True).then_inc(gated, 1)
                pe.wait_ge(kb_ready, 1)
                for b in range(2):
                    nc.tensor.matmul(ps[:, 4 + b, :], mat("blockones"), sq[:, 4 + 2 * b:6 + 2 * b, :].rearrange(flat),
                                     start=True, stop=True).then_inc(bonus_sum, 1)

            @block.scalar
            def _(act):
                act.wait_ge(kk_ready, 2)
                nc.scalar.activation(inv[:, :, :], inv[:, :, :], ACT.Sqrt).then_inc(kk_root, 1)
                act.wait_ge(gated, 4)
                nc.scalar.activation(gT[:, :, :].rearrange(flat), ps[:, 2:4, :].rearrange("p b n -> p (b n)"),
                                     ACT.Copy).then_inc(g_done, 1)
                for d in range(2):
                    act.wait_ge(exp_in, d + 1)
                    upto, sign = (cum, 1.0) if d == 0 else (off, -1.0)
                    before = off if d == 0 else cum
                    nc.scalar.activation(rho[:, d], upto[:, d], ACT.Exp).then_inc(exps, 1)
                    nc.scalar.activation(inv2[:, d], upto[:, d], ACT.Exp, scale=-1.0).then_inc(exps, 1)
                    nc.scalar.activation(alpha[:, d], before[:, d], ACT.Exp, scale=sign).then_inc(exps, 1)
                act.wait_ge(carry_in, 2)
                nc.scalar.activation(carry[:, :, :], carry[:, :, :], ACT.Exp)

            @block.vector
            def _(dve):
                n = counter()
                for b in range(2):
                    dve.wait_ge(summed, b + 1)
                    nc.vector.tensor_scalar(inv[:, 2 * b:2 * b + 2, :].rearrange(flat), ps[:, b, :], 1e-12, None,
                                            ALU.max).then_inc(kk_ready, 1)
                for d in range(2):
                    for j in range(4):
                        for c in range(2):
                            cols = slice(c * P, c * P + P)
                            nc.vector.tensor_tensor_scan(off[:, d, j, cols], mat("ones"), logw[:, d, j, cols], 0.0,
                                                         ALU.mult, ALU.add).then_inc(v, n.one())
                    dve.wait_ge(v, n.now)
                    chunks = off[:, d].rearrange("p a (c t) -> p (a c) t", t=P)
                    nc.vector.tensor_tensor(cum[:, d].rearrange("p a (c t) -> p (a c) t", t=P), chunks,
                                            chunks[:, :, P // 2 - 1:P // 2].broadcast_to([P, 8, P]),
                                            ALU.subtract).then_inc(v, n.one())
                    dve.wait_ge(v, n.now)
                    pair = (cum[:, d], logw[:, d]) if d == 0 else (logw[:, d], cum[:, d])
                    nc.vector.tensor_tensor(off[:, d], pair[0], pair[1], ALU.subtract).then_inc(exp_in, 1)
                    dve.wait_ge(exp_in, d + 1)
                    nc.vector.tensor_tensor(carry[:, d, :], cum[:, d, :, P - 1:P].rearrange("p a b -> p (a b)"),
                                            off[:, d, :, P:P + 1].rearrange("p a b -> p (a b)"),
                                            ALU.subtract if d == 0 else ALU.add).then_inc(carry_in, 1)
                dve.wait_ge(kk_root, 1)
                nc.vector.reciprocal(inv[:, :, :], inv[:, :, :]).then_inc(v, n.one())
                dve.wait_ge(v, n.now)
                nc.vector.tensor_tensor(kk[:, :, :], kk[:, :, :], inv[:, :, :], ALU.mult).then_inc(v, n.one())
                dve.wait_ge(v, n.now)
                nc.vector.tensor_tensor(inv[:, :, :], aa[:, 0], aa[:, 1], ALU.add).then_inc(v, n.one())
                dve.wait_ge(v, n.now)
                nc.vector.tensor_scalar(inv[:, :, :].rearrange(flat), inv[:, :, :].rearrange(flat), 0.5, None,
                                        ALU.mult).then_inc(v, n.one())
                dve.wait_ge(v, n.now)
                for j in range(4):
                    nc.vector.tensor_scalar(inv[:, j, :], inv[:, j, :], vec("k_a", j), omka[:, j:j + 1], ALU.mult,
                                            ALU.add).then_inc(v, n.one())
                dve.wait_ge(v, n.now)
                nc.vector.tensor_tensor(inv[:, :, :], inv[:, :, :], kT, ALU.mult).then_inc(v, n.one())
                dve.wait_ge(v, n.now)
                for j in range(4):
                    nc.vector.scalar_tensor_tensor(sq[:, 4 + j, :], inv[:, j, :], vec("r_k", j), rT[:, j, :],
                                                   ALU.mult, ALU.mult).then_inc(kb_ready if j == 3 else w, 1)
                dve.wait_ge(kb_ready, 1)
                dve.wait_ge(w, 3)
                for d in range(2):
                    dve.wait_ge(v, n.now)
                    for j in range(4):
                        nc.vector.tensor_scalar(kd[:, j, :], aa[:, d, j, :], vec("k_a", j), omka[:, j:j + 1],
                                                ALU.mult, ALU.add).then_inc(v, n.one())
                    nc.vector.tensor_tensor(beta[:, d], kk[:, :, :], aa[:, d], ALU.mult).then_inc(v, n.one())
                    dve.wait_ge(v, n.now)
                    nc.vector.tensor_tensor(kd[:, :, :], kd[:, :, :], kT, ALU.mult).then_inc(v, n.one())
                    dve.wait_ge(exps, 3 * d + 3)
                    dve.wait_ge(v, n.now)
                    nc.vector.tensor_tensor(kappa[:, d], kd[:, :, :], inv2[:, d], ALU.mult).then_inc(v, n.one())
                    nc.vector.tensor_tensor(beta[:, d], beta[:, d], inv2[:, d], ALU.mult).then_inc(v, n.one())
                    nc.vector.tensor_tensor(alpha[:, d], alpha[:, d], kk[:, :, :], ALU.mult).then_inc(v, n.one())
                    nc.vector.tensor_tensor(rho[:, d], rho[:, d], rT, ALU.mult).then_inc(v, n.one())
                dve.wait_ge(bonus_sum, 2)
                for b in range(2):
                    nc.vector.tensor_tensor(bonus[:, 2 * b:2 * b + 2, :].rearrange(flat), ps[:, 4 + b, :],
                                            vT[:, 2 * b:2 * b + 2, :].rearrange(flat), ALU.mult)
        feat.close()

        solve = ExitStack()
        v_tok = sb("v_tok", [P, 2, 512], where=solve)
        bk_tok = sb("bk_tok", [P, 2, 2, 512], where=solve)
        with stage() as (block, (turned, *_)):
            jobs = [(v_tok[:, c, :], vT, c) for c in range(2)]
            jobs += [(bk_tok[:, d, i, :], (beta, kappa)[i][:, d], d) for d in range(2) for i in range(2)]

            @block.tensor
            def _(pe):
                for n, (_, src, c) in enumerate(jobs):
                    for j in range(4):
                        last = nc.tensor.transpose(ps[:, n, j * P:(j + 1) * P], src[:, j, c * P:(c + 1) * P],
                                                   mat("ident"))
                    last.then_inc(turned, 1)

            @block.vector
            def _(dve):
                for n, (dst, _, _) in enumerate(jobs):
                    if n % 2 == 0:
                        dve.wait_ge(turned, n + 1)
                        nc.vector.tensor_copy(dst, ps[:, n, :])

            @block.scalar
            def _(act):
                for n, (dst, _, _) in enumerate(jobs):
                    if n % 2:
                        act.wait_ge(turned, n + 1)
                        nc.scalar.activation(dst, ps[:, n, :], ACT.Copy)

        states = [sb(f"state{d}", [P, 4, HD], where=solve) for d in range(2)]
        LT, X, XT, Y, LmT, MT, N1, N2 = (sb(n, [P, NH, P], where=solve) for n in
                                         ("LT", "X", "XT", "Y", "LmT", "MT", "N1", "N2"))
        G = sb("G", [P, 512], where=solve)
        SA = sb("SA", [P, 512], where=solve)
        heads = "p h t -> p (h t)"

        def all_heads(m):
            return mat(m).unsqueeze(1).broadcast_to([P, NH, P])

        def banks(b):
            return ps[:, b:b + 2, :].rearrange("p b (h t) -> p (b h) t", t=P)

        def place_of(h):
            return h % 2 * 4 + h // 2

        def rows(h):
            return slice(HD * (h % 2), HD * (h % 2) + HD)

        for first_chunk in (True, False):
            for d in range(2):
                c = d if first_chunk else 1 - d
                cols = slice(c * P, c * P + P)
                with stage() as (block, (products, masked, y_used, x_ready, xt_ready, level_in, g_ready, v, sa_ready,
                                         y_ready, state_ready, sq_ready, *_)):
                    @block.tensor
                    def _(pe):
                        def product(bank, left, right, counted):
                            for h in range(NH):
                                last = nc.tensor.matmul(ps[:, bank + h % 2, h // 2 * P:h // 2 * P + P],
                                                        left[rows(h), d, h // 2, cols],
                                                        right[rows(h), d, h // 2, cols], start=True, stop=True)
                            last.then_inc(counted, 1)
                        product(0, beta, alpha, products)
                        product(2, alpha, beta, products)
                        product(4, kappa, alpha, products)
                        product(6, beta, rho, products)
                        pe.wait_ge(masked, 3)
                        product(4, kappa, rho, products)
                        for lv in range(6):
                            def doubling(bank, left, right, counted):
                                for h in range(NH):
                                    last = nc.tensor.matmul(ps[:, bank + h // 4, h % 4 * P:h % 4 * P + P],
                                                            left[:, h, :], right[:, h, :], start=True, stop=True)
                                last.then_inc(counted, 1)
                            pe.wait_ge(level_in, lv + 1)
                            pe.wait_ge(x_ready, lv + 1)
                            doubling(0, LmT, X, products)
                            pe.wait_ge(sq_ready, lv + 1)
                            pe.wait_ge(xt_ready, lv + 1)
                            if lv == 0:
                                pe.wait_ge(masked, 5)
                            if lv < 5:
                                doubling(2, XT, Y, products)
                            doubling(4, Y, XT, products)
                        pe.wait_ge(masked, 5)
                        for h in range(NH):
                            dst = ps[:, 6 + h % 2, h // 2 * HD:(h // 2 + 1) * HD]
                            if not first_chunk:
                                nc.tensor.matmul(dst, alpha[rows(h), d, h // 2, cols], states[d][rows(h), h // 2, :],
                                                 start=True, stop=False)
                            last = nc.tensor.matmul(dst, MT[:, place_of(h), :], v_tok[:, c, h * HD:(h + 1) * HD],
                                                    start=first_chunk, stop=True)
                        last.then_inc(g_ready, 1)
                        pe.wait_ge(xt_ready, 7)
                        pe.wait_ge(g_ready, 2)
                        for h in range(NH):
                            at = place_of(h)
                            last = nc.tensor.matmul(ps[:, 2, h * HD:(h + 1) * HD], XT[:, at, :],
                                                    G[:, at * HD:(at + 1) * HD], start=True, stop=True)
                        last.then_inc(sa_ready, 1)
                        pe.wait_ge(sa_ready, 2)
                        for h in range(NH):
                            hv = slice(h * HD, (h + 1) * HD)
                            dst = ps[:, 3 * (h % 2), h // 2 * HD:(h // 2 + 1) * HD]
                            if not first_chunk:
                                nc.tensor.matmul(dst, rho[rows(h), d, h // 2, cols], states[d][rows(h), h // 2, :],
                                                 start=True, stop=False)
                            nc.tensor.matmul(dst, N1[:, place_of(h), :], SA[:, hv], start=first_chunk, stop=False)
                            last = nc.tensor.matmul(dst, N2[:, place_of(h), :], v_tok[:, c, hv], start=False, stop=True)
                        last.then_inc(y_ready, 1)
                        if first_chunk:
                            for h in range(NH):
                                hv = slice(h * HD, (h + 1) * HD)
                                dst = ps[rows(h), 1, h // 2 * HD:(h // 2 + 1) * HD]
                                nc.tensor.matmul(dst, bk_tok[:, d, 0, hv], SA[:, hv], start=True, stop=False)
                                last = nc.tensor.matmul(dst, bk_tok[:, d, 1, hv], v_tok[:, c, hv], start=False,
                                                        stop=True)
                            last.then_inc(state_ready, 1)

                    @block.scalar
                    def _(act):
                        for lv in range(6):
                            act.wait_ge(products, 5 + 3 * lv + 1)
                            if lv:
                                act.wait_ge(products, 5 + 3 * lv)
                            nc.scalar.activation(Y[:, :, :], banks(0), ACT.Copy).then_inc(sq_ready, 1)
                        act.wait_ge(g_ready, 1)
                        nc.scalar.activation(G[:, :].rearrange("p (a n) -> p a n", a=2), ps[:, 6:8, 0:S],
                                             ACT.Copy).then_inc(g_ready, 1)

                    @block.gpsimd
                    def _(pool):
                        pool.wait_ge(masked, 1)
                        for lv, b in enumerate((2, 4, 8, 16, 32, 64)):
                            if lv:
                                pool.wait_ge(products, 5 + 3 * (lv - 1) + 1)
                            nc.gpsimd.tensor_tensor(LmT[:, :, :], LT[:, :, :], all_heads(f"level{d}_{b}"),
                                                    ALU.mult).then_inc(level_in, 1)

                    @block.vector
                    def _(dve):
                        n = counter()
                        dve.wait_ge(products, 1)
                        nc.vector.tensor_tensor(LT[:, :, :], banks(0), all_heads(f"strict{d}"),
                                                ALU.mult).then_inc(masked, 1)
                        dve.wait_ge(products, 2)
                        nc.vector.tensor_tensor(X[:, :, :], banks(2), all_heads(f"level_row{d}"),
                                                ALU.mult).then_inc(masked, 1)
                        dve.wait_ge(products, 3)
                        nc.vector.tensor_tensor(MT[:, :, :], banks(4), all_heads(f"strict{d}"),
                                                ALU.mult).then_inc(masked, 1)
                        dve.wait_ge(masked, 2)
                        nc.vector.tensor_tensor(XT[:, :, :], LT[:, :, :], all_heads(f"level{d}_1"),
                                                ALU.mult).then_inc(v, n.one())
                        nc.vector.tensor_tensor(X[:, :, :], all_heads("ident"), X[:, :, :],
                                                ALU.subtract).then_inc(x_ready, 1)
                        dve.wait_ge(v, n.now)
                        nc.vector.tensor_tensor(XT[:, :, :], all_heads("ident"), XT[:, :, :],
                                                ALU.subtract).then_inc(xt_ready, 1)
                        dve.wait_ge(products, 4)
                        nc.vector.tensor_tensor(N1[:, :, :], banks(6), all_heads(f"upto{d}"),
                                                ALU.mult).then_inc(masked, 1)
                        dve.wait_ge(products, 5)
                        nc.vector.tensor_tensor(N2[:, :, :], banks(4), all_heads(f"upto{d}"),
                                                ALU.mult).then_inc(masked, 1)
                        for lv in range(6):
                            if lv < 5:
                                dve.wait_ge(products, 5 + 3 * lv + 2)
                                dve.wait_ge(x_ready, lv + 1)
                                nc.vector.tensor_tensor(X[:, :, :], X[:, :, :], banks(2),
                                                        ALU.subtract).then_inc(x_ready, 1)
                            dve.wait_ge(products, 5 + 3 * lv + (3 if lv < 5 else 2))
                            dve.wait_ge(xt_ready, lv + 1)
                            nc.vector.tensor_tensor(XT[:, :, :], XT[:, :, :], banks(4),
                                                    ALU.subtract).then_inc(xt_ready, 1)
                        dve.wait_ge(sa_ready, 1)
                        nc.vector.tensor_scalar(SA[:, :], ps[:, 2, :], -1.0, None, ALU.mult).then_inc(sa_ready, 1)
                        dve.wait_ge(y_ready, 1)
                        for odd in range(2):
                            mine = ysum[:, c, :].rearrange("p (j q e) -> p j q e", q=2, e=HD)[:, :, odd, :]
                            new = ps[:, 3 * odd, 0:S].rearrange("p (j e) -> p j e", e=HD)
                            if first_chunk:
                                nc.vector.tensor_copy(mine, new)
                            else:
                                nc.vector.tensor_tensor(mine, mine, new, ALU.add)
                        if first_chunk:
                            dve.wait_ge(state_ready, 1)
                            for j in range(4):
                                nc.vector.tensor_scalar(states[d][:, j, :], ps[:, 1, j * HD:(j + 1) * HD],
                                                        carry[:, d, j:j + 1], None, ALU.mult)
        solve.close()

        with ExitStack() as tmp, stage() as (block, (v, centred, squared, root, normed, turned, root_in, *_)):
            st = sb("st", [P, 2, 16], where=tmp)
            y = ysum[:, :, :].rearrange("p c (h e) -> p (c h) e", e=HD)
            ysq = sq[:, 0:4, :].rearrange("p a t -> p (a t)").rearrange("p (h e) -> p h e", e=HD)

            @block.scalar
            def _(act):
                act.wait_ge(centred, 1)
                nc.scalar.activation(ysq, y, ACT.Square).then_inc(squared, 1)
                act.wait_ge(root_in, 1)
                nc.scalar.activation(st[:, 1, :], st[:, 1, :], ACT.Sqrt).then_inc(root, 1)

            @block.vector
            def _(dve):
                n = counter()
                nc.vector.tensor_reduce(st[:, 0, :], y, AXX, ALU.add).then_inc(v, n.one())
                dve.wait_ge(v, n.now)
                nc.vector.tensor_scalar(st[:, 0, :], st[:, 0, :], 1.0 / HD, None, ALU.mult).then_inc(v, n.one())
                dve.wait_ge(v, n.now)
                nc.vector.tensor_tensor(y, y, st[:, 0, :].unsqueeze(2).broadcast_to([P, 16, HD]),
                                        ALU.subtract).then_inc(centred, 1)
                dve.wait_ge(squared, 1)
                nc.vector.tensor_reduce(st[:, 1, :], ysq, AXX, ALU.add).then_inc(v, n.one())
                dve.wait_ge(v, n.now)
                nc.vector.tensor_scalar(st[:, 1, :], st[:, 1, :], 1.0 / HD, 64e-5, ALU.mult,
                                        ALU.add).then_inc(root_in, 1)
                dve.wait_ge(root, 1)
                nc.vector.reciprocal(st[:, 1, :], st[:, 1, :]).then_inc(v, n.one())
                dve.wait_ge(v, n.now)
                nc.vector.tensor_tensor(y, y, st[:, 1, :].unsqueeze(2).broadcast_to([P, 16, HD]),
                                        ALU.mult).then_inc(normed, 1)
                for j in range(4):
                    dve.wait_ge(turned, j + 1)
                    nc.vector.tensor_scalar(mix[:, 4 + j, :], ps[:, j, 0:S], vec("lnx_g", j), vec("lnx_b", j),
                                            ALU.mult, ALU.add).then_inc(v, n.one())
                dve.wait_ge(v, n.now)
                nc.vector.tensor_tensor(mix[:, 4:8, :], mix[:, 4:8, :], bonus[:, :, :], ALU.add).then_inc(v, n.one())
                dve.wait_ge(v, n.now)
                nc.vector.tensor_tensor(mix[:, 4:8, :], mix[:, 4:8, :], gT[:, :, :], ALU.mult)

            @block.tensor
            def _(pe):
                pe.wait_ge(normed, 1)
                for j in range(4):
                    for c in range(2):
                        last = nc.tensor.transpose(ps[:, j, c * P:(c + 1) * P], ysum[:, c, j * P:(j + 1) * P],
                                                   mat("ident"))
                    last.then_inc(turned, 1)
        wkv.close()
        mixer.close()

        def add_gated(col):
            return lambda i, src: nc.vector.scalar_tensor_tensor(one(xT, i), src, mod[:, col:col + 8][:, bass.ds(i, 1)],
                                                                 one(xT, i), ALU.mult, ALU.add)

        project(T_OUT, mix, add_gated(16))
        rms_norm(lambda k: gs[:, 1, k:k + 1], lambda k: mod[:, 24 + k:25 + k])

        peer = ExitStack()
        h_tok = sb("h_tok", [P, TT, D], where=peer)
        experts = sb("experts", [P, TT, SLOTS], U32, where=peer)
        gates = sb("gates", [P, TT, SLOTS], where=peer)
        pick = ExitStack()
        scores = sb("scores", [P, TT, 2, NH, NE], where=pick)
        with ExitStack() as tmp:
            queries = sb("queries", [P, T_QUERY, S], where=tmp)
            subkeys = sb("subkeys", [P, 2, NE], where=tmp)
            project(T_QUERY, hT, lambda i, src: nc.vector.tensor_scalar(one(queries, i), src, 1.0, None, ALU.mult))
            with stage() as (block, (keys_in, scored, turned, bank_free, *_)):
                @block.sync
                def _(sp):
                    sp.dma_start(subkeys[:, :, :], A["subkeys"]).then_inc(keys_in, 16)

                @block.tensor
                def _(pe):
                    pe.wait_ge(keys_in, 16)
                    for t in range(TT):
                        for half in range(2):
                            if t:
                                pe.wait_ge(bank_free, half + 1)
                            for h in range(NH):
                                last = nc.tensor.matmul(ps[:, 2 * half + h // 4, h % 4 * P:h % 4 * P + P],
                                                        queries[:, 2 * h + half, t * P:(t + 1) * P],
                                                        subkeys[:, half, :], start=True, stop=True)
                            last.then_inc(scored, 1)
                    for t in range(TT):
                        for k in range(KT):
                            last = nc.tensor.transpose(ps[:, 4 + 2 * t + k // 4, k % 4 * P:k % 4 * P + P],
                                                       hT[:, k, t * P:(t + 1) * P], mat("ident"))
                        last.then_inc(turned, 1)

                @block.vector
                def _(dve):
                    for n in range(2 * TT):
                        dve.wait_ge(scored, n + 1)
                        b = n % 2 * 2
                        nc.vector.tensor_copy(scores[:, n // 2, n % 2, :, :].rearrange(heads),
                                              ps[:, b:b + 2, :].rearrange("p b n -> p (b n)")).then_inc(bank_free, 1)

                @block.scalar
                def _(act):
                    for t in range(TT):
                        act.wait_ge(turned, t + 1)
                        nc.scalar.activation(h_tok[:, t, :], ps[:, 4 + 2 * t:6 + 2 * t, :].rearrange("p b n -> p (b n)"),
                                             ACT.Copy)

        top = sb("top", [P, TT, 2, NH, TOPK], where=pick)
        at = sb("at", [P, TT, 2, NH, TOPK], U32, where=pick)
        sums = sb("sums", [P, TT, NH, TOPK, TOPK], where=pick)
        best = sb("best", [P, TT, NH, TOPK], where=pick)
        place = sb("place", [P, TT, NH, TOPK], U32, where=pick)

        def top16(dve, v, n, values, out, index):
            for r in range(2):
                eight = slice(8 * r, 8 * r + 8)
                nc.vector.max(out[:, eight], values).then_inc(v, n.one())
                dve.wait_ge(v, n.now)
                nc.vector.max_index(index[:, eight], out[:, eight], values).then_inc(v, n.one())
                dve.wait_ge(v, n.now)
                if r == 0:
                    nc.vector.match_replace(values, out[:, eight], values, -3e38).then_inc(v, n.one())
                    dve.wait_ge(v, n.now)

        with stage() as (block, (v, *_)):
            @block.vector
            def _(dve):
                n = counter()
                for t in range(TT):
                    for half in range(2):
                        for h in range(NH):
                            top16(dve, v, n, scores[:, t, half, h, :], top[:, t, half, h, :], at[:, t, half, h, :])
                dve.wait_ge(v, n.now)
                for t in range(TT):
                    nc.vector.tensor_tensor(sums[:, t], top[:, t, 0].unsqueeze(3).broadcast_to([P, NH, TOPK, TOPK]),
                                            top[:, t, 1].unsqueeze(2).broadcast_to([P, NH, TOPK, TOPK]),
                                            ALU.add).then_inc(v, n.one())
                dve.wait_ge(v, n.now)
                for t in range(TT):
                    for h in range(NH):
                        top16(dve, v, n, sums[:, t, h].rearrange("p a b -> p (a b)"), best[:, t, h, :],
                              place[:, t, h, :])

        with ExitStack() as tmp, stage() as (block, (v, exp_in, exped, counted, *_)):
            digits = sb("digits", [P, TOPK], where=tmp)
            atf = sb("atf", [P, TT, 2, NH, TOPK], where=tmp)
            half_int = sb("half_int", [P, TT, SLOTS], U32, where=tmp)
            half_place = sb("half_place", [P, TT, SLOTS], where=tmp)
            found = sb("found", [P, 2, TT, SLOTS], where=tmp)
            den = sb("den", [P, TT * NH], where=tmp)
            hot = sums

            @block.gpsimd
            def _(pool):
                nc.gpsimd.iota(digits[:, :], [[1, TOPK]], base=0, channel_multiplier=0,
                               allow_small_or_imprecise_dtypes=True).then_inc(counted, 1)

            @block.scalar
            def _(act):
                act.wait_ge(exp_in, 1)
                nc.scalar.activation(gates[:, :, :], gates[:, :, :], ACT.Exp).then_inc(exped, 1)

            @block.vector
            def _(dve):
                n = counter()
                b4 = "p t (h k) -> p (t h) k"
                g3 = gates[:, :, :].rearrange(b4, k=TOPK)
                best3 = best[:, :, :, :].rearrange("p t h k -> p (t h) k")
                nc.vector.tensor_tensor(g3, best3, best3[:, :, 0:1].broadcast_to([P, TT * NH, TOPK]),
                                        ALU.subtract).then_inc(exp_in, 1)
                nc.vector.tensor_copy(atf[:, :, :, :, :], at[:, :, :, :, :]).then_inc(v, n.one())
                dve.wait_ge(counted, 1)
                flat_place = place[:, :, :, :].rearrange("p t h k -> p t (h k)")
                for half in range(2):
                    if half == 0:
                        nc.vector.tensor_scalar(half_int[:, :, :], flat_place, 4, None,
                                                ALU.logical_shift_right).then_inc(v, n.one())
                    else:
                        nc.vector.tensor_scalar(half_int[:, :, :], flat_place, 15, None,
                                                ALU.bitwise_and).then_inc(v, n.one())
                    dve.wait_ge(v, n.now)
                    nc.vector.tensor_copy(half_place[:, :, :], half_int[:, :, :]).then_inc(v, n.one())
                    dve.wait_ge(v, n.now)
                    for t in range(TT):
                        four = [P, NH, TOPK, TOPK]
                        nc.vector.tensor_tensor(hot[:, t], digits[:, :].unsqueeze(1).unsqueeze(1).broadcast_to(four),
                                                half_place[:, t, :].rearrange("p (h k) -> p h k", k=TOPK)
                                                .unsqueeze(3).broadcast_to(four), ALU.is_equal).then_inc(v, n.one())
                        dve.wait_ge(v, n.now)
                        nc.vector.tensor_tensor(hot[:, t], hot[:, t], atf[:, t, half].unsqueeze(2).broadcast_to(four),
                                                ALU.mult).then_inc(v, n.one())
                        dve.wait_ge(v, n.now)
                        nc.vector.tensor_reduce(found[:, half, t, :].rearrange("p (h k) -> p h k", k=TOPK), hot[:, t],
                                                AXX, ALU.add).then_inc(v, n.one())
                        dve.wait_ge(v, n.now)
                nc.vector.scalar_tensor_tensor(experts[:, :, :], found[:, 0], float(NE), found[:, 1], ALU.mult,
                                               ALU.add)
                dve.wait_ge(exped, 1)
                nc.vector.tensor_reduce(den[:, :], g3, AXX, ALU.add).then_inc(v, n.one())
                dve.wait_ge(v, n.now)
                nc.vector.reciprocal(den[:, :], den[:, :]).then_inc(v, n.one())
                dve.wait_ge(v, n.now)
                nc.vector.tensor_tensor(g3, g3, den[:, :].unsqueeze(2).broadcast_to([P, TT * NH, TOPK]), ALU.mult)
        pick.close()

        BATCH = 8
        TURNS = SLOTS // (2 * BATCH)
        y_tok = sb("y_tok", [P, TT, D], where=peer)
        weights = sb("weights", [P, TT, SLOTS], where=peer)
        row_in = [[sem(f"row_in{s}_{i}") for i in range(BATCH)] for s in range(2)]
        row_used = sem("row_used")
        with ExitStack() as tmp:
            index = sb("index", [P, 2, BATCH], U32, where=tmp)
            row = sb("row", [P, 2, BATCH, D], where=tmp)
            dots = sb("dots", [P, 2 * BATCH], where=tmp)
            idle = sb("idle", [P, 2], where=tmp)
            with stage() as (block, (index_ready, index_read, logits, gelued, weighted, v, idle_set, *_)):
                phases = [("peer_u", t) for t in range(TT)] + [("peer_v", t) for t in range(TT)]

                @block.gpsimd
                def _(pool):
                    nc.gpsimd.memset(idle[:, :], 0.0).then_inc(idle_set, 1)
                    pool.wait_ge(idle_set, 1)
                    for p, (table, t) in enumerate(phases):
                        def batch(g, s, again):
                            before = g * (2 * BATCH) + (2 * p * TURNS + s - 1) * BATCH
                            if again:
                                pool.wait_ge(index_read, before)
                                pool.wait_ge(row_used, before)
                            nc.gpsimd.tensor_copy(index[:, s, :],
                                                  experts[:, t, bass.ds(g * (2 * BATCH) + s * BATCH, BATCH)]
                                                  ).then_inc(index_ready, 1)
                            pool.wait_ge(index_ready, g * 2 + (2 * p * TURNS + s + 1))
                            nc.gpsimd.tensor_tensor(idle[:, 0:1], idle[:, 1:2], idle[:, 1:2], ALU.add)
                            for i in range(BATCH):
                                pool.indirect_dma_start(
                                    out=row[:, s, i, :], out_offset=None, in_=A[table],
                                    in_offset=bass.IndirectOffsetOnAxis(ap=index[:, s, i:i + 1], axis=0),
                                    engine_sem=index_read).then_inc(row_in[s][i], 16)
                        if p == 0:
                            batch(0, 0, False)
                            batch(0, 1, False)
                        with pool.Fori(1 if p == 0 else 0, TURNS) as g:
                            batch(g, 0, True)
                            batch(g, 1, True)

                @block.scalar
                def _(act):
                    for t in range(TT):
                        act.wait_ge(logits, t + 1)
                        nc.scalar.activation(weights[:, t, :], weights[:, t, :], ACT.Gelu).then_inc(gelued, 1)

                @block.vector
                def _(dve):
                    for t in range(TT):
                        nc.vector.memset(y_tok[:, t, :], 0.0).then_inc(v, 1)
                    dve.wait_ge(v, TT)
                    for t in range(TT):
                        with dve.Fori(0, TURNS) as g:
                            dve.wait_ge(v, g + (TT + t * TURNS))
                            for e in range(2 * BATCH):
                                dve.wait_ge(row_in[e // BATCH][e % BATCH], g * 16 + 16 * (t * TURNS + 1))
                                u_row = row[:, e // BATCH, e % BATCH, :]
                                nc.vector.tensor_tensor_reduce(u_row, u_row, h_tok[:, t, :], 1.0, 0.0, ALU.mult,
                                                               ALU.add, dots[:, e:e + 1]).then_inc(row_used, 1)
                            dve.wait_ge(row_used, g * (2 * BATCH) + (t * TURNS + 1) * 2 * BATCH)
                            nc.vector.tensor_scalar(weights[:, t, bass.ds(g * (2 * BATCH), 2 * BATCH)], dots[:, :],
                                                    1.0, None, ALU.mult).then_inc(v, 1)
                        dve.wait_ge(v, TT + (t + 1) * TURNS)
                        dve.sem_inc(logits, 1)
                    for t in range(TT):
                        dve.wait_ge(gelued, t + 1)
                        nc.vector.tensor_tensor(weights[:, t, :], weights[:, t, :], gates[:, t, :],
                                                ALU.mult).then_inc(weighted, 1)
                    dve.wait_ge(weighted, TT)
                    for t in range(TT):
                        turns = (TT + t) * TURNS
                        with dve.Fori(0, TURNS) as g:
                            for e in range(2 * BATCH):
                                dve.wait_ge(row_in[e // BATCH][e % BATCH], g * 16 + 16 * (turns + 1))
                                dve.wait_ge(row_used, g * (2 * BATCH) + (turns * 2 * BATCH + e))
                                nc.vector.scalar_tensor_tensor(y_tok[:, t, :], row[:, e // BATCH, e % BATCH, :],
                                                               weights[:, t, bass.ds(g * (2 * BATCH) + e, 1)],
                                                               y_tok[:, t, :], ALU.mult, ALU.add
                                                               ).then_inc(row_used, 1)

        with stage() as (block, (turned, *_)):
            @block.tensor
            def _(pe):
                for k in range(KT):
                    for t in range(TT):
                        last = nc.tensor.transpose(ps[:, k, t * P:(t + 1) * P], y_tok[:, t, k * P:(k + 1) * P],
                                                   mat("ident"))
                    last.then_inc(turned, 1)

            @block.vector
            def _(dve):
                for k in range(KT):
                    dve.wait_ge(turned, k + 1)
                    nc.vector.scalar_tensor_tensor(xT[:, k, :], ps[:, k, 0:S], mod[:, 40 + k:41 + k], xT[:, k, :],
                                                   ALU.mult, ALU.add)
        peer.close()

        def norm_w(layer, which):
            return lambda k: vec("norm_w", (layer * 3 + which) * KT + k)

        rms_norm(norm_w(0, 0), None)
        swiglu()
        rms_norm(norm_w(0, 1), None)

        even = ExitStack()
        ez = sb("ez", [P, T_EV, S], where=even)
        et = sb("et", [P, TT, T_EV_TOK * P], where=even)
        project(T_EV, hT, lambda i, src: nc.vector.tensor_scalar(one(ez, i), src, 1.0, None, ALU.mult),
                T_EV_TOK, lambda i, src: nc.vector.tensor_copy(et[:, :, i * P:(i + 1) * P], src))
        with ExitStack() as tmp, stage() as (block, (tables_in, gelu_u, gelu_v, root_in, root, centred, v, normed,
                                                     w_masked, gated, sq_done, sig, *_)):
            ws = sb("ws", [P, NH, P], where=tmp)
            gb = sb("gb", [P, 4, P], where=tmp)
            st2 = sb("st2", [P, 2, 16], where=tmp)
            vg = et[:, :, 0:512].rearrange("p t (h e) -> p t h e", e=HD)
            mean4 = st2[:, 0, :].rearrange("p (t h) -> p t h", t=TT).unsqueeze(3).broadcast_to([P, TT, NH, HD])
            var4 = st2[:, 1, :].rearrange("p (t h) -> p t h", t=TT).unsqueeze(3).broadcast_to([P, TT, NH, HD])
            sq4 = sq[:, 0:4, :].rearrange("p (t a) (h e) -> p t (a h) e", t=TT, e=HD)

            @block.sync
            def _(sp):
                sp.dma_start(ws[:, :, :], A["gm_w"]).then_inc(tables_in, 16)
                sp.dma_start(gb[:, :, :], A["gm_b"]).then_inc(tables_in, 16)

            @block.scalar
            def _(act):
                nc.scalar.activation(et[:, :, 0:512], et[:, :, 0:512], ACT.Gelu_apprx_tanh).then_inc(gelu_v, 1)
                nc.scalar.activation(ez[:, 0:4, :], ez[:, 0:4, :], ACT.Gelu_apprx_tanh).then_inc(gelu_u, 1)
                act.wait_ge(root_in, 1)
                nc.scalar.activation(st2[:, 1, :], st2[:, 1, :], ACT.Sqrt).then_inc(root, 1)
                nc.scalar.activation(et[:, :, 768:792], et[:, :, 768:792], ACT.Sigmoid)

            @block.vector
            def _(dve):
                n = counter()
                dve.wait_ge(tables_in, 32)
                causal = mat("upto0").unsqueeze(1).broadcast_to([P, NH, P])
                nc.vector.tensor_tensor(ws[:, :, :], ws[:, :, :], causal, ALU.mult).then_inc(w_masked, 1)
                dve.wait_ge(gelu_v, 1)
                nc.vector.tensor_reduce(st2[:, 0, :].rearrange("p (t h) -> p t h", t=TT), vg, AXX,
                                        ALU.add).then_inc(v, n.one())
                dve.wait_ge(v, n.now)
                nc.vector.tensor_scalar(st2[:, 0, :], st2[:, 0, :], 1.0 / HD, None, ALU.mult).then_inc(v, n.one())
                dve.wait_ge(v, n.now)
                nc.vector.tensor_tensor(vg, vg, mean4, ALU.subtract).then_inc(v, n.one())
                dve.wait_ge(v, n.now)
                nc.vector.tensor_tensor(sq4, vg, vg, ALU.mult).then_inc(v, n.one())
                dve.wait_ge(v, n.now)
                nc.vector.tensor_reduce(st2[:, 1, :].rearrange("p (t h) -> p t h", t=TT), sq4, AXX,
                                        ALU.add).then_inc(v, n.one())
                dve.wait_ge(v, n.now)
                nc.vector.tensor_scalar(st2[:, 1, :], st2[:, 1, :], 1.0 / HD, 1e-5, ALU.mult,
                                        ALU.add).then_inc(root_in, 1)
                dve.wait_ge(root, 1)
                nc.vector.reciprocal(st2[:, 1, :], st2[:, 1, :]).then_inc(v, n.one())
                dve.wait_ge(v, n.now)
                nc.vector.tensor_tensor(vg, vg, var4, ALU.mult).then_inc(normed, 1)
                dve.wait_ge(gelu_u, 1)
                for j in range(4):
                    dve.wait_ge(gated, j + 1)
                    m2 = mix[:, j, :].rearrange("p (c t) -> p c t", c=TT)
                    nc.vector.tensor_tensor(m2, ps[:, j, 0:S].rearrange("p (c t) -> p c t", c=TT),
                                            gb[:, j, :].unsqueeze(1).broadcast_to([P, TT, P]), ALU.add
                                            ).then_inc(v, n.one())
                    dve.wait_ge(v, n.now)
                    nc.vector.tensor_tensor(mix[:, j, :], mix[:, j, :], ez[:, j, :], ALU.mult)

            @block.tensor
            def _(pe):
                pe.wait_ge(w_masked, 1)
                pe.wait_ge(normed, 1)
                for j in range(4):
                    for h in (2 * j, 2 * j + 1):
                        for c in range(TT):
                            last = nc.tensor.matmul(ps[rows(h), j, c * P:(c + 1) * P], et[:, c, h * HD:(h + 1) * HD],
                                                    ws[:, h, :], start=True, stop=True)
                    last.then_inc(gated, 1)

        nsa = ExitStack()
        kcmp = sb("kcmp", [P, NC_CMP], where=nsa)
        vcmp = sb("vcmp", [NC_CMP, P], where=nsa)
        cmp_mask = sb("cmp_mask", [P, TT, NC_CMP], where=nsa)
        causal = sb("causal", [P, TT, S], where=nsa)
        any_cmp = sb("any_cmp", [P, TT], where=nsa)
        cmp_gate = sb("cmp_gate", [P, TT, NH], where=nsa)
        with ExitStack() as tmp, stage() as (block, (rope_in, w_in, rotated, v, pooled, hidden, hidden_ready, keys,
                                                     keys_copied, keys_rot, small_in, *_)):
            cos, sin = sb("cos", [P, S], where=tmp), sb("sin", [P, S], where=tmp)
            cosc, sinc = sb("cosc", [P, NC_CMP], where=tmp), sb("sinc", [P, NC_CMP], where=tmp)
            pe_cmp = sb("pe_cmp", [P, 2, 32], where=tmp)
            w1 = sb("w1", [P, 2, 32, HD], where=tmp)
            w2 = sb("w2", [P, 2, HD], where=tmp)
            blocks = sb("blocks", [P, 2, 32, NC_CMP], where=tmp)
            hc = sb("hc", [P, 2, NC_CMP], where=tmp)
            kraw = sb("kraw", [P, NC_CMP], where=tmp)
            krot = sb("krot", [P, NC_CMP], where=tmp)
            turned_qk = sb("turned_qk", [P, 6, S], where=tmp)
            roped = [4, 5, 6, 7, 10, 11]

            @block.sync
            def _(sp):
                for dst, name in ((cos[:, :], "cos"), (sin[:, :], "sin")):
                    sp.dma_start(dst, A[name]).then_inc(rope_in, 16)
                for dst, name in ((cosc[:, :], "cosc"), (sinc[:, :], "sinc"), (pe_cmp[:, :, :], "pe_cmp"),
                                  (cmp_mask[:, :, :], "cmp_mask"), (causal[:, :, :], "causal"),
                                  (any_cmp[:, :], "any_cmp")):
                    sp.dma_start(dst, A[name]).then_inc(small_in, 16)
                sp.dma_start(w1[:, :, :, :], A["cmp_w1"]).then_inc(w_in, 16)
                sp.dma_start(w2[:, :, :], A["cmp_w2"]).then_inc(w_in, 16)

            @block.tensor
            def _(pe):
                for n, i in enumerate(roped):
                    nc.tensor.matmul(ps[:, n // 2, n % 2 * S:n % 2 * S + S], mat("rotate"), ez[:, i, :], start=True,
                                     stop=True).then_inc(rotated, 1)
                pe.wait_ge(w_in, 32)
                pe.wait_ge(pooled, 2)
                for kv in range(2):
                    for g in range(2):
                        r = slice(g * HD, (g + 1) * HD)
                        for pos in range(32):
                            last = nc.tensor.matmul(ps[r, 3 + kv, 0:NC_CMP], w1[r, kv, pos, :],
                                                    blocks[r, kv, pos, :], start=(pos == 0), stop=(pos == 31))
                    last.then_inc(hidden, 1)
                pe.wait_ge(hidden_ready, 2)
                for g in range(2):
                    r = slice(g * HD, (g + 1) * HD)
                    nc.tensor.matmul(ps[r, 5, 0:NC_CMP], w2[r, 0, :], hc[r, 0, :], start=True, stop=True
                                     ).then_inc(keys, 1)
                    nc.tensor.matmul(ps[0:NC_CMP, 3 + g, r], hc[r, 1, :], w2[r, 1, :], start=True, stop=True
                                     ).then_inc(keys, 1)
                pe.wait_ge(keys_copied, 1)
                nc.tensor.matmul(ps[:, 7, 0:NC_CMP], mat("rotate"), kraw[:, :], start=True, stop=True
                                 ).then_inc(keys_rot, 1)

            @block.scalar
            def _(act):
                for kv in range(2):
                    act.wait_ge(hidden, kv + 1)
                    nc.scalar.activation(hc[:, kv, :], ps[:, 3 + kv, 0:NC_CMP], ACT.Gelu_apprx_tanh
                                         ).then_inc(hidden_ready, 1)
                act.wait_ge(keys, 4)
                for g in range(2):
                    r = slice(g * HD, (g + 1) * HD)
                    nc.scalar.activation(vcmp[:, r], ps[0:NC_CMP, 3 + g, r], ACT.Copy)

            @block.vector
            def _(dve):
                n = counter()
                dve.wait_ge(small_in, 16 * 6)
                for kv in range(2):
                    for part in range(2):
                        src = ez[:, 8 + kv, 16 * part:16 * part + 16 * NC_CMP].rearrange("p (n l) -> p l n", l=16)
                        nc.vector.tensor_tensor(blocks[:, kv, 16 * part:16 * part + 16, :], src,
                                                pe_cmp[:, kv, 16 * part:16 * part + 16].unsqueeze(2)
                                                .broadcast_to([P, 16, NC_CMP]), ALU.add).then_inc(v, n.one())
                dve.wait_ge(v, n.now)
                dve.sem_inc(pooled, 2)
                dve.wait_ge(rope_in, 32)
                dve.wait_ge(rotated, 6)
                nc.vector.tensor_tensor(turned_qk[:, :, :], ps[:, 0:3, :].rearrange("p b (c t) -> p (b c) t", t=S),
                                        sin[:, :].unsqueeze(1).broadcast_to([P, 6, S]), ALU.mult).then_inc(v, n.one())
                for a, b in ((4, 8), (10, 12)):
                    nc.vector.tensor_tensor(ez[:, a:b, :], ez[:, a:b, :],
                                            cos[:, :].unsqueeze(1).broadcast_to([P, b - a, S]),
                                            ALU.mult).then_inc(v, n.one())
                dve.wait_ge(v, n.now)
                nc.vector.tensor_tensor(ez[:, 4:8, :], ez[:, 4:8, :], turned_qk[:, 0:4, :], ALU.add)
                nc.vector.tensor_tensor(ez[:, 10:12, :], ez[:, 10:12, :], turned_qk[:, 4:6, :], ALU.add)
                gl = et[:, :, 768:792].rearrange("p t (h b) -> p t h b", b=3)
                nc.vector.tensor_tensor(cmp_gate[:, :, :], gl[:, :, :, 0:1].rearrange("p t h b -> p t (h b)"),
                                        any_cmp[:, :].unsqueeze(2).broadcast_to([P, TT, NH]), ALU.mult)
                dve.wait_ge(keys, 4)
                nc.vector.tensor_copy(kraw[:, :], ps[:, 5, 0:NC_CMP]).then_inc(keys_copied, 1)
                dve.wait_ge(keys_rot, 1)
                nc.vector.tensor_tensor(krot[:, :], ps[:, 7, 0:NC_CMP], sinc[:, :], ALU.mult).then_inc(v, n.one())
                dve.wait_ge(keys_copied, 1)
                nc.vector.tensor_tensor(kraw[:, :], kraw[:, :], cosc[:, :], ALU.mult).then_inc(v, n.one())
                dve.wait_ge(v, n.now)
                nc.vector.tensor_tensor(kcmp[:, :], kraw[:, :], krot[:, :], ALU.add)

        gl = et[:, :, 768:792].rearrange("p t (h b) -> p t h b", b=3)
        units = []
        for j in range(4):
            for g in range(2):
                h, r = j + 4 * g, slice(g * HD, (g + 1) * HD)
                base = dict(po=g * HD, j=4 + j, q=ez[r, 4 + j, :])
                units.append(dict(base, n=NC_CMP, k=kcmp[r, :], bias=cmp_mask[:, :, :], v=[vcmp[:, r]],
                                  gate=cmp_gate[:, :, h]))
                for b, keys_at, v_at in ((1, 10, 512), (2, 11, 640)):
                    units.append(dict(base, n=S, k=ez[r, keys_at, :], bias=causal[:, :, :],
                                      v=[et[:, t, v_at + g * HD:v_at + (g + 1) * HD] for t in range(TT)],
                                      gate=gl[:, :, h, b]))
        attention(units, mix, "nsa")
        nsa.close()
        even.close()
        project(T_OUT, mix, lambda i, src: nc.vector.tensor_tensor(one(xT, i), src, one(xT, i), ALU.add))
        rms_norm(norm_w(0, 2), None)
        swiglu()

        rms_norm(norm_w(1, 0), None)
        swiglu()
        rms_norm(norm_w(1, 1), None)
        odd = ExitStack()
        oz = sb("oz", [P, KT, S], where=odd)
        project(KT, hT, lambda i, src: nc.vector.tensor_scalar(one(oz, i), src, 1.0, None, ALU.mult))

        with ExitStack() as tmp, stage() as (block, (pool_in, v, pooled, mapped, *_)):
            pw = sb("pw", [P, 4, P], where=tmp)
            inv_count = sb("inv_count", [P, 4, S], where=tmp)
            sums_a = sb("sums_a", [P, 4, S], where=tmp)
            sums_b = sb("sums_b", [P, 4, S], where=tmp)

            @block.sync
            def _(sp):
                sp.dma_start(pw[:, :, :], A["pool_w"].rearrange("g c d -> c g d")).then_inc(pool_in, 16)
                sp.dma_start(inv_count[:, :, :], A["inv_count"]).then_inc(pool_in, 16)

            @block.vector
            def _(dve):
                n = counter()
                cur, nxt = oz[:, 0:4, :], sums_a[:, :, :]
                bufs = [sums_a[:, :, :], sums_b[:, :, :]]
                for lv in range(4):
                    shift = 1 << lv
                    nxt = bufs[lv % 2]
                    if lv:
                        nc.vector.tensor_copy(nxt[:, 0:lv, :], cur[:, 0:lv, :]).then_inc(v, n.one())
                    nc.vector.tensor_copy(nxt[:, lv:4, 0:shift], cur[:, lv:4, 0:shift]).then_inc(v, n.one())
                    nc.vector.tensor_tensor(nxt[:, lv:4, shift:S], cur[:, lv:4, shift:S], cur[:, lv:4, 0:S - shift],
                                            ALU.add).then_inc(v, n.one())
                    dve.wait_ge(v, n.now)
                    cur = nxt
                dve.wait_ge(pool_in, 32)
                nc.vector.tensor_tensor(sums_a[:, :, :], cur, inv_count[:, :, :], ALU.mult).then_inc(v, n.one())
                dve.wait_ge(v, n.now)
                nc.vector.tensor_tensor(sums_a[:, :, :], sums_a[:, :, :], oz[:, 0:4, :], ALU.subtract
                                        ).then_inc(pooled, 1)
                for g in range(4):
                    dve.wait_ge(mapped, g + 1)
                    nc.vector.tensor_scalar(mix[:, g, :], ps[:, g, 0:S], vec("pool_scale", g), None, ALU.mult)

            @block.tensor
            def _(pe):
                pe.wait_ge(pooled, 1)
                for g in range(4):
                    nc.tensor.matmul(ps[:, g, 0:S], pw[:, g, :], sums_a[:, g, :], start=True, stop=True
                                     ).then_inc(mapped, 1)

        s5 = ExitStack()
        decay = sb("decay", [P, S5T], where=s5)
        fre, fim = sb("fre", [P, S5T], where=s5), sb("fim", [P, S5T], where=s5)
        wre, wim = sb("wre", [P, S5T, S], where=s5), sb("wim", [P, S5T, S], where=s5)
        s5_b = sb("s5_b", [P, 4, 2, P], where=s5)
        s5_c = sb("s5_c", [P, 2, S5T, 32], where=s5)
        with ExitStack() as tmp, stage() as (block, (dt_ready, args, trig, v, b_in, half_in, *_)):
            dt = sb("dt", [P, S5T], where=tmp)
            t1, t2, t3, t4, th = (sb(f"t{i}", [P, S5T], where=tmp) for i in range(5))
            cre = sb("cre", [P, S5T, 32], where=tmp)
            big1, big2 = sb("big1", [P, S5T, P], where=tmp), sb("big2", [P, S5T, P], where=tmp)
            step_re, step_im = sb("step_re", [P, S5T], where=tmp), sb("step_im", [P, S5T], where=tmp)

            @block.sync
            def _(sp):
                sp.dma_start(s5_b[:, :, :, :], A["s5_b"]).then_inc(b_in, 16)
                sp.dma_start(s5_c[:, :, :, :], A["s5_c"]).then_inc(b_in, 16)

            @block.scalar
            def _(act):
                nc.scalar.activation(dt[:, :], vec_all("log_dt"), ACT.Exp).then_inc(dt_ready, 1)
                act.wait_ge(args, 1)
                nc.scalar.activation(decay[:, :], decay[:, :], ACT.Exp).then_inc(trig, 1)
                act.wait_ge(args, 2)
                nc.scalar.activation(t1[:, :], th[:, :], ACT.Sin).then_inc(trig, 1)
                nc.scalar.activation(t2[:, :], th[:, :], ACT.Sin, scale=0.5).then_inc(trig, 1)

            @block.vector
            def _(dve):
                n = counter()

                def step(ins):
                    ins.then_inc(v, n.one())
                    dve.wait_ge(v, n.now)
                tt, ts = nc.vector.tensor_tensor, nc.vector.tensor_scalar
                lre, lim = vec_all("lam_re"), vec_all("lam_im")
                dve.wait_ge(dt_ready, 1)
                tt(decay[:, :], lre, dt[:, :], ALU.mult).then_inc(args, 1)
                step(tt(th[:, :], lim, dt[:, :], ALU.mult))
                step(ts(t3[:, :], th[:, :], 1.0 / (2 * np.pi), None, ALU.mult))
                step(ts(t3[:, :], t3[:, :], 12582912.0, None, ALU.add))
                step(ts(t3[:, :], t3[:, :], -12582912.0, None, ALU.add))
                rest = 2 * np.pi
                for part in (6.28125, 0.0019350051879882812, float(2 * np.pi - 6.28125 - 0.0019350051879882812)):
                    step(nc.vector.scalar_tensor_tensor(th[:, :], t3[:, :], -part, th[:, :], ALU.mult, ALU.add))
                ts(th[:, :], th[:, :], 3.1415925, -3.1415925, ALU.min, ALU.max).then_inc(args, 1)
                dve.wait_ge(trig, 3)
                step(tt(t2[:, :], t2[:, :], t2[:, :], ALU.mult))
                step(ts(t2[:, :], t2[:, :], -2.0, 1.0, ALU.mult, ALU.add))
                tt(t4[:, :], decay[:, :], t1[:, :], ALU.mult).then_inc(v, n.one())
                step(tt(t3[:, :], decay[:, :], t2[:, :], ALU.mult))
                step(ts(t3[:, :], t3[:, :], -1.0, None, ALU.add))
                tt(fre[:, :], t3[:, :], lre, ALU.mult).then_inc(v, n.one())
                tt(fim[:, :], t4[:, :], lre, ALU.mult).then_inc(v, n.one())
                tt(th[:, :], t4[:, :], lim, ALU.mult).then_inc(v, n.one())
                step(tt(t3[:, :], t3[:, :], lim, ALU.mult))
                tt(fre[:, :], fre[:, :], th[:, :], ALU.add).then_inc(v, n.one())
                tt(fim[:, :], fim[:, :], t3[:, :], ALU.subtract).then_inc(v, n.one())
                tt(dt[:, :], lre, lre, ALU.mult).then_inc(v, n.one())
                step(tt(t4[:, :], lim, lim, ALU.mult))
                step(tt(dt[:, :], dt[:, :], t4[:, :], ALU.add))
                step(nc.vector.reciprocal(dt[:, :], dt[:, :]))
                tt(fre[:, :], fre[:, :], dt[:, :], ALU.mult).then_inc(v, n.one())
                step(tt(fim[:, :], fim[:, :], dt[:, :], ALU.mult))
                dve.wait_ge(b_in, 32)
                wide = [P, S5T, 32]
                fr, fi = fre[:, :].unsqueeze(2).broadcast_to(wide), fim[:, :].unsqueeze(2).broadcast_to(wide)
                tt(cre[:, :, :], s5_c[:, 0], fi, ALU.mult).then_inc(v, n.one())
                step(tt(big1[:, :, 0:32], s5_c[:, 1], fi, ALU.mult))
                tt(s5_c[:, 0], s5_c[:, 0], fr, ALU.mult).then_inc(v, n.one())
                step(tt(s5_c[:, 1], s5_c[:, 1], fr, ALU.mult))
                tt(s5_c[:, 0], s5_c[:, 0], big1[:, :, 0:32], ALU.subtract).then_inc(v, n.one())
                step(tt(s5_c[:, 1], s5_c[:, 1], cre[:, :, :], ALU.add))
                step(ts(s5_c[:, 1].rearrange("p a b -> p (a b)"), s5_c[:, 1].rearrange("p a b -> p (a b)"), -1.0, None,
                        ALU.mult))
                nc.vector.memset(wre[:, :, 0:1], 1.0).then_inc(v, n.one())
                nc.vector.memset(wim[:, :, 0:1], 0.0).then_inc(v, n.one())
                nc.vector.tensor_copy(step_re[:, :], t2[:, :]).then_inc(v, n.one())
                step(nc.vector.tensor_copy(step_im[:, :], t1[:, :]))
                size = 1
                while size < S:
                    low, high = slice(0, size), slice(size, 2 * size)
                    shape = [P, S5T, size]
                    sr = step_re[:, :].unsqueeze(2).broadcast_to(shape)
                    si = step_im[:, :].unsqueeze(2).broadcast_to(shape)
                    tt(wre[:, :, high], wre[:, :, low], sr, ALU.mult).then_inc(v, n.one())
                    tt(wim[:, :, high], wre[:, :, low], si, ALU.mult).then_inc(v, n.one())
                    tt(big1[:, :, low], wim[:, :, low], si, ALU.mult).then_inc(v, n.one())
                    tt(big2[:, :, low], wim[:, :, low], sr, ALU.mult).then_inc(v, n.one())
                    dve.wait_ge(v, n.now)
                    tt(wre[:, :, high], wre[:, :, high], big1[:, :, low], ALU.subtract).then_inc(v, n.one())
                    tt(wim[:, :, high], wim[:, :, high], big2[:, :, low], ALU.add).then_inc(v, n.one())
                    tt(t3[:, :], step_re[:, :], step_re[:, :], ALU.mult).then_inc(v, n.one())
                    tt(t4[:, :], step_im[:, :], step_im[:, :], ALU.mult).then_inc(v, n.one())
                    step(tt(th[:, :], step_re[:, :], step_im[:, :], ALU.mult))
                    tt(step_re[:, :], t3[:, :], t4[:, :], ALU.subtract).then_inc(v, n.one())
                    step(ts(step_im[:, :], th[:, :], 2.0, None, ALU.mult))
                    size *= 2

        with ExitStack() as tmp, stage() as (block, (fed, v, scanned, w, turned_back, out_ready, crossed, *_)):
            a1, a2, a3, a4 = (sb(f"a{i}", [P, S], where=tmp) for i in range(4))
            zre, zim = sb("zre", [P, 2, S], where=tmp), sb("zim", [P, 2, S], where=tmp)
            b1, b2, b3, b4 = (sb(f"b{i}", [P, S], where=tmp) for i in range(4))
            xre, xim = sb("xre", [P, 2, S], where=tmp), sb("xim", [P, 2, S], where=tmp)

            @block.tensor
            def _(pe):
                for s in range(S5T + 2):
                    if s < S5T:
                        if s >= 2:
                            pe.wait_ge(v, s - 1)
                        r = slice(32 * (s % 4), 32 * (s % 4) + 32)
                        for c in range(2):
                            last = nc.tensor.matmul(ps[:, s % 2, c * S:(c + 1) * S], s5_b[r, s // 4, c, :],
                                                    oz[r, 4 + s // 4, :], start=True, stop=True)
                        last.then_inc(fed, 1)
                    if s >= 2:
                        i = s - 2
                        pe.wait_ge(turned_back, i + 1)
                        r = slice(32 * (i % 4), 32 * (i % 4) + 32)
                        nc.tensor.matmul(ps[r, 2 + i // 4, 0:S], s5_c[:, 0, i, :], xre[:, i % 2, :], start=True,
                                         stop=False)
                        nc.tensor.matmul(ps[r, 2 + i // 4, 0:S], s5_c[:, 1, i, :], xim[:, i % 2, :], start=False,
                                         stop=True).then_inc(out_ready, 1)

            @block.vector
            def _(dve):
                tt = nc.vector.tensor_tensor
                n = counter()
                for s in range(S5T):
                    dve.wait_ge(fed, s + 1)
                    bre, bim = ps[:, s % 2, 0:S], ps[:, s % 2, S:2 * S]
                    if s:
                        dve.wait_ge(scanned, 2 * s)
                    tt(a1[:, :], bre, wre[:, s, :], ALU.mult).then_inc(w, n.one())
                    tt(a2[:, :], bim, wim[:, s, :], ALU.mult).then_inc(w, n.one())
                    tt(a3[:, :], bim, wre[:, s, :], ALU.mult).then_inc(w, n.one())
                    tt(a4[:, :], bre, wim[:, s, :], ALU.mult).then_inc(v, 1)
                    dve.wait_ge(w, n.now)
                    tt(a1[:, :], a1[:, :], a2[:, :], ALU.add).then_inc(w, n.one())
                    dve.wait_ge(v, s + 1)
                    tt(a3[:, :], a3[:, :], a4[:, :], ALU.subtract).then_inc(w, n.one())
                    dve.wait_ge(w, n.now)
                    if s >= 2:
                        dve.wait_ge(turned_back, s - 1)
                    nc.vector.tensor_tensor_scan(zre[:, s % 2, :], decay[:, s:s + 1].broadcast_to([P, S]), a1[:, :], 0.0, ALU.mult,
                                                 ALU.add).then_inc(scanned, 1)
                    nc.vector.tensor_tensor_scan(zim[:, s % 2, :], decay[:, s:s + 1].broadcast_to([P, S]), a3[:, :], 0.0, ALU.mult,
                                                 ALU.add).then_inc(scanned, 1)

            @block.gpsimd
            def _(pool):
                tt = nc.gpsimd.tensor_tensor
                for s in range(S5T):
                    pool.wait_ge(scanned, 2 * s + 2)
                    zr, zi, cr, ci = zre[:, s % 2, :], zim[:, s % 2, :], wre[:, s, :], wim[:, s, :]
                    if s:
                        pool.wait_ge(turned_back, s)
                    tt(b1[:, :], zr, cr, ALU.mult)
                    tt(b2[:, :], zi, ci, ALU.mult)
                    tt(b3[:, :], zr, ci, ALU.mult)
                    tt(b4[:, :], zi, cr, ALU.mult).then_inc(crossed, 1)
                    pool.wait_ge(crossed, s + 1)
                    if s >= 2:
                        pool.wait_ge(out_ready, s - 1)
                    tt(xre[:, s % 2, :], b1[:, :], b2[:, :], ALU.subtract)
                    tt(xim[:, s % 2, :], b3[:, :], b4[:, :], ALU.add).then_inc(turned_back, 1)

        with stage() as (block, (skipped, gelued, *_)):
            @block.vector
            def _(dve):
                for j in range(4):
                    nc.vector.scalar_tensor_tensor(oz[:, 4 + j, :], oz[:, 4 + j, :], vec("s5_d", j), ps[:, 2 + j, 0:S],
                                                   ALU.mult, ALU.add).then_inc(skipped, 1)

            @block.scalar
            def _(act):
                act.wait_ge(skipped, 4)
                nc.scalar.activation(oz[:, 4:8, :], oz[:, 4:8, :], ACT.Gelu_apprx_tanh)
        s5.close()

        with ExitStack() as tmp, stage() as (block, (sig_done, multiplied, *_)):
            sg = sb("sg", [P, 2, S], where=tmp)
            first = take(T_GLU)

            @block.sync
            def _(sp):
                refill(sp, first, T_GLU)

            @block.tensor
            def _(pe):
                for i in range(T_GLU):
                    slot, turn = (first + i) % RING, (first + i) // RING
                    pe.wait_ge(loaded[slot], 16 * turn + 16)
                    for q in range(2):
                        for k in range(4):
                            last = nc.tensor.matmul(ps[:, i, q * S:(q + 1) * S],
                                                    ring[:, slot, (4 * q + k) * P:(4 * q + k + 1) * P],
                                                    oz[:, 4 + k, :], start=(k == 0), stop=(k == 3))
                    last.then_inc(tiles_used, 1)

            @block.scalar
            def _(act):
                for i in range(T_GLU):
                    act.wait_ge(tiles_used, first + i + 1)
                    if i >= 2:
                        act.wait_ge(multiplied, i - 1)
                    nc.scalar.activation(sg[:, i % 2, :], ps[:, i, S:2 * S], ACT.Sigmoid).then_inc(sig_done, 1)

            @block.vector
            def _(dve):
                for i in range(T_GLU):
                    dve.wait_ge(sig_done, i + 1)
                    nc.vector.tensor_tensor(mix[:, 4 + i, :], ps[:, i, 0:S], sg[:, i % 2, :], ALU.mult
                                            ).then_inc(multiplied, 1)
        odd.close()
        project(KT, mix, lambda i, src: nc.vector.tensor_tensor(one(xT, i), src, one(xT, i), ALU.add))
        rms_norm(norm_w(1, 2), None)
        swiglu()
        rms_norm(lambda k: vec("final", k), None)
        assert stream[0] == TOTAL, (stream[0], TOTAL)
        with stage() as (block, _):
            @block.sync
            def _(sp):
                sp.dma_start(A["out"].rearrange("(k p) t -> p k t", p=P), hT[:, :, :]).then_inc(stored, 16)
                sp.wait_ge(stored, 16)


def tiles_of(w, order=None):
    k, n = w.shape
    t = w.reshape(k // P, P, n // P, P).transpose(2, 1, 0, 3).reshape(n // P, P, -1)
    return t if order is None else t[order]


def layout(a):
    f = {k: np.asarray(v) for k, v in a.items()}
    parts = [tiles_of(f["ada_w"][0]),
             tiles_of(f["w_in"][0], list(range(8, 12)) + list(range(0, 8)) + list(range(12, 26))),
             tiles_of(f["w_out"][0]), tiles_of(f["peer_w_query"][0])]

    def ffn(layer, which):
        g, u = tiles_of(f["ffn_w_gate_2"][layer, which]), tiles_of(f["ffn_w_up_2"][layer, which])
        d = f["ffn_w_down_2"][layer, which].reshape(FJ, P, D)
        seq = [g[0], u[0]]
        for j in range(1, FJ):
            seq += [g[j], u[j], d[j - 1]]
        return np.stack(seq + [d[FJ - 1]])
    parts.append(ffn(0, 0))
    w = f["ev_w_in_2"][0]
    q = w[:, 1024:1536].reshape(D, 2, 4, HD).transpose(0, 2, 1, 3).reshape(D, 512)
    kc, vc, ks, vs, kw, vw = (w[:, 1536 + P * i:1536 + P * i + P] for i in range(6))
    gl = np.zeros((D, P), np.float32)
    gl[:, :24] = w[:, 2304:2328]
    parts.append(tiles_of(np.concatenate([w[:, 512:1024], vs, vw, gl, w[:, 0:512], q, kc, vc, ks, kw], axis=1)))
    wo = f["ev_w_out_2"][0]
    parts.append(tiles_of(np.concatenate([wo[:512], wo[512:].reshape(2, 4, HD, D).transpose(1, 0, 2, 3)
                                          .reshape(512, D)], axis=0)))
    parts += [ffn(0, 1), ffn(1, 0), tiles_of(f["od_w_in_2"][0])]
    glu = f["s5_w_glu_2"][0]
    ab = np.stack([tiles_of(glu[:, :512]), tiles_of(glu[:, 512:])], axis=2)
    parts += [ab.reshape(4, P, D), tiles_of(f["od_w_out_2"][0]), ffn(1, 1)]
    out = {"stream": np.concatenate(parts, axis=0)}

    def cols(v):
        return np.asarray(v).reshape(-1, P).T
    vectors = {"c": cols(f["c"]), "ada_b": cols(f["ada_b"]), "norm1_g": cols(f["norm1_g"]), "mu_prev": cols(f["mu_prev"]),
               "mu_next": cols(f["mu_next"]), "w_decay0": cols(f["w_decay0"]), "a_gate0": cols(f["a_gate0"]),
               "k_k": cols(f["k_k"]), "k_a": cols(f["k_a"]), "r_k": cols(f["r_k"]), "lnx_g": cols(f["lnx_g"]),
               "lnx_b": cols(f["lnx_b"]), "norm2_g": cols(f["norm2_g"]), "q_norm_g": cols(np.tile(f["q_norm_g"][0], 2)),
               "k_norm_g": cols(np.tile(f["k_norm_g"][0], 2)), "norm_w": cols(f["norm_w_2"]),
               "final": cols(f["final_norm_w_2"]), "pool_scale": cols(f["pool_scale_2"]), "s5_d": cols(f["s5_d_2"]),
               "lam_re": cols(f["s5_lam_re_2"]), "lam_im": cols(f["s5_lam_im_2"]),
               "log_dt": cols(np.repeat(f["s5_log_dt_2"][0], 64))}
    out["vecs"] = np.concatenate([vectors[n] for n in VEC], axis=1)
    out["xT"] = f["x"][0].T
    out["mats"] = constant_matrices()
    out["lora_up"] = np.concatenate([f["w_decay_up"][0].transpose(1, 0, 2), f["a_gate_up"][0].transpose(1, 0, 2)], 0)
    out["g_up"] = f["g_up"][0]
    out["subkeys"] = np.stack([f["peer_sub_keys1"][0].T, f["peer_sub_keys2"][0].T], axis=1)
    out["peer_u"], out["peer_v"] = f["peer_u"][0], f["peer_v"][0]
    out["gm_w"] = f["gm_w_s_2"][0].transpose(2, 0, 1)
    out["gm_b"] = np.repeat(f["gm_b_2"][0].reshape(4, 2, P), HD, axis=1).transpose(1, 0, 2)
    out["cmp_w1"] = np.tile(f["nsa_cmp_w1_2"][0].reshape(2, 32, HD, HD).transpose(2, 0, 1, 3), (2, 1, 1, 1))
    out["cmp_w2"] = np.tile(f["nsa_cmp_w2_2"][0].transpose(1, 0, 2), (2, 1, 1))
    out["pe_cmp"] = np.tile(f["nsa_cmp_pe_2"][0].transpose(2, 0, 1), (2, 1, 1))
    out["pool_w"] = f["pool_w_2"][0]
    b = np.zeros((4, 4, 2, 16, 2, 2, 64), np.float32)
    c = np.zeros((2, 64, 2, S5T, 2, 16), np.float32)
    for i, (bb, cc) in enumerate(((f["s5_b_re_2"][0], f["s5_c_re_2"][0]), (f["s5_b_im_2"][0], f["s5_c_im_2"][0]))):
        bb = bb.reshape(4, 4, 2, 64, 16)
        cc = cc.reshape(S5T, 2, 16, 64)
        for g in range(2):
            b[:, :, g, :, i, g, :] = bb[:, :, g].transpose(0, 1, 3, 2)
            c[g, :, i, :, g, :] = cc[:, g].transpose(2, 0, 1)
    out["s5_b"] = b.reshape(4, P, 2, P).transpose(1, 0, 2, 3)
    out["s5_c"] = c.reshape(P, 2, S5T, 32)

    t = np.arange(S)
    dist = np.abs(t[:, None] - t[None, :])
    patterns = ((128, 1), (512, 4), (2048, 16))
    seen = sum(((dist % d == 0) & (dist <= w // 2)).astype(np.float32) for w, d in patterns)
    slopes = np.exp2(-8.0 * (np.arange(NH, dtype=np.float32) + 1) / NH).astype(np.float32)
    logs = np.where(seen > 0, np.log(np.maximum(seen, 1)), NEG).astype(np.float32)
    out["attn_bias"] = (logs[None] - slopes[:, None, None] * dist[None].astype(np.float32)).astype(np.float32)
    out["causal"] = np.where(t[None, :] <= t[:, None], 0, NEG).astype(np.float32).reshape(TT, P, S).transpose(1, 0, 2)
    end = np.arange(NC_CMP) * 16 + 31
    valid = end[None, :] <= t[:, None]
    out["cmp_mask"] = np.where(valid, 0, NEG).astype(np.float32).reshape(TT, P, NC_CMP).transpose(1, 0, 2)
    out["any_cmp"] = valid.any(axis=1).astype(np.float32).reshape(TT, P).T
    half = HD // 2
    inv = np.float32(10000.0) ** (-np.arange(half, dtype=np.float32) / half)
    for pos, tag in ((t, ""), (end, "c")):
        ang = pos.astype(np.float32)[None, :] * np.tile(inv, 4)[:, None]
        out["cos" + tag], out["sin" + tag] = np.cos(ang).astype(np.float32), np.sin(ang).astype(np.float32)
    counts = np.minimum(t[None, :] + 1, np.array([2, 4, 8, 16])[:, None]).astype(np.float32)
    out["inv_count"] = np.broadcast_to((1 / counts).astype(np.float32), (P, 4, S))
    return {k: np.ascontiguousarray(v) for k, v in out.items()}


def kernel(**inputs):
    import concourse.bacc as bacc
    from concourse.bass_utils import run_bass_kernel_spmd

    nc = bacc.Bacc("TRN2", target_bir_lowering=False, num_devices=1)
    arrays = {"in_" + k: v for k, v in layout(inputs).items()}
    aps = {k[3:]: nc.dram_tensor(k, v.shape, F32, kind="ExternalInput").ap() for k, v in arrays.items()}
    aps["out"] = nc.dram_tensor("out_xT", (D, S), F32, kind="ExternalOutput").ap()
    build(nc, aps)
    result = run_bass_kernel_spmd(nc, [arrays], core_ids=[0]).results[0]["out_xT"]
    return np.ascontiguousarray(np.asarray(result).T).reshape(1, S, D)
```

```python
from contextlib import ExitStack, contextmanager

import numpy as np

import concourse.bass as bass
from concourse import mybir

F32 = mybir.dt.float32
F32R = mybir.dt.float32r
U32 = mybir.dt.uint32
ACT = mybir.ActivationFunctionType
ALU = mybir.AluOpType
AXX = mybir.AxisListType.X

P = 128
S = 256
TT = S // P
D = 1024
KT = D // P
HD = 64
NH = 8
RING = 6
PAIRS = 3
AHEAD = 2
FFN = 2816
FJ = FFN // P
NE = 128
TOPK = 16
SLOTS = NH * TOPK
NEG = -1e30
NC_CMP = (S - 32) // 16 + 1
S5T = 16
NORM_EPS = 1e-6

T_ADA, T_IN_TOK, T_IN, T_OUT, T_QUERY = 48, 4, 22, 8, 16
T_FFN = 3 * FJ
T_EV_TOK, T_EV, T_GLU = 8, 12, 4
TOTAL = (T_ADA + T_IN_TOK + T_IN + T_OUT + T_QUERY + 4 * T_FFN + T_EV_TOK + T_EV + T_OUT + KT + T_GLU + KT)

VEC = {}
_at = 0
for _name, _n in (("c", 8), ("ada_b", 48), ("norm1_g", 8), ("mu_prev", 14), ("mu_next", 14), ("w_decay0", 8), ("a_gate0", 8),
                  ("k_k", 4), ("k_a", 4), ("r_k", 4), ("lnx_g", 4), ("lnx_b", 4), ("norm2_g", 8), ("q_norm_g", 1),
                  ("k_norm_g", 1), ("norm_w", 48), ("final", 8), ("pool_scale", 4), ("s5_d", 4), ("lam_re", S5T),
                  ("lam_im", S5T), ("log_dt", S5T)):
    VEC[_name] = (_at, _at + _n)
    _at += _n
NVEC = _at

MATS = ["ident", "ones", "blockones", "rotate"]
for _d in range(2):
    MATS += [f"strict{_d}", f"upto{_d}"] + [f"level{_d}_{b}" for b in (1, 2, 4, 8, 16, 32, 64)]
MATS += ["level_row0", "level_row1"]
MAT = {n: i for i, n in enumerate(MATS)}


def constant_matrices():
    t = np.arange(P)
    a, b = t[:, None], t[None, :]
    out = np.zeros((len(MATS), P, P), np.float32)
    out[MAT["ident"]] = a == b
    out[MAT["ones"]] = 1
    out[MAT["blockones"]] = a // HD == b // HD
    half = HD // 2
    rot = np.zeros((P, P), np.float32)
    for m in range(P):
        rot[(m + half, m) if m % HD < half else (m - half, m)] = -1 if m % HD < half else 1
    out[MAT["rotate"]] = rot
    for d in range(2):
        later = (b > a) if d == 0 else (b < a)
        out[MAT[f"strict{d}"]] = later
        out[MAT[f"upto{d}"]] = later | (a == b)
        for n in (1, 2, 4, 8, 16, 32, 64):
            out[MAT[f"level{d}_{n}"]] = later & (a // (2 * n) == b // (2 * n)) & (a // n != b // n)
        out[MAT[f"level_row{d}"]] = out[MAT[f"level{d}_1"]].T
    return out


class counter:
    def __init__(self):
        self.now = 0

    def __call__(self):
        self.now += 1
        return self.now

    def one(self):
        self.now += 1
        return 1


def over_tiles(eng, first, count, body):
    turns = count // RING if count >= 2 * RING else 0
    if turns:
        with eng.Fori(0, turns) as g:
            for u in range(RING):
                body(g * RING + u, (first + u) % RING, g + (first + u) // RING)
    for i in range(turns * RING, count):
        body(i, (first + i) % RING, (first + i) // RING)


def build(nc, A):
    with ExitStack() as ctx:
        def sb(name, shape, dt=F32, where=ctx):
            return where.enter_context(nc.sbuf_tensor(name, shape, dt))

        def sem(name):
            return ctx.enter_context(nc.semaphore(name))

        ring = sb("ring", [P, RING, D])
        xT = sb("xT", [P, KT, S])
        hT = sb("hT", [P, KT, S])
        srch, srcl = sb("srch", [P, KT, S], F32R), sb("srcl", [P, KT, S], F32R)
        wh, wl = sb("wh", [P, PAIRS, D], F32R), sb("wl", [P, PAIRS, D], F32R)
        mix = sb("mix", [P, KT, S])
        sq = sb("sq", [P, KT, S])
        rstd = sb("rstd", [P, S])
        vecs = sb("vecs", [P, NVEC])
        mats = sb("mats", [P, len(MATS), P])
        mod = sb("mod", [P, 48])
        gs = sb("gs", [P, 2, KT])
        ps = ctx.enter_context(nc.psum_tensor("ps", [P, 8, 512], F32))

        loaded = [sem(f"tile_loaded{i}") for i in range(RING)]
        high_done = sem("high_done")
        tiles_freed = sem("tiles_freed")
        tiles_used = sem("tiles_used")
        consts_in = sem("consts_in")
        table_in = sem("table_in")
        stored = sem("stored")
        tables = counter()
        sets = [[sem(f"stage{j}_{i}") for i in range(14)] for j in range(2)]
        stages = [0]
        stream = [0]

        def vec(name, i=0):
            return vecs[:, VEC[name][0] + i:VEC[name][0] + i + 1]

        def vec_all(name):
            return vecs[:, VEC[name][0]:VEC[name][1]]

        def mat(name):
            return mats[:, MAT[name], :]

        @contextmanager
        def stage():
            mine, other = sets[stages[0] % 2], sets[1 - stages[0] % 2]
            again = stages[0] > 0
            stages[0] += 1
            with nc.Block() as block:
                if again:
                    @block.gpsimd
                    def _(pool):
                        pool.sem_clear(range(other[0].num, other[0].num + len(other)))
                yield block, mine

        def take(count):
            stream[0] += count
            return stream[0] - count

        def refill(sp, first, count):
            def load(i, slot, turn):
                sp.wait_ge(tiles_freed, i + (first + 1))
                sp.dma_start(ring[:, slot, :], A["stream"][bass.ds(i + (first + RING), 1)]
                             .rearrange("a p n -> (a p) n")).then_inc(loaded[slot], 16)
            over_tiles(sp, first, min(count, TOTAL - RING - first), load)

        with stage() as (block, _):
            @block.sync
            def _(sp):
                for i in range(RING):
                    sp.dma_start(ring[:, i, :], A["stream"][i]).then_inc(loaded[i], 16)

            @block.scalar
            def _(act):
                act.dma_start(vecs[:, :], A["vecs"]).then_inc(consts_in, 16)
                act.dma_start(xT[:, :, :], A["xT"].rearrange("(k p) t -> p k t", p=P)).then_inc(consts_in, 16)
                act.dma_start(mats[:, :, :], A["mats"].rearrange("m p n -> p m n")).then_inc(consts_in, 16)
                act.wait_ge(consts_in, 48)

        def high(act, tile, turns=0):
            n = tile - T_ADA
            act.wait_ge(loaded[tile % RING], turns * 16 + 16 * (tile // RING + 1))
            if n >= PAIRS:
                act.wait_ge(tiles_used, turns * RING + (n - PAIRS + 1))
            nc.scalar.activation(wh[:, n % PAIRS, :], ring[:, tile % RING, :], ACT.Copy).then_inc(high_done, 1)

        def low(dve, tile, turns=0):
            n = tile - T_ADA
            dve.wait_ge(high_done, turns * RING + (n + 1))
            nc.vector.tensor_tensor(wl[:, n % PAIRS, :], ring[:, tile % RING, :],
                                    wh[:, n % PAIRS, :].bitcast(F32), ALU.subtract).then_inc(tiles_freed, 1)

        def product(out, tile, k, source, start, stop, turns=0, token_major=False, src=None):
            n = (tile - T_ADA) % PAIRS
            cols = slice(k * S, (k + 1) * S) if token_major else slice(k * P, (k + 1) * P)
            w = wh[:, n, cols], wl[:, n, cols]
            for p, (a, b) in enumerate(((0, 0), (0, 1), (1, 0))):
                left, right = (source[b], w[a]) if token_major else (w[a], source[b])
                last = nc.tensor.matmul(out, left, right, start=(start and p == 0), stop=(stop and p == 2),
                                        skip_group_check=True)
            return last

        def split_high(act, src, gain, done):
            for k in range(KT):
                nc.scalar.activation(srch[:, k, :], src[:, k, :], ACT.Copy, scale=gain(k) if gain else 1.0
                                     ).then_inc(done, 1)

        def split_low(dve, src, gain, high_part, done):
            for k in range(KT):
                dve.wait_ge(high_part, k + 1)
                nc.vector.scalar_tensor_tensor(srcl[:, k, :], src[:, k, :], gain(k) if gain else 1.0,
                                               srch[:, k, :].bitcast(F32), ALU.mult, ALU.subtract).then_inc(done, 1)

        CHUNKS = 6 * D // D
        with ExitStack() as tmp, stage() as (block, (c_ready, columns, v, *_)):
            cs = sb("cs", [P, KT], where=tmp)
            acc = sb("acc", [P, CHUNKS, D], where=tmp)
            first = take(T_ADA)

            @block.sync
            def _(sp):
                refill(sp, first, T_ADA)

            @block.scalar
            def _(act):
                nc.scalar.activation(cs[:, :], vec_all("c"), ACT.Silu).then_inc(c_ready, 1)
                for n in range(AHEAD):
                    high(act, T_ADA + n)

            @block.vector
            def _(dve):
                dve.wait_ge(c_ready, 1)
                assert CHUNKS == RING
                for u in range(CHUNKS):
                    dve.wait_ge(loaded[u], 16)
                    nc.vector.tensor_scalar(acc[:, u, :], ring[:, u, :], cs[:, 0:1], None, ALU.mult
                                            ).then_inc(tiles_freed, 1)
                with dve.Fori(1, KT) as g:
                    for u in range(CHUNKS):
                        dve.wait_ge(loaded[u], g * 16 + 16)
                        dve.wait_ge(tiles_freed, g * RING + u)
                        nc.vector.scalar_tensor_tensor(acc[:, u, :], ring[:, u, :], cs[:, bass.ds(g, 1)],
                                                       acc[:, u, :], ALU.mult, ALU.add).then_inc(tiles_freed, 1)
                for n in range(AHEAD):
                    low(dve, T_ADA + n)
                dve.wait_ge(columns, 1)
                nc.vector.tensor_tensor(mod[:, :], ps[:, 0, 0:48], vec_all("ada_b"), ALU.add).then_inc(v, 1)
                dve.wait_ge(v, 1)
                for n, name in ((0, "norm1_g"), (1, "norm2_g")):
                    nc.vector.scalar_tensor_tensor(gs[:, n, :], mod[:, 24 * n + 8:24 * n + 16], 1.0, vec_all(name),
                                                   ALU.add, ALU.mult)

            @block.tensor
            def _(pe):
                for u in range(CHUNKS):
                    pe.wait_ge(tiles_freed, first + T_ADA - CHUNKS + u + 1)
                    for j in range(KT):
                        last = nc.tensor.matmul(ps[:, 0, u * KT + j:u * KT + j + 1], acc[:, u, j * P:(j + 1) * P],
                                                mat("ones")[:, 0:1], start=True, stop=True)
                last.then_inc(columns, 1)

        def rms_norm(gain, shift):
            with stage() as (block, (squared, summed, scaled, root, v, *_)):
                @block.scalar
                def _(act):
                    for k in range(KT):
                        nc.scalar.activation(sq[:, k, :], xT[:, k, :], ACT.Square).then_inc(squared, 1)
                    act.wait_ge(scaled, 1)
                    nc.scalar.activation(rstd[:, :], rstd[:, :], ACT.Sqrt).then_inc(root, 1)

                @block.tensor
                def _(pe):
                    for k in range(KT):
                        pe.wait_ge(squared, k + 1)
                        last = nc.tensor.matmul(ps[:, 0, 0:S], mat("ones"), sq[:, k, :], start=(k == 0),
                                                stop=(k == KT - 1))
                    last.then_inc(summed, 1)

                @block.vector
                def _(dve):
                    n = counter()
                    dve.wait_ge(summed, 1)
                    nc.vector.tensor_scalar(rstd[:, :], ps[:, 0, 0:S], 1.0 / D, NORM_EPS, ALU.mult,
                                            ALU.add).then_inc(scaled, 1)
                    dve.wait_ge(root, 1)
                    nc.vector.reciprocal(rstd[:, :], rstd[:, :]).then_inc(v, 1)
                    dve.wait_ge(v, n())
                    for k in range(KT):
                        nc.vector.scalar_tensor_tensor(hT[:, k, :], xT[:, k, :], gain(k), rstd[:, :], ALU.mult,
                                                       ALU.mult).then_inc(v, n.one())
                    if shift:
                        for k in range(KT):
                            dve.wait_ge(v, k + 2)
                            nc.vector.tensor_scalar(hT[:, k, :], hT[:, k, :], shift(k), None, ALU.add)

        def mean_square(pe, squared, summed):
            for k in range(KT):
                pe.wait_ge(squared, k + 1)
                last = nc.tensor.matmul(ps[:, 3, 0:S], mat("ones"), sq[:, k, :], start=(k == 0), stop=(k == KT - 1))
            last.then_inc(summed, 1)

        def take_rstd(dve, summed, scaled, root, inverted):
            dve.wait_ge(summed, 1)
            nc.vector.tensor_scalar(rstd[:, :], ps[:, 3, 0:S], 1.0 / D, NORM_EPS, ALU.mult, ALU.add).then_inc(scaled, 1)
            dve.wait_ge(root, 1)
            nc.vector.reciprocal(rstd[:, :], rstd[:, :]).then_inc(inverted, 1)
            dve.wait_ge(inverted, 1)

        def project(count, src, evacuate, tok_count=0, tok_evacuate=None, gain=None):
            with stage() as (block, (bank_free, src_high, src_low, squared, summed, scaled, root, inverted, *_)):
                first = take(tok_count + count)
                total = tok_count + count
                splits = min(total, TOTAL - AHEAD - first)

                def bank(i):
                    return i - tok_count + tok_count // 2

                @block.sync
                def _(sp):
                    refill(sp, first, total)

                @block.scalar
                def _(act):
                    split_high(act, src, gain, src_high)
                    if gain:
                        for k in range(KT):
                            nc.scalar.activation(sq[:, k, :], src[:, k, :], ACT.Square).then_inc(squared, 1)
                        high(act, first + AHEAD)
                        act.wait_ge(scaled, 1)
                        nc.scalar.activation(rstd[:, :], rstd[:, :], ACT.Sqrt).then_inc(root, 1)
                    else:
                        high(act, first + AHEAD)
                    begin = 1
                    turns = (splits - begin) // RING
                    if turns >= 2:
                        with act.Fori(0, turns) as g:
                            for u in range(RING):
                                high(act, first + AHEAD + begin + u, g)
                    else:
                        turns = 0
                    for i in range(begin + turns * RING, splits):
                        high(act, first + AHEAD + i)

                @block.tensor
                def _(pe):
                    for i in range(tok_count):
                        pe.wait_ge(tiles_freed, first + i + 1)
                        if i % 2 == 0:
                            pe.wait_ge(bank_free, i // 2 + 1)
                        for k in range(KT // 2):
                            src_k = i % 2 * (KT // 2) + k
                            if i < 2:
                                pe.wait_ge(src_low, src_k + 1)
                            for t in range(TT):
                                begins, ends = i % 2 == 0 and k == 0, i % 2 == 1 and k == KT // 2 - 1
                                cols = slice(t * P, (t + 1) * P)
                                last = product(ps[:, i // 2 % 2, t * S:(t + 1) * S], first + i, k,
                                               (srch[:, src_k, cols], srcl[:, src_k, cols]), begins and t == 0, ends,
                                               token_major=True)
                        last.then_inc(tiles_used, 1)

                    def tile(i, turns=0):
                        b = bank(i)
                        pe.wait_ge(tiles_freed, turns * RING + (first + i + 1))
                        pe.wait_ge(bank_free, turns * RING + (b + 1))
                        for k in range(KT):
                            if i == 0:
                                pe.wait_ge(src_low, k + 1)
                            last = product(ps[:, b % 2, 0:S], first + i, k, (srch[:, k, :], srcl[:, k, :]), k == 0,
                                           k == KT - 1)
                        last.then_inc(tiles_used, 1)
                    begin = tok_count
                    if gain:
                        tile(0)
                        mean_square(pe, squared, summed)
                        begin = 1
                    turns = (total - begin) // RING
                    if turns >= 2:
                        with pe.Fori(0, turns) as g:
                            for u in range(RING):
                                tile(begin + u, g)
                    else:
                        turns = 0
                    for i in range(begin + turns * RING, total):
                        tile(i)

                @block.vector
                def _(dve):
                    dve.sem_inc(bank_free, 2)
                    split_low(dve, src, gain, src_high, src_low)
                    if gain:
                        low(dve, first + AHEAD)
                        take_rstd(dve, summed, scaled, root, inverted)

                    def out(i, turns=0, at=None):
                        dve.wait_ge(tiles_used, turns * RING + (first + i - T_ADA + 1))
                        evacuate((i if at is None else at) - tok_count, ps[:, bank(i) % 2, 0:S]).then_inc(bank_free, 1)
                    for i in range(tok_count):
                        low(dve, first + AHEAD + i)
                        if i % 2:
                            dve.wait_ge(tiles_used, first + i - T_ADA + 1)
                            tok_evacuate(i // 2, ps[:, i // 2 % 2, :].rearrange("p (t f) -> p t f", t=TT)
                                         ).then_inc(bank_free, 1)
                    begin = tok_count
                    if gain:
                        out(0)
                        begin = 1
                    turns = (splits - begin) // RING
                    if turns >= 2:
                        with dve.Fori(0, turns) as g:
                            for u in range(RING):
                                low(dve, first + AHEAD + begin + u, g)
                                out(begin + u, g, g * RING + (begin + u))
                    else:
                        turns = 0
                    for i in range(begin + turns * RING, total):
                        if i < splits:
                            low(dve, first + AHEAD + i)
                        out(i)

        def one(tensor, i):
            return tensor[:, bass.ds(i, 1), :].rearrange("p a t -> p (a t)")

        def swiglu(gain):
            with ExitStack() as tmp, stage() as (block, (src_high, src_low, squared, summed, scaled, root, inverted,
                                                         gate_ready, silu_done, up_ready, hid_ready, hid_high, act_ready,
                                                         *_)):
                tag = stream[0]
                gt, up, hid = (sb(f"{n}{tag}", [P, 2, S], where=tmp) for n in ("gt", "up", "hid"))
                hidh, hidl = (sb(f"{n}{tag}", [P, 2, S], F32R, where=tmp) for n in ("hidh", "hidl"))
                first = take(T_FFN)
                ACC = 4
                splits = min(T_FFN, TOTAL - AHEAD - first) + AHEAD

                def used(at):
                    return first - T_ADA + at + 1

                @block.sync
                def _(sp):
                    refill(sp, first, T_FFN)

                @block.tensor
                def _(pe):
                    def gate_up(j, at, turns=0):
                        if j >= 2:
                            pe.wait_ge(up_ready, turns * 2 + (j - 1))
                        for q in range(2):
                            pe.wait_ge(tiles_freed, turns * RING + (first + at + q + 1))
                            for k in range(KT):
                                if j == 0 and q == 0:
                                    pe.wait_ge(src_low, k + 1)
                                last = product(ps[:, j % 2, q * S:(q + 1) * S], first + at + q, k,
                                               (srch[:, k, :], srcl[:, k, :]), k == 0, k == KT - 1)
                            last.then_inc(tiles_used, 1)

                    def down(j, at, turns=0, begin=False, end=False):
                        pe.wait_ge(act_ready, turns * 2 + (j + 1))
                        pe.wait_ge(tiles_freed, turns * RING + (first + at + 1))
                        for d in range(KT):
                            last = product(ps[:, ACC + d // 2, d % 2 * S:(d % 2 + 1) * S], first + at, d,
                                           (hidh[:, j % 2, :], hidl[:, j % 2, :]), begin and d % 2 == 0, end)
                        last.then_inc(tiles_used, 1)

                    gate_up(0, 0)
                    mean_square(pe, squared, summed)
                    gate_up(1, 2)
                    down(0, 4, begin=True)
                    gate_up(2, 5)
                    down(1, 7)
                    with pe.Fori(0, FJ // 2 - 2) as g:
                        gate_up(3, 8, g)
                        down(2, 10, g)
                        gate_up(4, 11, g)
                        down(3, 13, g)
                    gate_up(FJ - 1, T_FFN - 4)
                    down(FJ - 2, T_FFN - 2)
                    down(FJ - 1, T_FFN - 1, end=True)

                def hidden_tiles(eng, step):
                    step(0)
                    step(1)
                    with eng.Fori(0, FJ // 2 - 2) as g:
                        step(2, g)
                        step(3, g)
                    step(FJ - 2)
                    step(FJ - 1)

                @block.scalar
                def _(act):
                    split_high(act, xT, gain, src_high)
                    for k in range(KT):
                        nc.scalar.activation(sq[:, k, :], xT[:, k, :], ACT.Square).then_inc(squared, 1)
                    high(act, first + AHEAD)
                    act.wait_ge(scaled, 1)
                    nc.scalar.activation(rstd[:, :], rstd[:, :], ACT.Sqrt).then_inc(root, 1)

                    def step(j, turns=0):
                        def weight(at):
                            if at < splits:
                                high(act, first + at, turns)
                        weight(3 * j + 3)
                        act.wait_ge(gate_ready, turns * 2 + (j + 1))
                        nc.scalar.activation(gt[:, j % 2, :], gt[:, j % 2, :], ACT.Silu).then_inc(silu_done, 1)
                        weight(3 * j + 4)
                        weight(3 * j + 5)
                        act.wait_ge(hid_ready, turns * 2 + (j + 1))
                        if j >= 2:
                            act.wait_ge(tiles_used, turns * RING + used(3 * (j - 2) + 4))
                        nc.scalar.activation(hidh[:, j % 2, :], hid[:, j % 2, :], ACT.Copy).then_inc(hid_high, 1)
                    hidden_tiles(act, step)

                @block.vector
                def _(dve):
                    split_low(dve, xT, gain, src_high, src_low)
                    low(dve, first + AHEAD)
                    take_rstd(dve, summed, scaled, root, inverted)

                    def step(j, turns=0):
                        def weight(at):
                            if at < splits:
                                low(dve, first + at, turns)
                        weight(3 * j + 3)
                        dve.wait_ge(tiles_used, turns * RING + used(1 if j == 0 else 3 * j))
                        nc.vector.tensor_tensor(gt[:, j % 2, :], ps[:, j % 2, 0:S], rstd[:, :], ALU.mult
                                                ).then_inc(gate_ready, 1)
                        nc.vector.tensor_tensor(up[:, j % 2, :], ps[:, j % 2, S:2 * S], rstd[:, :], ALU.mult
                                                ).then_inc(up_ready, 1)
                        weight(3 * j + 4)
                        dve.wait_ge(silu_done, turns * 2 + (j + 1))
                        dve.wait_ge(up_ready, turns * 2 + (j + 1))
                        nc.vector.tensor_tensor(hid[:, j % 2, :], up[:, j % 2, :], gt[:, j % 2, :], ALU.mult
                                                ).then_inc(hid_ready, 1)
                        weight(3 * j + 5)
                        dve.wait_ge(hid_high, turns * 2 + (j + 1))
                        nc.vector.tensor_tensor(hidl[:, j % 2, :], hid[:, j % 2, :], hidh[:, j % 2, :].bitcast(F32),
                                                ALU.subtract).then_inc(act_ready, 1)
                    hidden_tiles(dve, step)
                    dve.wait_ge(tiles_used, used(T_FFN - 1))
                    for b in range(4):
                        pair = xT[:, 2 * b:2 * b + 2, :].rearrange("p a t -> p (a t)")
                        nc.vector.scalar_tensor_tensor(pair, ps[:, ACC + b, :], 0.5, pair, ALU.mult, ALU.add)

        def attention(units, out, tag):
            U = len(units)
            WIDE = max(u["n"] for u in units)
            with ExitStack() as tmp, stage() as (block, (scored, shifted, maxed, exped, probs_ready, turned, turned_back,
                                                         out_ready, out_copied, v, a, *_)):
                sc = sb(f"sc_{tag}", [P, 2, TT, WIDE], where=tmp)
                pT = sb(f"pT_{tag}", [P, 2, TT, S], where=tmp)
                stat = sb(f"stat_{tag}", [P, U, 6], where=tmp)

                done = [u for u in range(U) if u == U - 1 or units[u + 1]["j"] != units[u]["j"]]

                @block.tensor
                def _(pe):
                    for step in range(U + 2):
                        if step < U:
                            u = units[step]
                            if step >= 2:
                                pe.wait_ge(shifted, step - 1)
                            for t in range(TT):
                                last = nc.tensor.matmul(ps[:, step % 2, t * u["n"]:(t + 1) * u["n"]],
                                                        u["q"][:, t * P:(t + 1) * P], u["k"], start=True, stop=True)
                            last.then_inc(scored, 1)
                        if 1 <= step <= U:
                            i = step - 1
                            u = units[i]
                            pe.wait_ge(probs_ready, i + 1)
                            if i >= 2:
                                pe.wait_ge(turned_back, i - 1)
                            for kt in range(len(u["v"])):
                                n = min(P, u["n"] - kt * P)
                                for t in range(TT):
                                    dst = ps[0:n, 2 + i % 2, kt * S + t * P:kt * S + (t + 1) * P]
                                    src = sc[:, i % 2, t, kt * P:kt * P + n]
                                    if n == P:
                                        last = nc.tensor.transpose(dst, src, mat("ident"))
                                    else:
                                        last = nc.tensor.matmul(dst, src, mat("ident"), start=True, stop=True)
                            last.then_inc(turned, 1)
                        if step >= 2:
                            i = step - 2
                            u = units[i]
                            pe.wait_ge(turned_back, i + 1)
                            fresh = i == 0 or (units[i - 1]["j"], units[i - 1]["po"]) != (u["j"], u["po"])
                            ends = i == U - 1 or (units[i + 1]["j"], units[i + 1]["po"]) != (u["j"], u["po"])
                            tiles = sum(x < i for x in done)
                            if tiles >= 2:
                                pe.wait_ge(out_copied, tiles - 1)
                            for kt, vv in enumerate(u["v"]):
                                n = min(P, u["n"] - kt * P)
                                last = nc.tensor.matmul(ps[u["po"]:u["po"] + HD, 4 + tiles % 2, 0:S], vv,
                                                        pT[0:n, i % 2, kt, :], start=(fresh and kt == 0),
                                                        stop=(ends and kt == len(u["v"]) - 1), skip_group_check=True)
                            if i in done:
                                last.then_inc(out_ready, 1)
                            else:
                                last.then_inc(a, 1)

                @block.vector
                def _(dve):
                    n = counter()
                    for i in range(U + 1):
                        if i < U:
                            u = units[i]
                            dve.wait_ge(scored, i + 1)
                            if i >= 2:
                                dve.wait_ge(turned, i - 1)
                            w = u["n"]
                            nc.vector.scalar_tensor_tensor(sc[:, i % 2, :, 0:w],
                                                           ps[:, i % 2, 0:TT * w].rearrange("p (t n) -> p t n", t=TT),
                                                           HD ** -0.5, u["bias"], ALU.mult, ALU.add).then_inc(shifted, 1)
                            dve.wait_ge(shifted, i + 1)
                            nc.vector.tensor_reduce(stat[:, i, 0:2], sc[:, i % 2, :, 0:w], AXX, ALU.max,
                                                    negate=True).then_inc(maxed, 1)
                        if i >= 1:
                            g = i - 1
                            dve.wait_ge(exped, TT * (g + 1))
                            nc.vector.reciprocal(stat[:, g, 4:6], stat[:, g, 2:4]).then_inc(v, 1)
                            dve.wait_ge(v, n())
                            if units[g].get("gate") is not None:
                                nc.vector.tensor_tensor(stat[:, g, 4:6], stat[:, g, 4:6], units[g]["gate"],
                                                        ALU.mult).then_inc(v, 1)
                                dve.wait_ge(v, n())
                            w = units[g]["n"]
                            nc.vector.tensor_tensor(sc[:, g % 2, :, 0:w], sc[:, g % 2, :, 0:w],
                                                    stat[:, g, 4:6].unsqueeze(2).broadcast_to([P, TT, w]),
                                                    ALU.mult).then_inc(probs_ready, 1)

                @block.scalar
                def _(act):
                    outs = 0
                    for i in range(U + 2):
                        if i < U:
                            act.wait_ge(maxed, i + 1)
                            for t in range(TT):
                                x = sc[:, i % 2, t, 0:units[i]["n"]]
                                nc.scalar.activation(x, x, ACT.Exp, bias=stat[:, i, t:t + 1],
                                                     accum_out=stat[:, i, 2 + t:3 + t]).then_inc(exped, 1)
                        if 1 <= i <= U:
                            g = i - 1
                            act.wait_ge(turned, g + 1)
                            n = min(P, units[g]["n"])
                            w = len(units[g]["v"]) * S
                            if g >= 2:
                                ends = sum(x <= g - 2 for x in done)
                                act.wait_ge(out_ready, ends) if ends else None
                                act.wait_ge(a, g - 1 - ends) if g - 1 - ends else None
                            nc.scalar.activation(pT[0:n, g % 2, 0:len(units[g]["v"]), :].rearrange("p a b -> p (a b)"),
                                                 ps[0:n, 2 + g % 2, 0:w], ACT.Copy).then_inc(turned_back, 1)
                        if i >= 2 and i - 2 in done:
                            act.wait_ge(out_ready, outs + 1)
                            nc.scalar.activation(out[:, units[i - 2]["j"], :], ps[:, 4 + outs % 2, 0:S],
                                                 ACT.Copy).then_inc(out_copied, 1)
                            outs += 1

        mixer = ExitStack()
        zT = sb("zT", [P, T_IN, S], where=mixer)
        vtok = sb("vtok", [P, TT, 512], where=mixer)

        rms_norm(lambda k: gs[:, 0, k:k + 1], lambda k: mod[:, k:k + 1])

        def copy_in(i, src):
            return nc.vector.tensor_scalar(one(zT, i), src, 1.0, None, ALU.mult)

        project(T_IN, hT, copy_in, T_IN_TOK,
                lambda i, src: nc.vector.tensor_copy(vtok[:, :, i * S:(i + 1) * S], src))

        attn = ExitStack()
        bias = sb("bias", [P, NH, TT, S], where=attn)
        with ExitStack() as tmp, stage() as (block, (squared, summed, scaled, root, v, c0_ready, weighted, *_)):
            root_qk = sb("root_qk", [P, NH * S], where=tmp)
            c0 = sb("c0", [P, 14], where=tmp)
            shiftd = sb("shiftd", [P, 14, S], where=tmp)
            qk = zT[:, 0:8, :].rearrange("p a t -> p (a t)")
            zr = zT[:, 8:22, :]

            @block.sync
            def _(sp):
                for h in range(NH):
                    sp.dma_start(bias[:, h, :, :], A["attn_bias"][h].rearrange("(t p) k -> p t k", p=P)
                                 ).then_inc(table_in, 16)
                    tables()
                sp.wait_ge(table_in, 16 * NH)

            @block.scalar
            def _(act):
                nc.scalar.activation(sq[:, :, :].rearrange("p a t -> p (a t)"), qk, ACT.Square).then_inc(squared, 1)
                act.wait_ge(c0_ready, 2)
                for i in range(14):
                    nc.scalar.activation(shiftd[:, i, :], zr[:, i, :], ACT.Copy, scale=c0[:, i:i + 1]
                                         ).then_inc(weighted, 1)
                act.wait_ge(scaled, 4)
                nc.scalar.activation(root_qk[:, :], root_qk[:, :], ACT.Sqrt).then_inc(root, 1)

            @block.tensor
            def _(pe):
                pe.wait_ge(squared, 1)
                for b in range(4):
                    nc.tensor.matmul(ps[:, b, :], mat("blockones"),
                                     sq[:, 2 * b:2 * b + 2, :].rearrange("p a t -> p (a t)"),
                                     start=True, stop=True).then_inc(summed, 1)

            @block.vector
            def _(dve):
                n = counter()
                nc.vector.tensor_tensor(c0[:, :], vec_all("mu_prev"), vec_all("mu_next"), ALU.add).then_inc(c0_ready, 1)
                dve.wait_ge(c0_ready, 1)
                nc.vector.tensor_scalar(c0[:, :], c0[:, :], -1.0, 1.0, ALU.mult, ALU.add).then_inc(c0_ready, 1)
                for i in range(14):
                    dve.wait_ge(weighted, i + 1)
                    nc.vector.scalar_tensor_tensor(shiftd[:, i, 1:S], zr[:, i, 0:S - 1], vec("mu_prev", i),
                                                   shiftd[:, i, 1:S], ALU.mult, ALU.add).then_inc(v, 1)
                    dve.wait_ge(v, n())
                    nc.vector.scalar_tensor_tensor(shiftd[:, i, 0:S - 1], zr[:, i, 1:S], vec("mu_next", i),
                                                   shiftd[:, i, 0:S - 1], ALU.mult, ALU.add).then_inc(v, 1)
                    dve.wait_ge(v, n())
                for b in range(4):
                    dve.wait_ge(summed, b + 1)
                    nc.vector.tensor_scalar(root_qk[:, 512 * b:512 * b + 512], ps[:, b, :], 1.0 / HD, NORM_EPS,
                                            ALU.mult, ALU.add).then_inc(scaled, 1)
                dve.wait_ge(root, 1)
                nc.vector.reciprocal(root_qk[:, :], root_qk[:, :]).then_inc(v, 1)
                dve.wait_ge(v, n())
                for b, name in enumerate(("q_norm_g", "k_norm_g")):
                    cols = slice(1024 * b, 1024 * b + 1024)
                    nc.vector.scalar_tensor_tensor(qk[:, cols], qk[:, cols], vec(name), root_qk[:, cols], ALU.mult,
                                                   ALU.mult)
                nc.vector.tensor_copy(zr, shiftd[:, :, :])

        attention([dict(po=HD * (h % 2), j=h // 2, n=S, q=zT[HD * (h % 2):HD * (h % 2) + HD, h // 2, :],
                        k=zT[HD * (h % 2):HD * (h % 2) + HD, 4 + h // 2, :], bias=bias[:, h, :, :],
                        v=[vtok[:, t, h * HD:(h + 1) * HD] for t in range(TT)]) for h in range(NH)], mix, "dilated")
        attn.close()

        wkv = ExitStack()
        rT, kT, vT = zT[:, 8:12, :], zT[:, 12:16, :], zT[:, 16:20, :]
        flat = "p a t -> p (a t)"
        alpha, beta, kappa, rho = (sb(n, [P, 2, 4, S], where=wkv) for n in ("alpha", "beta", "kappa", "rho"))
        gT = sb("gT", [P, 4, S], where=wkv)
        bonus = sb("bonus", [P, 4, S], where=wkv)
        ysum = sb("ysum", [P, 2, 512], where=wkv)
        carry = sb("carry", [P, 2, 4], where=wkv)
        feat = ExitStack()
        lora = sb("lora", [P, 2, 512], where=feat)
        g_up = sb("g_up", [P, 512], where=feat)
        logw = sb("logw", [P, 2, 4, S], where=feat)
        aa = sb("aa", [P, 2, 4, S], where=feat)
        kk = sb("kk", [P, 4, S], where=feat)
        omka = sb("omka", [P, 4], where=feat)
        with stage() as (block, (ups_in, squashed, raised, sig_done, v, kk_scaled, summed, *_)):
            @block.sync
            def _(sp):
                sp.dma_start(lora[:, :, :], A["lora_up"]).then_inc(ups_in, 16)
                sp.dma_start(g_up[:, :], A["g_up"]).then_inc(ups_in, 16)

            @block.scalar
            def _(act):
                nc.scalar.activation(zT[0:64, 20, :], zT[0:64, 20, :], ACT.Tanh).then_inc(squashed, 1)
                nc.scalar.activation(zT[:, 21, :], zT[:, 21, :], ACT.Sigmoid).then_inc(squashed, 1)
                for d in range(2):
                    act.wait_ge(raised, 8 * d + 8)
                    for j in range(4):
                        bank, col = 4 * d + j // 2, j % 2 * S
                        nc.scalar.activation(logw[:, d, j, :], ps[:, bank, col:col + S], ACT.Sigmoid,
                                             bias=vec("w_decay0", 4 * d + j)).then_inc(sig_done, 1)
                        nc.scalar.activation(aa[:, d, j, :], ps[:, bank + 2, col:col + S], ACT.Sigmoid,
                                             bias=vec("a_gate0", 4 * d + j)).then_inc(sig_done, 1)

            @block.tensor
            def _(pe):
                pe.wait_ge(ups_in, 32)
                pe.wait_ge(squashed, 2)
                for d in range(2):
                    for j in range(4):
                        bank, col = 4 * d + j // 2, j % 2 * S
                        nc.tensor.matmul(ps[:, bank, col:col + S], lora[0:64, d, j * P:(j + 1) * P], zT[0:64, 20, :],
                                         start=True, stop=True).then_inc(raised, 1)
                        nc.tensor.matmul(ps[:, bank + 2, col:col + S], lora[64:128, d, j * P:(j + 1) * P],
                                         zT[64:128, 20, :], start=True, stop=True).then_inc(raised, 1)

            @block.vector
            def _(dve):
                for j in range(4):
                    nc.vector.tensor_scalar(kk[:, j, :], kT[:, j, :], vec("k_k", j), None, ALU.mult).then_inc(v, 1)
                nc.vector.tensor_scalar(omka[:, :], vec_all("k_a"), -1.0, 1.0, ALU.mult, ALU.add)
                dve.wait_ge(v, 4)
                nc.vector.tensor_tensor(sq[:, 0:4, :], kk[:, :, :], kk[:, :, :], ALU.mult)
                dve.wait_ge(sig_done, 16)
                nc.vector.tensor_scalar(logw[:, :, :, :].rearrange("p d a t -> p (d a t)"),
                                        logw[:, :, :, :].rearrange("p d a t -> p (d a t)"),
                                        -float(np.exp(-0.5)), None, ALU.mult)

        with ExitStack() as tmp, stage() as (block, (summed, gated, kk_ready, exp_in, exps, v, w, kb_ready, bonus_sum,
                                                     g_done, kk_root, carry_in, *_)):
            cum = zT[:, 0:8, :].rearrange("p (d a) t -> p d a t", d=2)
            inv2 = hT[:, :, :].rearrange("p (d a) t -> p d a t", d=2)
            inv = sq[:, 0:4, :]
            kd = vtok[:, :, :].rearrange("p a (b t) -> p (a b) t", t=S)
            off = logw[:, :, :, :]
            mid = sb("mid", [P, 2, 8], where=tmp)

            @block.tensor
            def _(pe):
                for b in range(2):
                    nc.tensor.matmul(ps[:, b, :], mat("blockones"), sq[:, 2 * b:2 * b + 2, :].rearrange(flat),
                                     start=True, stop=True).then_inc(summed, 1)
                for j in range(4):
                    nc.tensor.matmul(ps[:, 2 + j // 2, j % 2 * S:j % 2 * S + S], g_up[:, j * P:(j + 1) * P],
                                     zT[:, 21, :], start=True, stop=True).then_inc(gated, 1)
                pe.wait_ge(kb_ready, 1)
                for b in range(2):
                    nc.tensor.matmul(ps[:, 4 + b, :], mat("blockones"), sq[:, 4 + 2 * b:6 + 2 * b, :].rearrange(flat),
                                     start=True, stop=True).then_inc(bonus_sum, 1)

            @block.scalar
            def _(act):
                act.wait_ge(kk_ready, 2)
                nc.scalar.activation(inv[:, :, :], inv[:, :, :], ACT.Sqrt).then_inc(kk_root, 1)
                act.wait_ge(gated, 4)
                nc.scalar.activation(gT[:, :, :].rearrange(flat), ps[:, 2:4, :].rearrange("p b n -> p (b n)"),
                                     ACT.Copy).then_inc(g_done, 1)
                for d in range(2):
                    act.wait_ge(exp_in, d + 1)
                    upto, sign = (cum, 1.0) if d == 0 else (off, -1.0)
                    before = off if d == 0 else cum
                    nc.scalar.activation(rho[:, d], upto[:, d], ACT.Exp).then_inc(exps, 1)
                    nc.scalar.activation(inv2[:, d], upto[:, d], ACT.Exp, scale=-1.0).then_inc(exps, 1)
                    nc.scalar.activation(alpha[:, d], before[:, d], ACT.Exp, scale=sign).then_inc(exps, 1)
                act.wait_ge(carry_in, 2)
                nc.scalar.activation(carry[:, :, :], carry[:, :, :], ACT.Exp)

            @block.vector
            def _(dve):
                n = counter()
                for b in range(2):
                    dve.wait_ge(summed, b + 1)
                    nc.vector.tensor_scalar(inv[:, 2 * b:2 * b + 2, :].rearrange(flat), ps[:, b, :], 1e-12, None,
                                            ALU.max).then_inc(kk_ready, 1)
                for d in range(2):
                    for j in range(4):
                        for c in range(2):
                            cols = slice(c * P, c * P + P)
                            nc.vector.tensor_tensor_scan(cum[:, d, j, cols], mat("ones"), logw[:, d, j, cols], 0.0,
                                                         ALU.mult, ALU.add).then_inc(v, n.one())
                    dve.wait_ge(v, n.now)
                    chunks = cum[:, d].rearrange("p a (c t) -> p (a c) t", t=P)
                    nc.vector.tensor_copy(mid[:, d, :], chunks[:, :, P // 2 - 1:P // 2].rearrange("p a b -> p (a b)")
                                          ).then_inc(v, n.one())
                    dve.wait_ge(v, n.now)
                    nc.vector.tensor_tensor(chunks, chunks, mid[:, d, :].unsqueeze(2).broadcast_to([P, 8, P]),
                                            ALU.subtract).then_inc(v, n.one())
                    dve.wait_ge(v, n.now)
                    pair = (cum[:, d], logw[:, d]) if d == 0 else (logw[:, d], cum[:, d])
                    nc.vector.tensor_tensor(off[:, d], pair[0], pair[1], ALU.subtract).then_inc(exp_in, 1)
                    dve.wait_ge(exp_in, d + 1)
                    nc.vector.tensor_tensor(carry[:, d, :], cum[:, d, :, P - 1:P].rearrange("p a b -> p (a b)"),
                                            off[:, d, :, P:P + 1].rearrange("p a b -> p (a b)"),
                                            ALU.subtract if d == 0 else ALU.add).then_inc(carry_in, 1)
                dve.wait_ge(kk_root, 1)
                nc.vector.reciprocal(inv[:, :, :], inv[:, :, :]).then_inc(v, n.one())
                dve.wait_ge(v, n.now)
                nc.vector.tensor_tensor(kk[:, :, :], kk[:, :, :], inv[:, :, :], ALU.mult).then_inc(v, n.one())
                dve.wait_ge(v, n.now)
                nc.vector.tensor_tensor(inv[:, :, :], aa[:, 0], aa[:, 1], ALU.add).then_inc(v, n.one())
                dve.wait_ge(v, n.now)
                nc.vector.tensor_scalar(inv[:, :, :].rearrange(flat), inv[:, :, :].rearrange(flat), 0.5, None,
                                        ALU.mult).then_inc(v, n.one())
                dve.wait_ge(v, n.now)
                for j in range(4):
                    nc.vector.tensor_scalar(inv[:, j, :], inv[:, j, :], vec("k_a", j), omka[:, j:j + 1], ALU.mult,
                                            ALU.add).then_inc(v, n.one())
                dve.wait_ge(v, n.now)
                nc.vector.tensor_tensor(inv[:, :, :], inv[:, :, :], kT, ALU.mult).then_inc(v, n.one())
                dve.wait_ge(v, n.now)
                for j in range(4):
                    nc.vector.scalar_tensor_tensor(sq[:, 4 + j, :], inv[:, j, :], vec("r_k", j), rT[:, j, :],
                                                   ALU.mult, ALU.mult).then_inc(kb_ready if j == 3 else w, 1)
                dve.wait_ge(kb_ready, 1)
                dve.wait_ge(w, 3)
                for d in range(2):
                    dve.wait_ge(v, n.now)
                    for j in range(4):
                        nc.vector.tensor_scalar(kd[:, j, :], aa[:, d, j, :], vec("k_a", j), omka[:, j:j + 1],
                                                ALU.mult, ALU.add).then_inc(v, n.one())
                    nc.vector.tensor_tensor(beta[:, d], kk[:, :, :], aa[:, d], ALU.mult).then_inc(v, n.one())
                    dve.wait_ge(v, n.now)
                    nc.vector.tensor_tensor(kd[:, :, :], kd[:, :, :], kT, ALU.mult).then_inc(v, n.one())
                    dve.wait_ge(exps, 3 * d + 3)
                    dve.wait_ge(v, n.now)
                    nc.vector.tensor_tensor(kappa[:, d], kd[:, :, :], inv2[:, d], ALU.mult).then_inc(v, n.one())
                    nc.vector.tensor_tensor(beta[:, d], beta[:, d], inv2[:, d], ALU.mult).then_inc(v, n.one())
                    nc.vector.tensor_tensor(alpha[:, d], alpha[:, d], kk[:, :, :], ALU.mult).then_inc(v, n.one())
                    nc.vector.tensor_tensor(rho[:, d], rho[:, d], rT, ALU.mult).then_inc(v, n.one())
                dve.wait_ge(bonus_sum, 2)
                for b in range(2):
                    nc.vector.tensor_tensor(bonus[:, 2 * b:2 * b + 2, :].rearrange(flat), ps[:, 4 + b, :],
                                            vT[:, 2 * b:2 * b + 2, :].rearrange(flat), ALU.mult)
        feat.close()

        solve = ExitStack()
        v_tok = vtok
        bk_tok = sb("bk_tok", [P, 2, 2, 512], where=solve)
        with stage() as (block, (turned, *_)):
            jobs = [(v_tok[:, c, :], vT, c) for c in range(2)]
            jobs += [(bk_tok[:, d, i, :], (beta, kappa)[i][:, d], d) for d in range(2) for i in range(2)]

            @block.tensor
            def _(pe):
                for n, (_, src, c) in enumerate(jobs):
                    for j in range(4):
                        last = nc.tensor.transpose(ps[:, n, j * P:(j + 1) * P], src[:, j, c * P:(c + 1) * P],
                                                   mat("ident"))
                    last.then_inc(turned, 1)

            @block.vector
            def _(dve):
                for n, (dst, _, _) in enumerate(jobs):
                    if n % 2 == 0:
                        dve.wait_ge(turned, n + 1)
                        nc.vector.tensor_copy(dst, ps[:, n, :])

            @block.scalar
            def _(act):
                for n, (dst, _, _) in enumerate(jobs):
                    if n % 2:
                        act.wait_ge(turned, n + 1)
                        nc.scalar.activation(dst, ps[:, n, :], ACT.Copy)

        states = [sb(f"state{d}", [P, 4, HD], where=solve) for d in range(2)]
        def matrices(tensor, n):
            return tensor[:, 4 * n:4 * n + 4, :].rearrange("p a (b t) -> p (a b) t", t=P)
        LT, X, XT, Y = matrices(hT, 0), matrices(hT, 1), matrices(zT, 0), matrices(zT, 1)
        LmT, MT, N1, N2 = matrices(zT, 2), matrices(zT, 3), matrices(sq, 0), matrices(sq, 1)
        G, SA = mix[:, 4:6, :].rearrange("p a t -> p (a t)"), mix[:, 6:8, :].rearrange("p a t -> p (a t)")
        heads = "p h t -> p (h t)"

        def all_heads(m):
            return mat(m).unsqueeze(1).broadcast_to([P, NH, P])

        def banks(b):
            return ps[:, b:b + 2, :].rearrange("p b (h t) -> p (b h) t", t=P)

        def place_of(h):
            return h % 2 * 4 + h // 2

        def rows(h):
            return slice(HD * (h % 2), HD * (h % 2) + HD)

        for first_chunk in (True, False):
            for d in range(2):
                c = d if first_chunk else 1 - d
                cols = slice(c * P, c * P + P)
                with stage() as (block, (products, masked, y_used, x_ready, xt_ready, level_in, g_ready, v, sa_ready,
                                         y_ready, state_ready, sq_ready, *_)):
                    @block.tensor
                    def _(pe):
                        def outer(bank, left, right, counted):
                            for h in range(NH):
                                last = nc.tensor.matmul(ps[:, bank + h % 2, h // 2 * P:h // 2 * P + P],
                                                        left[rows(h), d, h // 2, cols],
                                                        right[rows(h), d, h // 2, cols], start=True, stop=True)
                            last.then_inc(counted, 1)
                        outer(0, beta, alpha, products)
                        outer(2, alpha, beta, products)
                        outer(4, kappa, alpha, products)
                        outer(6, beta, rho, products)
                        pe.wait_ge(masked, 3)
                        outer(4, kappa, rho, products)
                        for lv in range(6):
                            def doubling(bank, left, right, counted):
                                for h in range(NH):
                                    last = nc.tensor.matmul(ps[:, bank + h // 4, h % 4 * P:h % 4 * P + P],
                                                            left[:, h, :], right[:, h, :], start=True, stop=True)
                                last.then_inc(counted, 1)
                            pe.wait_ge(level_in, lv + 1)
                            pe.wait_ge(x_ready, lv + 1)
                            doubling(0, LmT, X, products)
                            pe.wait_ge(sq_ready, lv + 1)
                            pe.wait_ge(xt_ready, lv + 1)
                            if lv == 0:
                                pe.wait_ge(masked, 5)
                            if lv < 5:
                                doubling(2, XT, Y, products)
                            doubling(4, Y, XT, products)
                        pe.wait_ge(masked, 5)
                        for h in range(NH):
                            dst = ps[:, 6 + h % 2, h // 2 * HD:(h // 2 + 1) * HD]
                            if not first_chunk:
                                nc.tensor.matmul(dst, alpha[rows(h), d, h // 2, cols], states[d][rows(h), h // 2, :],
                                                 start=True, stop=False)
                            last = nc.tensor.matmul(dst, MT[:, place_of(h), :], v_tok[:, c, h * HD:(h + 1) * HD],
                                                    start=first_chunk, stop=True)
                        last.then_inc(g_ready, 1)
                        pe.wait_ge(xt_ready, 7)
                        pe.wait_ge(g_ready, 2)
                        for h in range(NH):
                            at = place_of(h)
                            last = nc.tensor.matmul(ps[:, 2, h * HD:(h + 1) * HD], XT[:, at, :],
                                                    G[:, at * HD:(at + 1) * HD], start=True, stop=True)
                        last.then_inc(sa_ready, 1)
                        pe.wait_ge(sa_ready, 2)
                        for h in range(NH):
                            hv = slice(h * HD, (h + 1) * HD)
                            dst = ps[:, 3 * (h % 2), h // 2 * HD:(h // 2 + 1) * HD]
                            if not first_chunk:
                                nc.tensor.matmul(dst, rho[rows(h), d, h // 2, cols], states[d][rows(h), h // 2, :],
                                                 start=True, stop=False)
                            nc.tensor.matmul(dst, N1[:, place_of(h), :], SA[:, hv], start=first_chunk, stop=False)
                            last = nc.tensor.matmul(dst, N2[:, place_of(h), :], v_tok[:, c, hv], start=False, stop=True)
                        last.then_inc(y_ready, 1)
                        if first_chunk:
                            for h in range(NH):
                                hv = slice(h * HD, (h + 1) * HD)
                                dst = ps[rows(h), 1, h // 2 * HD:(h // 2 + 1) * HD]
                                nc.tensor.matmul(dst, bk_tok[:, d, 0, hv], SA[:, hv], start=True, stop=False)
                                last = nc.tensor.matmul(dst, bk_tok[:, d, 1, hv], v_tok[:, c, hv], start=False,
                                                        stop=True)
                            last.then_inc(state_ready, 1)

                    @block.scalar
                    def _(act):
                        for lv in range(6):
                            act.wait_ge(products, 5 + 3 * lv + 1)
                            if lv:
                                act.wait_ge(products, 5 + 3 * lv)
                            nc.scalar.activation(Y[:, :, :], banks(0), ACT.Copy).then_inc(sq_ready, 1)
                        act.wait_ge(g_ready, 1)
                        nc.scalar.activation(G[:, :].rearrange("p (a n) -> p a n", a=2), ps[:, 6:8, 0:S],
                                             ACT.Copy).then_inc(g_ready, 1)

                    @block.gpsimd
                    def _(pool):
                        pool.wait_ge(masked, 1)
                        for lv, b in enumerate((2, 4, 8, 16, 32, 64)):
                            if lv:
                                pool.wait_ge(products, 5 + 3 * (lv - 1) + 1)
                            nc.gpsimd.tensor_tensor(LmT[:, :, :], LT[:, :, :], all_heads(f"level{d}_{b}"),
                                                    ALU.mult).then_inc(level_in, 1)

                    @block.vector
                    def _(dve):
                        n = counter()
                        dve.wait_ge(products, 1)
                        nc.vector.tensor_tensor(LT[:, :, :], banks(0), all_heads(f"strict{d}"),
                                                ALU.mult).then_inc(masked, 1)
                        dve.wait_ge(products, 2)
                        nc.vector.tensor_tensor(X[:, :, :], banks(2), all_heads(f"level_row{d}"),
                                                ALU.mult).then_inc(masked, 1)
                        dve.wait_ge(products, 3)
                        nc.vector.tensor_tensor(MT[:, :, :], banks(4), all_heads(f"strict{d}"),
                                                ALU.mult).then_inc(masked, 1)
                        dve.wait_ge(masked, 2)
                        nc.vector.tensor_tensor(XT[:, :, :], LT[:, :, :], all_heads(f"level{d}_1"),
                                                ALU.mult).then_inc(v, n.one())
                        nc.vector.tensor_tensor(X[:, :, :], all_heads("ident"), X[:, :, :],
                                                ALU.subtract).then_inc(x_ready, 1)
                        dve.wait_ge(v, n.now)
                        nc.vector.tensor_tensor(XT[:, :, :], all_heads("ident"), XT[:, :, :],
                                                ALU.subtract).then_inc(xt_ready, 1)
                        dve.wait_ge(products, 4)
                        nc.vector.tensor_tensor(N1[:, :, :], banks(6), all_heads(f"upto{d}"),
                                                ALU.mult).then_inc(masked, 1)
                        dve.wait_ge(products, 5)
                        nc.vector.tensor_tensor(N2[:, :, :], banks(4), all_heads(f"upto{d}"),
                                                ALU.mult).then_inc(masked, 1)
                        for lv in range(6):
                            if lv < 5:
                                dve.wait_ge(products, 5 + 3 * lv + 2)
                                dve.wait_ge(x_ready, lv + 1)
                                nc.vector.tensor_tensor(X[:, :, :], X[:, :, :], banks(2),
                                                        ALU.subtract).then_inc(x_ready, 1)
                            dve.wait_ge(products, 5 + 3 * lv + (3 if lv < 5 else 2))
                            dve.wait_ge(xt_ready, lv + 1)
                            nc.vector.tensor_tensor(XT[:, :, :], XT[:, :, :], banks(4),
                                                    ALU.subtract).then_inc(xt_ready, 1)
                        dve.wait_ge(sa_ready, 1)
                        nc.vector.tensor_scalar(SA[:, :], ps[:, 2, :], -1.0, None, ALU.mult).then_inc(sa_ready, 1)
                        dve.wait_ge(y_ready, 1)
                        for odd in range(2):
                            mine = ysum[:, c, :].rearrange("p (j q e) -> p j q e", q=2, e=HD)[:, :, odd, :]
                            new = ps[:, 3 * odd, 0:S].rearrange("p (j e) -> p j e", e=HD)
                            if first_chunk:
                                nc.vector.tensor_copy(mine, new)
                            else:
                                nc.vector.tensor_tensor(mine, mine, new, ALU.add)
                        if first_chunk:
                            dve.wait_ge(state_ready, 1)
                            for j in range(4):
                                nc.vector.tensor_scalar(states[d][:, j, :], ps[:, 1, j * HD:(j + 1) * HD],
                                                        carry[:, d, j:j + 1], None, ALU.mult)
        solve.close()

        with ExitStack() as tmp, stage() as (block, (v, centred, squared, root, normed, turned, root_in, *_)):
            st = sb("st", [P, 2, 16], where=tmp)
            y = ysum[:, :, :].rearrange("p c (h e) -> p (c h) e", e=HD)
            ysq = sq[:, 0:4, :].rearrange("p a t -> p (a t)").rearrange("p (h e) -> p h e", e=HD)

            @block.scalar
            def _(act):
                act.wait_ge(centred, 1)
                nc.scalar.activation(ysq, y, ACT.Square).then_inc(squared, 1)
                act.wait_ge(root_in, 1)
                nc.scalar.activation(st[:, 1, :], st[:, 1, :], ACT.Sqrt).then_inc(root, 1)

            @block.vector
            def _(dve):
                n = counter()
                nc.vector.tensor_reduce(st[:, 0, :], y, AXX, ALU.add).then_inc(v, n.one())
                dve.wait_ge(v, n.now)
                nc.vector.tensor_scalar(st[:, 0, :], st[:, 0, :], 1.0 / HD, None, ALU.mult).then_inc(v, n.one())
                dve.wait_ge(v, n.now)
                nc.vector.tensor_tensor(y, y, st[:, 0, :].unsqueeze(2).broadcast_to([P, 16, HD]),
                                        ALU.subtract).then_inc(centred, 1)
                dve.wait_ge(squared, 1)
                nc.vector.tensor_reduce(st[:, 1, :], ysq, AXX, ALU.add).then_inc(v, n.one())
                dve.wait_ge(v, n.now)
                nc.vector.tensor_scalar(st[:, 1, :], st[:, 1, :], 1.0 / HD, 64e-5, ALU.mult,
                                        ALU.add).then_inc(root_in, 1)
                dve.wait_ge(root, 1)
                nc.vector.reciprocal(st[:, 1, :], st[:, 1, :]).then_inc(v, n.one())
                dve.wait_ge(v, n.now)
                nc.vector.tensor_tensor(y, y, st[:, 1, :].unsqueeze(2).broadcast_to([P, 16, HD]),
                                        ALU.mult).then_inc(normed, 1)
                for j in range(4):
                    dve.wait_ge(turned, j + 1)
                    nc.vector.tensor_scalar(mix[:, 4 + j, :], ps[:, j, 0:S], vec("lnx_g", j), vec("lnx_b", j),
                                            ALU.mult, ALU.add).then_inc(v, n.one())
                dve.wait_ge(v, n.now)
                nc.vector.tensor_tensor(mix[:, 4:8, :], mix[:, 4:8, :], bonus[:, :, :], ALU.add).then_inc(v, n.one())
                dve.wait_ge(v, n.now)
                nc.vector.tensor_tensor(mix[:, 4:8, :], mix[:, 4:8, :], gT[:, :, :], ALU.mult)

            @block.tensor
            def _(pe):
                pe.wait_ge(normed, 1)
                for j in range(4):
                    for c in range(2):
                        last = nc.tensor.transpose(ps[:, j, c * P:(c + 1) * P], ysum[:, c, j * P:(j + 1) * P],
                                                   mat("ident"))
                    last.then_inc(turned, 1)
        wkv.close()
        mixer.close()

        def add_gated(col):
            return lambda i, src: nc.vector.scalar_tensor_tensor(one(xT, i), src, mod[:, col:col + 8][:, bass.ds(i, 1)],
                                                                 one(xT, i), ALU.mult, ALU.add)

        project(T_OUT, mix, add_gated(16))
        rms_norm(lambda k: gs[:, 1, k:k + 1], lambda k: mod[:, 24 + k:25 + k])

        peer = ExitStack()
        h_tok = sb("h_tok", [P, TT, D], where=peer)
        experts = sb("experts", [P, TT, SLOTS], U32, where=peer)
        gates = sb("gates", [P, TT, SLOTS], where=peer)
        best = sb("best", [P, TT, NH, TOPK], where=peer)
        digits = sb("digits", [P, TOPK], where=peer)
        scores = [free[:, :, :].rearrange("p k t -> p (k t)").rearrange("p (s h n) -> p s h n", s=2, h=NH)
                  for free in (mix, sq)]
        with ExitStack() as tmp:
            queries = sb("queries", [P, T_QUERY, S], where=tmp)
            subkeys = sb("subkeys", [P, 2, NE], where=tmp)
            project(T_QUERY, hT, lambda i, src: nc.vector.tensor_scalar(one(queries, i), src, 1.0, None, ALU.mult))
            with stage() as (block, (keys_in, scored, turned, bank_free, *_)):
                @block.sync
                def _(sp):
                    sp.dma_start(subkeys[:, :, :], A["subkeys"]).then_inc(keys_in, 16)

                @block.tensor
                def _(pe):
                    pe.wait_ge(keys_in, 16)
                    for t in range(TT):
                        for half in range(2):
                            if t:
                                pe.wait_ge(bank_free, half + 1)
                            for h in range(NH):
                                last = nc.tensor.matmul(ps[:, 2 * half + h // 4, h % 4 * P:h % 4 * P + P],
                                                        queries[:, 2 * h + half, t * P:(t + 1) * P],
                                                        subkeys[:, half, :], start=True, stop=True)
                            last.then_inc(scored, 1)
                    for t in range(TT):
                        for k in range(KT):
                            last = nc.tensor.transpose(ps[:, 4 + 2 * t + k // 4, k % 4 * P:k % 4 * P + P],
                                                       hT[:, k, t * P:(t + 1) * P], mat("ident"))
                        last.then_inc(turned, 1)

                @block.vector
                def _(dve):
                    for n in range(2 * TT):
                        dve.wait_ge(scored, n + 1)
                        b = n % 2 * 2
                        nc.vector.tensor_copy(scores[n // 2][:, n % 2, :, :].rearrange(heads),
                                              ps[:, b:b + 2, :].rearrange("p b n -> p (b n)")).then_inc(bank_free, 1)

                @block.scalar
                def _(act):
                    for t in range(TT):
                        act.wait_ge(turned, t + 1)
                        nc.scalar.activation(h_tok[:, t, :], ps[:, 4 + 2 * t:6 + 2 * t, :].rearrange("p b n -> p (b n)"),
                                             ACT.Copy)

        def choice_buffers(tag, heads, where):
            b = {n: sb(f"{n}_{tag}", shape, dt, where=where) for n, shape, dt in (
                ("top", [P, 2, heads, TOPK], F32), ("at", [P, 2, heads, TOPK], U32), ("atf", [P, 2, heads, TOPK], F32),
                ("sums", [P, heads, TOPK, TOPK], F32), ("hot", [P, 2, heads, TOPK, TOPK], F32),
                ("place", [P, heads, TOPK], U32), ("half", [P, 2, heads, TOPK], U32),
                ("halff", [P, 2, heads, TOPK], F32), ("found", [P, 2, heads, TOPK], F32))}
            b["heads"] = heads
            return b

        def choice_steps(heads):
            return 5 * 2 * heads + 1 + 5 * heads + 12

        def top16(done, n, units, hold):
            def step(first, op):
                for u in range(len(units)):
                    hold(n.now - u if first else n.now - len(units) + 1)
                    op(*units[u]).then_inc(done, n.one())
            step(True, lambda values, out, places: nc.vector.max(out[:, 0:8], values))
            step(False, lambda values, out, places: nc.vector.max_index(places[:, 0:8], out[:, 0:8], values))
            step(False, lambda values, out, places: nc.vector.match_replace(values, out[:, 0:8], values, -3e38))
            step(False, lambda values, out, places: nc.vector.max(out[:, 8:16], values))
            step(False, lambda values, out, places: nc.vector.max_index(places[:, 8:16], out[:, 8:16], values))

        def choose(dve, done, n, before, b, scores_of, best_of, expert_slots, hold, meanwhile):
            H = b["heads"]
            four = [P, H, TOPK, TOPK]
            top16(done, n, [(scores_of(half, h), b["top"][:, half, h, :], b["at"][:, half, h, :])
                            for half in range(2) for h in range(H)], hold)
            dve.wait_ge(done, before + n.now)
            nc.vector.tensor_tensor(b["sums"][:, :, :, :], b["top"][:, 0].unsqueeze(3).broadcast_to(four),
                                    b["top"][:, 1].unsqueeze(2).broadcast_to(four), ALU.add).then_inc(done, n.one())
            top16(done, n, [(b["sums"][:, h].rearrange("p a b -> p (a b)"), best_of(h), b["place"][:, h, :])
                            for h in range(H)], hold)
            nc.vector.tensor_copy(b["atf"][:, :, :, :], b["at"][:, :, :, :]).then_inc(done, n.one())
            meanwhile()
            dve.wait_ge(done, before + (n.now - 1))
            nc.vector.tensor_scalar(b["half"][:, 0], b["place"][:, :, :], 4, None, ALU.logical_shift_right
                                    ).then_inc(done, n.one())
            nc.vector.tensor_scalar(b["half"][:, 1], b["place"][:, :, :], 15, None, ALU.bitwise_and
                                    ).then_inc(done, n.one())
            meanwhile()
            for half in range(2):
                dve.wait_ge(done, before + (n.now - 1))
                nc.vector.tensor_copy(b["halff"][:, half], b["half"][:, half]).then_inc(done, n.one())
            meanwhile()
            for half in range(2):
                dve.wait_ge(done, before + (n.now - 1))
                nc.vector.tensor_tensor(b["hot"][:, half], digits[:, :].unsqueeze(1).unsqueeze(1).broadcast_to(four),
                                        b["halff"][:, half].unsqueeze(3).broadcast_to(four), ALU.is_equal
                                        ).then_inc(done, n.one())
                meanwhile()
            for half in range(2):
                dve.wait_ge(done, before + (n.now - 1))
                nc.vector.tensor_tensor(b["hot"][:, half], b["hot"][:, half],
                                        b["atf"][:, half].unsqueeze(2).broadcast_to(four), ALU.mult
                                        ).then_inc(done, n.one())
                meanwhile()
            for half in range(2):
                dve.wait_ge(done, before + (n.now - 1))
                nc.vector.tensor_reduce(b["found"][:, half], b["hot"][:, half], AXX, ALU.add).then_inc(done, n.one())
                meanwhile()
            dve.wait_ge(done, before + n.now)
            nc.vector.scalar_tensor_tensor(expert_slots, b["found"][:, 0], float(NE), b["found"][:, 1], ALU.mult,
                                           ALU.add).then_inc(done, n.one())

        def gate_softmax(dve, t, den, exp_in, exped, v):
            g3 = gates[:, t, :].rearrange("p (h k) -> p h k", k=TOPK)
            n = counter()
            n.now = 3 * t
            nc.vector.tensor_tensor(g3, best[:, t], best[:, t, :, 0:1].broadcast_to([P, NH, TOPK]),
                                    ALU.subtract).then_inc(exp_in, 1)
            dve.wait_ge(exped, t + 1)
            nc.vector.tensor_reduce(den[:, :], g3, AXX, ALU.add).then_inc(v, n.one())
            dve.wait_ge(v, n.now)
            nc.vector.reciprocal(den[:, :], den[:, :]).then_inc(v, n.one())
            dve.wait_ge(v, n.now)
            nc.vector.tensor_tensor(g3, g3, den[:, :].unsqueeze(2).broadcast_to([P, NH, TOPK]), ALU.mult
                                    ).then_inc(v, n.one())

        def gate_exp(act, t, exp_in, exped):
            act.wait_ge(exp_in, t + 1)
            nc.scalar.activation(gates[:, t, :], gates[:, t, :], ACT.Exp).then_inc(exped, 1)

        with ExitStack() as tmp, stage() as (block, (chosen, counted, *_)):
            buffers = choice_buffers("first", NH, tmp)

            @block.gpsimd
            def _(pool):
                nc.gpsimd.iota(digits[:, :], [[1, TOPK]], base=0, channel_multiplier=0,
                               allow_small_or_imprecise_dtypes=True).then_inc(counted, 1)

            @block.vector
            def _(dve):
                n = counter()
                dve.wait_ge(counted, 1)
                dve.sem_inc(chosen, n.one())
                choose(dve, chosen, n, 0, buffers, lambda half, h: scores[0][:, half, h, :], lambda h: best[:, 0, h, :],
                       experts[:, 0, :].rearrange("p (h k) -> p h k", k=TOPK), lambda c: dve.wait_ge(chosen, c),
                       lambda: None)
                assert n.now == choice_steps(NH) + 1

        BATCH = TOPK // 2
        TURNS = NH
        y_tok = sb("y_tok", [P, TT, D], where=peer)
        weights = sb("weights", [P, TT, SLOTS], where=peer)
        row_in = [[sem(f"row_in{s}_{i}") for i in range(BATCH)] for s in range(2)]
        row_used = sem("row_used")
        with ExitStack() as tmp:
            index = sb("index", [P, 2, BATCH], U32, where=tmp)
            row = sb("row", [P, 2, BATCH, D], where=tmp)
            dots = sb("dots", [P, TOPK], where=tmp)
            idle = sb("idle", [P, 2], where=tmp)
            buffers = choice_buffers("head", 1, tmp)
            den = sb("den", [P, NH], where=tmp)
            head_scores = sb("head_scores", [P, 2, NE], where=tmp)
            head_best = sb("head_best", [P, TOPK], where=tmp)
            STEPS = choice_steps(1) + 2
            with stage() as (block, (index_ready, index_read, gelu_in, gelued, weighted, v, idle_set, chosen, exp_in,
                                     exped, gate_steps, *_)):
                @block.gpsimd
                def _(pool):
                    nc.gpsimd.memset(idle[:, :], 0.0).then_inc(idle_set, 1)
                    pool.wait_ge(idle_set, 1)
                    for p in range(2 * TT):
                        t, table = p // 2, ("peer_u", "peer_v")[p % 2]

                        def batch(g, s, again):
                            before = g * TOPK + (2 * p * TURNS + s - 1) * BATCH
                            if again:
                                pool.wait_ge(index_read, before)
                                pool.wait_ge(row_used, before)
                            if p == 2 and s == 0:
                                pool.wait_ge(chosen, g * STEPS + (STEPS + 1))
                            nc.gpsimd.tensor_copy(index[:, s, :], experts[:, t, bass.ds(g * TOPK + s * BATCH, BATCH)]
                                                  ).then_inc(index_ready, 1)
                            pool.wait_ge(index_ready, g * 2 + (2 * p * TURNS + s + 1))
                            nc.gpsimd.tensor_tensor(idle[:, 0:1], idle[:, 1:2], idle[:, 1:2], ALU.add)
                            for i in range(BATCH):
                                pool.indirect_dma_start(
                                    out=row[:, s, i, :], out_offset=None, in_=A[table],
                                    in_offset=bass.IndirectOffsetOnAxis(ap=index[:, s, i:i + 1], axis=0),
                                    engine_sem=index_read).then_inc(row_in[s][i], 16)
                        if p == 0:
                            batch(0, 0, False)
                            batch(0, 1, False)
                        with pool.Fori(1 if p == 0 else 0, TURNS) as g:
                            batch(g, 0, True)
                            batch(g, 1, True)

                @block.scalar
                def _(act):
                    for t in range(TT):
                        gate_exp(act, t, exp_in, exped)
                        act.wait_ge(gelu_in, t + 1)
                        nc.scalar.activation(weights[:, t, :], weights[:, t, :], ACT.Gelu).then_inc(gelued, 1)

                @block.vector
                def _(dve):
                    def dot(p, g, e):
                        dve.wait_ge(row_in[e // BATCH][e % BATCH], g * 16 + 16 * (p * TURNS + 1))
                        u_row = row[:, e // BATCH, e % BATCH, :]
                        nc.vector.tensor_tensor_reduce(u_row, u_row, h_tok[:, p // 2, :], 1.0, 0.0, ALU.mult, ALU.add,
                                                       dots[:, e:e + 1]).then_inc(row_used, 1)

                    def dots_out(p, g):
                        dve.wait_ge(row_used, g * TOPK + (p * TURNS + 1) * TOPK)
                        nc.vector.tensor_scalar(weights[:, p // 2, bass.ds(g * TOPK, TOPK)], dots[:, :], 1.0, None,
                                                ALU.mult).then_inc(v, 1)

                    def sum_up(p, g, e):
                        t = p // 2
                        dve.wait_ge(row_in[e // BATCH][e % BATCH], g * 16 + 16 * (p * TURNS + 1))
                        dve.wait_ge(row_used, g * TOPK + (p * TURNS * TOPK + e))
                        nc.vector.scalar_tensor_tensor(y_tok[:, t, :], row[:, e // BATCH, e % BATCH, :],
                                                       weights[:, t, bass.ds(g * TOPK + e, 1)], y_tok[:, t, :],
                                                       ALU.mult, ALU.add).then_inc(row_used, 1)

                    def choose_head(h, work):
                        steps, slot, before = counter(), counter(), h * STEPS
                        steps.one()

                        def meanwhile():
                            if slot.now < TOPK:
                                work(slot.now)
                                slot.one()

                        def hold(c):
                            assert slot.now < TOPK
                            dve.wait_ge(chosen, before + c)
                            meanwhile()
                        dve.wait_ge(chosen, before + 1)
                        nc.vector.tensor_copy(head_scores[:, :, :],
                                              scores[1][:, :, bass.ds(h, 1), :].rearrange("p s a n -> p s (a n)")
                                              ).then_inc(chosen, steps.one())
                        choose(dve, chosen, steps, before, buffers, lambda half, i: head_scores[:, half, :],
                               lambda i: head_best[:, :], experts[:, 1, bass.ds(h * TOPK, TOPK)].unsqueeze(1), hold,
                               meanwhile)
                        nc.vector.tensor_copy(best[:, 1, bass.ds(h, 1), :].rearrange("p a n -> p (a n)"),
                                              head_best[:, :]).then_inc(chosen, steps.one())
                        assert steps.now == STEPS + 1
                        for e in range(slot.now, TOPK):
                            work(e)

                    def weigh(t):
                        if t == 1:
                            dve.wait_ge(chosen, NH * STEPS + 1)
                        gate_softmax(dve, t, den, exp_in, exped, gate_steps)
                        dve.wait_ge(gate_steps, 3 * (t + 1))
                        dve.wait_ge(gelued, t + 1)
                        nc.vector.tensor_tensor(weights[:, t, :], weights[:, t, :], gates[:, t, :],
                                                ALU.mult).then_inc(weighted, 1)
                        dve.wait_ge(weighted, t + 1)

                    for t in range(TT):
                        nc.vector.memset(y_tok[:, t, :], 0.0).then_inc(v, 1)
                    dve.wait_ge(v, TT)
                    dve.sem_inc(chosen, 1)
                    with dve.Fori(0, TURNS // 2) as g:
                        for odd in range(2):
                            turn = g * 2 + odd
                            dve.wait_ge(v, turn + TT)
                            if odd == 0:
                                choose_head(g, lambda e: dot(0, turn, e))
                            else:
                                for e in range(TOPK):
                                    dot(0, turn, e)
                            dots_out(0, turn)
                    dve.wait_ge(v, TT + TURNS)
                    dve.sem_inc(gelu_in, 1)
                    weigh(0)
                    with dve.Fori(0, TURNS // 2) as g:
                        choose_head(g + NH // 2, lambda e: sum_up(1, g * 2, e))
                        for e in range(TOPK):
                            sum_up(1, g * 2 + 1, e)
                    with dve.Fori(0, TURNS) as g:
                        dve.wait_ge(v, g + (TT + TURNS))
                        for e in range(TOPK):
                            dot(2, g, e)
                        dots_out(2, g)
                    dve.wait_ge(v, TT + 2 * TURNS)
                    dve.sem_inc(gelu_in, 1)
                    weigh(1)
                    with dve.Fori(0, TURNS) as g:
                        for e in range(TOPK):
                            sum_up(3, g, e)

        with stage() as (block, (turned, *_)):
            @block.tensor
            def _(pe):
                for k in range(KT):
                    for t in range(TT):
                        last = nc.tensor.transpose(ps[:, k, t * P:(t + 1) * P], y_tok[:, t, k * P:(k + 1) * P],
                                                   mat("ident"))
                    last.then_inc(turned, 1)

            @block.vector
            def _(dve):
                for k in range(KT):
                    dve.wait_ge(turned, k + 1)
                    nc.vector.scalar_tensor_tensor(xT[:, k, :], ps[:, k, 0:S], mod[:, 40 + k:41 + k], xT[:, k, :],
                                                   ALU.mult, ALU.add)
        peer.close()

        def norm_w(layer, which):
            return lambda k: vec("norm_w", (layer * 3 + which) * KT + k)

        swiglu(norm_w(0, 0))
        rms_norm(norm_w(0, 1), None)

        even = ExitStack()
        ez = sb("ez", [P, T_EV, S], where=even)
        et = sb("et", [P, TT, T_EV_TOK * P], where=even)
        project(T_EV, hT, lambda i, src: nc.vector.tensor_scalar(one(ez, i), src, 1.0, None, ALU.mult),
                T_EV_TOK, lambda i, src: nc.vector.tensor_copy(et[:, :, i * S:(i + 1) * S], src))
        with ExitStack() as tmp, stage() as (block, (tables_in, gelu_u, gelu_v, root_in, root, centred, v, normed,
                                                     w_masked, gated, sq_done, sig, *_)):
            ws = sb("ws", [P, NH, P], where=tmp)
            gb = sb("gb", [P, 4, P], where=tmp)
            st2 = sb("st2", [P, 2, 16], where=tmp)
            vg = et[:, :, 0:512].rearrange("p t (h e) -> p t h e", e=HD)
            mean4 = st2[:, 0, :].rearrange("p (t h) -> p t h", t=TT).unsqueeze(3).broadcast_to([P, TT, NH, HD])
            var4 = st2[:, 1, :].rearrange("p (t h) -> p t h", t=TT).unsqueeze(3).broadcast_to([P, TT, NH, HD])
            sq4 = sq[:, 0:4, :].rearrange("p (t a) (h e) -> p t (a h) e", t=TT, e=HD)

            @block.sync
            def _(sp):
                sp.dma_start(ws[:, :, :], A["gm_w"]).then_inc(tables_in, 16)
                sp.dma_start(gb[:, :, :], A["gm_b"]).then_inc(tables_in, 16)

            @block.scalar
            def _(act):
                nc.scalar.activation(et[:, :, 0:512], et[:, :, 0:512], ACT.Gelu_apprx_tanh).then_inc(gelu_v, 1)
                nc.scalar.activation(ez[:, 0:4, :], ez[:, 0:4, :], ACT.Gelu_apprx_tanh).then_inc(gelu_u, 1)
                act.wait_ge(root_in, 1)
                nc.scalar.activation(st2[:, 1, :], st2[:, 1, :], ACT.Sqrt).then_inc(root, 1)
                nc.scalar.activation(et[:, :, 768:792], et[:, :, 768:792], ACT.Sigmoid)

            @block.vector
            def _(dve):
                n = counter()
                dve.wait_ge(tables_in, 32)
                causal = mat("upto0").unsqueeze(1).broadcast_to([P, NH, P])
                nc.vector.tensor_tensor(ws[:, :, :], ws[:, :, :], causal, ALU.mult).then_inc(w_masked, 1)
                dve.wait_ge(gelu_v, 1)
                nc.vector.tensor_reduce(st2[:, 0, :].rearrange("p (t h) -> p t h", t=TT), vg, AXX,
                                        ALU.add).then_inc(v, n.one())
                dve.wait_ge(v, n.now)
                nc.vector.tensor_scalar(st2[:, 0, :], st2[:, 0, :], 1.0 / HD, None, ALU.mult).then_inc(v, n.one())
                dve.wait_ge(v, n.now)
                nc.vector.tensor_tensor(vg, vg, mean4, ALU.subtract).then_inc(v, n.one())
                dve.wait_ge(v, n.now)
                nc.vector.tensor_tensor(sq4, vg, vg, ALU.mult).then_inc(v, n.one())
                dve.wait_ge(v, n.now)
                nc.vector.tensor_reduce(st2[:, 1, :].rearrange("p (t h) -> p t h", t=TT), sq4, AXX,
                                        ALU.add).then_inc(v, n.one())
                dve.wait_ge(v, n.now)
                nc.vector.tensor_scalar(st2[:, 1, :], st2[:, 1, :], 1.0 / HD, 1e-5, ALU.mult,
                                        ALU.add).then_inc(root_in, 1)
                dve.wait_ge(root, 1)
                nc.vector.reciprocal(st2[:, 1, :], st2[:, 1, :]).then_inc(v, n.one())
                dve.wait_ge(v, n.now)
                nc.vector.tensor_tensor(vg, vg, var4, ALU.mult).then_inc(normed, 1)
                dve.wait_ge(gelu_u, 1)
                for j in range(4):
                    dve.wait_ge(gated, j + 1)
                    m2 = mix[:, j, :].rearrange("p (c t) -> p c t", c=TT)
                    nc.vector.tensor_tensor(m2, ps[:, j, 0:S].rearrange("p (c t) -> p c t", c=TT),
                                            gb[:, j, :].unsqueeze(1).broadcast_to([P, TT, P]), ALU.add
                                            ).then_inc(v, n.one())
                    dve.wait_ge(v, n.now)
                    nc.vector.tensor_tensor(mix[:, j, :], mix[:, j, :], ez[:, j, :], ALU.mult)

            @block.tensor
            def _(pe):
                pe.wait_ge(w_masked, 1)
                pe.wait_ge(normed, 1)
                for j in range(4):
                    for h in (2 * j, 2 * j + 1):
                        for c in range(TT):
                            last = nc.tensor.matmul(ps[rows(h), j, c * P:(c + 1) * P], et[:, c, h * HD:(h + 1) * HD],
                                                    ws[:, h, :], start=True, stop=True)
                    last.then_inc(gated, 1)

        nsa = ExitStack()
        kcmp = sb("kcmp", [P, NC_CMP], where=nsa)
        vcmp = sb("vcmp", [NC_CMP, P], where=nsa)
        cmp_mask = sb("cmp_mask", [P, TT, NC_CMP], where=nsa)
        causal = sb("causal", [P, TT, S], where=nsa)
        any_cmp = sb("any_cmp", [P, TT], where=nsa)
        cmp_gate = sb("cmp_gate", [P, TT, NH], where=nsa)
        with ExitStack() as tmp, stage() as (block, (rope_in, w_in, rotated, v, pooled, hidden, hidden_ready, keys,
                                                     keys_copied, keys_rot, small_in, *_)):
            cos, sin = sb("cos", [P, S], where=tmp), sb("sin", [P, S], where=tmp)
            cosc, sinc = sb("cosc", [P, NC_CMP], where=tmp), sb("sinc", [P, NC_CMP], where=tmp)
            pe_cmp = sb("pe_cmp", [P, 2, 32], where=tmp)
            w1 = sb("w1", [P, 2, 32, HD], where=tmp)
            w2 = sb("w2", [P, 2, HD], where=tmp)
            blocks = sb("blocks", [P, 2, 32, NC_CMP], where=tmp)
            hc = sb("hc", [P, 2, NC_CMP], where=tmp)
            kraw = sb("kraw", [P, NC_CMP], where=tmp)
            krot = sb("krot", [P, NC_CMP], where=tmp)
            turned_qk = sb("turned_qk", [P, 6, S], where=tmp)
            roped = [4, 5, 6, 7, 10, 11]

            @block.sync
            def _(sp):
                for dst, name in ((cos[:, :], "cos"), (sin[:, :], "sin")):
                    sp.dma_start(dst, A[name]).then_inc(rope_in, 16)
                for dst, name in ((cosc[:, :], "cosc"), (sinc[:, :], "sinc"), (pe_cmp[:, :, :], "pe_cmp"),
                                  (cmp_mask[:, :, :], "cmp_mask"), (causal[:, :, :], "causal"),
                                  (any_cmp[:, :], "any_cmp")):
                    sp.dma_start(dst, A[name]).then_inc(small_in, 16)
                sp.dma_start(w1[:, :, :, :], A["cmp_w1"]).then_inc(w_in, 16)
                sp.dma_start(w2[:, :, :], A["cmp_w2"]).then_inc(w_in, 16)

            @block.tensor
            def _(pe):
                for n, i in enumerate(roped):
                    nc.tensor.matmul(ps[:, n // 2, n % 2 * S:n % 2 * S + S], mat("rotate"), ez[:, i, :], start=True,
                                     stop=True).then_inc(rotated, 1)
                pe.wait_ge(w_in, 32)
                pe.wait_ge(pooled, 2)
                for kv in range(2):
                    for g in range(2):
                        r = slice(g * HD, (g + 1) * HD)
                        for pos in range(32):
                            last = nc.tensor.matmul(ps[r, 3 + kv, 0:NC_CMP], w1[r, kv, pos, :],
                                                    blocks[r, kv, pos, :], start=(pos == 0), stop=(pos == 31))
                    last.then_inc(hidden, 1)
                pe.wait_ge(hidden_ready, 2)
                for g in range(2):
                    r = slice(g * HD, (g + 1) * HD)
                    nc.tensor.matmul(ps[r, 5, 0:NC_CMP], w2[r, 0, :], hc[r, 0, :], start=True, stop=True
                                     ).then_inc(keys, 1)
                    nc.tensor.matmul(ps[0:NC_CMP, 3 + g, r], hc[r, 1, :], w2[r, 1, :], start=True, stop=True
                                     ).then_inc(keys, 1)
                pe.wait_ge(keys_copied, 1)
                nc.tensor.matmul(ps[:, 7, 0:NC_CMP], mat("rotate"), kraw[:, :], start=True, stop=True
                                 ).then_inc(keys_rot, 1)

            @block.scalar
            def _(act):
                for kv in range(2):
                    act.wait_ge(hidden, kv + 1)
                    nc.scalar.activation(hc[:, kv, :], ps[:, 3 + kv, 0:NC_CMP], ACT.Gelu_apprx_tanh
                                         ).then_inc(hidden_ready, 1)
                act.wait_ge(keys, 4)
                for g in range(2):
                    r = slice(g * HD, (g + 1) * HD)
                    nc.scalar.activation(vcmp[:, r], ps[0:NC_CMP, 3 + g, r], ACT.Copy)

            @block.vector
            def _(dve):
                n = counter()
                dve.wait_ge(small_in, 16 * 6)
                for kv in range(2):
                    for part in range(2):
                        src = ez[:, 8 + kv, 16 * part:16 * part + 16 * NC_CMP].rearrange("p (n l) -> p l n", l=16)
                        nc.vector.tensor_tensor(blocks[:, kv, 16 * part:16 * part + 16, :], src,
                                                pe_cmp[:, kv, 16 * part:16 * part + 16].unsqueeze(2)
                                                .broadcast_to([P, 16, NC_CMP]), ALU.add).then_inc(v, n.one())
                dve.wait_ge(v, n.now)
                dve.sem_inc(pooled, 2)
                dve.wait_ge(rope_in, 32)
                dve.wait_ge(rotated, 6)
                nc.vector.tensor_tensor(turned_qk[:, :, :], ps[:, 0:3, :].rearrange("p b (c t) -> p (b c) t", t=S),
                                        sin[:, :].unsqueeze(1).broadcast_to([P, 6, S]), ALU.mult).then_inc(v, n.one())
                for a, b in ((4, 8), (10, 12)):
                    nc.vector.tensor_tensor(ez[:, a:b, :], ez[:, a:b, :],
                                            cos[:, :].unsqueeze(1).broadcast_to([P, b - a, S]),
                                            ALU.mult).then_inc(v, n.one())
                dve.wait_ge(v, n.now)
                nc.vector.tensor_tensor(ez[:, 4:8, :], ez[:, 4:8, :], turned_qk[:, 0:4, :], ALU.add)
                nc.vector.tensor_tensor(ez[:, 10:12, :], ez[:, 10:12, :], turned_qk[:, 4:6, :], ALU.add)
                gl = et[:, :, 768:792].rearrange("p t (h b) -> p t h b", b=3)
                nc.vector.tensor_tensor(cmp_gate[:, :, :], gl[:, :, :, 0:1].rearrange("p t h b -> p t (h b)"),
                                        any_cmp[:, :].unsqueeze(2).broadcast_to([P, TT, NH]), ALU.mult)
                dve.wait_ge(keys, 4)
                nc.vector.tensor_copy(kraw[:, :], ps[:, 5, 0:NC_CMP]).then_inc(keys_copied, 1)
                dve.wait_ge(keys_rot, 1)
                nc.vector.tensor_tensor(krot[:, :], ps[:, 7, 0:NC_CMP], sinc[:, :], ALU.mult).then_inc(v, n.one())
                dve.wait_ge(keys_copied, 1)
                nc.vector.tensor_tensor(kraw[:, :], kraw[:, :], cosc[:, :], ALU.mult).then_inc(v, n.one())
                dve.wait_ge(v, n.now)
                nc.vector.tensor_tensor(kcmp[:, :], kraw[:, :], krot[:, :], ALU.add)

        gl = et[:, :, 768:792].rearrange("p t (h b) -> p t h b", b=3)
        units = []
        for j in range(4):
            for g in range(2):
                h, r = j + 4 * g, slice(g * HD, (g + 1) * HD)
                base = dict(po=g * HD, j=4 + j, q=ez[r, 4 + j, :])
                units.append(dict(base, n=NC_CMP, k=kcmp[r, :], bias=cmp_mask[:, :, :], v=[vcmp[:, r]],
                                  gate=cmp_gate[:, :, h]))
                for b, keys_at, v_at in ((1, 10, 512), (2, 11, 640)):
                    units.append(dict(base, n=S, k=ez[r, keys_at, :], bias=causal[:, :, :],
                                      v=[et[:, t, v_at + g * HD:v_at + (g + 1) * HD] for t in range(TT)],
                                      gate=gl[:, :, h, b]))
        attention(units, mix, "nsa")
        nsa.close()
        even.close()
        project(T_OUT, mix, lambda i, src: nc.vector.tensor_tensor(one(xT, i), src, one(xT, i), ALU.add))
        swiglu(norm_w(0, 2))

        swiglu(norm_w(1, 0))
        odd = ExitStack()
        oz = sb("oz", [P, KT, S], where=odd)
        project(KT, xT, lambda i, src: nc.vector.tensor_tensor(one(oz, i), src, rstd[:, :], ALU.mult),
                gain=norm_w(1, 1))

        with ExitStack() as tmp, stage() as (block, (pool_in, v, pooled, mapped, *_)):
            pw = sb("pw", [P, 4, P], where=tmp)
            inv_count = sb("inv_count", [P, 4, S], where=tmp)
            sums_a = sb("sums_a", [P, 4, S], where=tmp)
            sums_b = sb("sums_b", [P, 4, S], where=tmp)

            @block.sync
            def _(sp):
                sp.dma_start(pw[:, :, :], A["pool_w"].rearrange("g c d -> c g d")).then_inc(pool_in, 16)
                sp.dma_start(inv_count[:, :, :], A["inv_count"]).then_inc(pool_in, 16)

            @block.vector
            def _(dve):
                n = counter()
                cur, nxt = oz[:, 0:4, :], sums_a[:, :, :]
                bufs = [sums_a[:, :, :], sums_b[:, :, :]]
                for lv in range(4):
                    shift = 1 << lv
                    nxt = bufs[lv % 2]
                    if lv:
                        nc.vector.tensor_copy(nxt[:, 0:lv, :], cur[:, 0:lv, :]).then_inc(v, n.one())
                    nc.vector.tensor_copy(nxt[:, lv:4, 0:shift], cur[:, lv:4, 0:shift]).then_inc(v, n.one())
                    nc.vector.tensor_tensor(nxt[:, lv:4, shift:S], cur[:, lv:4, shift:S], cur[:, lv:4, 0:S - shift],
                                            ALU.add).then_inc(v, n.one())
                    dve.wait_ge(v, n.now)
                    cur = nxt
                dve.wait_ge(pool_in, 32)
                nc.vector.tensor_tensor(sums_a[:, :, :], cur, inv_count[:, :, :], ALU.mult).then_inc(v, n.one())
                dve.wait_ge(v, n.now)
                nc.vector.tensor_tensor(sums_a[:, :, :], sums_a[:, :, :], oz[:, 0:4, :], ALU.subtract
                                        ).then_inc(pooled, 1)
                for g in range(4):
                    dve.wait_ge(mapped, g + 1)
                    nc.vector.tensor_scalar(mix[:, g, :], ps[:, g, 0:S], vec("pool_scale", g), None, ALU.mult)

            @block.tensor
            def _(pe):
                pe.wait_ge(pooled, 1)
                for g in range(4):
                    nc.tensor.matmul(ps[:, g, 0:S], pw[:, g, :], sums_a[:, g, :], start=True, stop=True
                                     ).then_inc(mapped, 1)

        s5 = ExitStack()
        decay = sb("decay", [P, S5T], where=s5)
        fre, fim = sb("fre", [P, S5T], where=s5), sb("fim", [P, S5T], where=s5)
        wre, wim = sb("wre", [P, S5T, S], where=s5), sb("wim", [P, S5T, S], where=s5)
        s5_b = sb("s5_b", [P, 4, 2, P], where=s5)
        s5_c = sb("s5_c", [P, 2, S5T, 32], where=s5)
        with ExitStack() as tmp, stage() as (block, (dt_ready, args, trig, v, b_in, half_in, *_)):
            dt = sb("dt", [P, S5T], where=tmp)
            t1, t2, t3, t4, th = (sb(f"t{i}", [P, S5T], where=tmp) for i in range(5))
            cre = sb("cre", [P, S5T, 32], where=tmp)
            big1, big2 = sb("big1", [P, S5T, P], where=tmp), sb("big2", [P, S5T, P], where=tmp)
            step_re, step_im = sb("step_re", [P, S5T], where=tmp), sb("step_im", [P, S5T], where=tmp)

            @block.sync
            def _(sp):
                sp.dma_start(s5_b[:, :, :, :], A["s5_b"]).then_inc(b_in, 16)
                sp.dma_start(s5_c[:, :, :, :], A["s5_c"]).then_inc(b_in, 16)

            @block.scalar
            def _(act):
                nc.scalar.activation(dt[:, :], vec_all("log_dt"), ACT.Exp).then_inc(dt_ready, 1)
                act.wait_ge(args, 1)
                nc.scalar.activation(decay[:, :], decay[:, :], ACT.Exp).then_inc(trig, 1)
                act.wait_ge(args, 2)
                nc.scalar.activation(t1[:, :], th[:, :], ACT.Sin).then_inc(trig, 1)
                nc.scalar.activation(t2[:, :], th[:, :], ACT.Sin, scale=0.5).then_inc(trig, 1)

            @block.vector
            def _(dve):
                n = counter()

                def step(ins):
                    ins.then_inc(v, n.one())
                    dve.wait_ge(v, n.now)
                tt, ts = nc.vector.tensor_tensor, nc.vector.tensor_scalar
                lre, lim = vec_all("lam_re"), vec_all("lam_im")
                dve.wait_ge(dt_ready, 1)
                tt(decay[:, :], lre, dt[:, :], ALU.mult).then_inc(args, 1)
                step(tt(th[:, :], lim, dt[:, :], ALU.mult))
                step(ts(t3[:, :], th[:, :], 1.0 / (2 * np.pi), None, ALU.mult))
                step(ts(t3[:, :], t3[:, :], 12582912.0, None, ALU.add))
                step(ts(t3[:, :], t3[:, :], -12582912.0, None, ALU.add))
                rest = 2 * np.pi
                for part in (6.28125, 0.0019350051879882812, float(2 * np.pi - 6.28125 - 0.0019350051879882812)):
                    step(nc.vector.scalar_tensor_tensor(th[:, :], t3[:, :], -part, th[:, :], ALU.mult, ALU.add))
                ts(th[:, :], th[:, :], 3.1415925, -3.1415925, ALU.min, ALU.max).then_inc(args, 1)
                dve.wait_ge(trig, 3)
                step(tt(t2[:, :], t2[:, :], t2[:, :], ALU.mult))
                step(ts(t2[:, :], t2[:, :], -2.0, 1.0, ALU.mult, ALU.add))
                tt(t4[:, :], decay[:, :], t1[:, :], ALU.mult).then_inc(v, n.one())
                step(tt(t3[:, :], decay[:, :], t2[:, :], ALU.mult))
                step(ts(t3[:, :], t3[:, :], -1.0, None, ALU.add))
                tt(fre[:, :], t3[:, :], lre, ALU.mult).then_inc(v, n.one())
                tt(fim[:, :], t4[:, :], lre, ALU.mult).then_inc(v, n.one())
                tt(th[:, :], t4[:, :], lim, ALU.mult).then_inc(v, n.one())
                step(tt(t3[:, :], t3[:, :], lim, ALU.mult))
                tt(fre[:, :], fre[:, :], th[:, :], ALU.add).then_inc(v, n.one())
                tt(fim[:, :], fim[:, :], t3[:, :], ALU.subtract).then_inc(v, n.one())
                tt(dt[:, :], lre, lre, ALU.mult).then_inc(v, n.one())
                step(tt(t4[:, :], lim, lim, ALU.mult))
                step(tt(dt[:, :], dt[:, :], t4[:, :], ALU.add))
                step(nc.vector.reciprocal(dt[:, :], dt[:, :]))
                tt(fre[:, :], fre[:, :], dt[:, :], ALU.mult).then_inc(v, n.one())
                step(tt(fim[:, :], fim[:, :], dt[:, :], ALU.mult))
                dve.wait_ge(b_in, 32)
                wide = [P, S5T, 32]
                fr, fi = fre[:, :].unsqueeze(2).broadcast_to(wide), fim[:, :].unsqueeze(2).broadcast_to(wide)
                tt(cre[:, :, :], s5_c[:, 0], fi, ALU.mult).then_inc(v, n.one())
                step(tt(big1[:, :, 0:32], s5_c[:, 1], fi, ALU.mult))
                tt(s5_c[:, 0], s5_c[:, 0], fr, ALU.mult).then_inc(v, n.one())
                step(tt(s5_c[:, 1], s5_c[:, 1], fr, ALU.mult))
                tt(s5_c[:, 0], s5_c[:, 0], big1[:, :, 0:32], ALU.subtract).then_inc(v, n.one())
                step(tt(s5_c[:, 1], s5_c[:, 1], cre[:, :, :], ALU.add))
                step(ts(s5_c[:, 1].rearrange("p a b -> p (a b)"), s5_c[:, 1].rearrange("p a b -> p (a b)"), -1.0, None,
                        ALU.mult))
                nc.vector.memset(wre[:, :, 0:1], 1.0).then_inc(v, n.one())
                nc.vector.memset(wim[:, :, 0:1], 0.0).then_inc(v, n.one())
                nc.vector.tensor_copy(step_re[:, :], t2[:, :]).then_inc(v, n.one())
                step(nc.vector.tensor_copy(step_im[:, :], t1[:, :]))
                size = 1
                while size < S:
                    low, high = slice(0, size), slice(size, 2 * size)
                    shape = [P, S5T, size]
                    sr = step_re[:, :].unsqueeze(2).broadcast_to(shape)
                    si = step_im[:, :].unsqueeze(2).broadcast_to(shape)
                    tt(wre[:, :, high], wre[:, :, low], sr, ALU.mult).then_inc(v, n.one())
                    tt(wim[:, :, high], wre[:, :, low], si, ALU.mult).then_inc(v, n.one())
                    tt(big1[:, :, low], wim[:, :, low], si, ALU.mult).then_inc(v, n.one())
                    tt(big2[:, :, low], wim[:, :, low], sr, ALU.mult).then_inc(v, n.one())
                    dve.wait_ge(v, n.now)
                    tt(wre[:, :, high], wre[:, :, high], big1[:, :, low], ALU.subtract).then_inc(v, n.one())
                    tt(wim[:, :, high], wim[:, :, high], big2[:, :, low], ALU.add).then_inc(v, n.one())
                    tt(t3[:, :], step_re[:, :], step_re[:, :], ALU.mult).then_inc(v, n.one())
                    tt(t4[:, :], step_im[:, :], step_im[:, :], ALU.mult).then_inc(v, n.one())
                    step(tt(th[:, :], step_re[:, :], step_im[:, :], ALU.mult))
                    tt(step_re[:, :], t3[:, :], t4[:, :], ALU.subtract).then_inc(v, n.one())
                    step(ts(step_im[:, :], th[:, :], 2.0, None, ALU.mult))
                    size *= 2

        with ExitStack() as tmp, stage() as (block, (fed, v, scanned, w, turned_back, out_ready, crossed, *_)):
            a1, a2, a3, a4 = (sb(f"a{i}", [P, S], where=tmp) for i in range(4))
            zre, zim = sb("zre", [P, 2, S], where=tmp), sb("zim", [P, 2, S], where=tmp)
            b1, b2, b3, b4 = (sb(f"b{i}", [P, S], where=tmp) for i in range(4))
            xre, xim = sb("xre", [P, 2, S], where=tmp), sb("xim", [P, 2, S], where=tmp)

            @block.tensor
            def _(pe):
                for s in range(S5T + 2):
                    if s < S5T:
                        if s >= 2:
                            pe.wait_ge(v, s - 1)
                        r = slice(32 * (s % 4), 32 * (s % 4) + 32)
                        for c in range(2):
                            last = nc.tensor.matmul(ps[:, s % 2, c * S:(c + 1) * S], s5_b[r, s // 4, c, :],
                                                    oz[r, 4 + s // 4, :], start=True, stop=True)
                        last.then_inc(fed, 1)
                    if s >= 2:
                        i = s - 2
                        pe.wait_ge(turned_back, i + 1)
                        r = slice(32 * (i % 4), 32 * (i % 4) + 32)
                        nc.tensor.matmul(ps[r, 2 + i // 4, 0:S], s5_c[:, 0, i, :], xre[:, i % 2, :], start=True,
                                         stop=False)
                        nc.tensor.matmul(ps[r, 2 + i // 4, 0:S], s5_c[:, 1, i, :], xim[:, i % 2, :], start=False,
                                         stop=True).then_inc(out_ready, 1)

            @block.vector
            def _(dve):
                tt = nc.vector.tensor_tensor
                n = counter()
                for s in range(S5T):
                    dve.wait_ge(fed, s + 1)
                    bre, bim = ps[:, s % 2, 0:S], ps[:, s % 2, S:2 * S]
                    if s:
                        dve.wait_ge(scanned, 2 * s)
                    tt(a1[:, :], bre, wre[:, s, :], ALU.mult).then_inc(w, n.one())
                    tt(a2[:, :], bim, wim[:, s, :], ALU.mult).then_inc(w, n.one())
                    tt(a3[:, :], bim, wre[:, s, :], ALU.mult).then_inc(w, n.one())
                    tt(a4[:, :], bre, wim[:, s, :], ALU.mult).then_inc(v, 1)
                    dve.wait_ge(w, n.now)
                    tt(a1[:, :], a1[:, :], a2[:, :], ALU.add).then_inc(w, n.one())
                    dve.wait_ge(v, s + 1)
                    tt(a3[:, :], a3[:, :], a4[:, :], ALU.subtract).then_inc(w, n.one())
                    dve.wait_ge(w, n.now)
                    if s >= 2:
                        dve.wait_ge(turned_back, s - 1)
                    nc.vector.tensor_tensor_scan(zre[:, s % 2, :], decay[:, s:s + 1].broadcast_to([P, S]), a1[:, :], 0.0, ALU.mult,
                                                 ALU.add).then_inc(scanned, 1)
                    nc.vector.tensor_tensor_scan(zim[:, s % 2, :], decay[:, s:s + 1].broadcast_to([P, S]), a3[:, :], 0.0, ALU.mult,
                                                 ALU.add).then_inc(scanned, 1)

            @block.gpsimd
            def _(pool):
                tt = nc.gpsimd.tensor_tensor
                for s in range(S5T):
                    pool.wait_ge(scanned, 2 * s + 2)
                    zr, zi, cr, ci = zre[:, s % 2, :], zim[:, s % 2, :], wre[:, s, :], wim[:, s, :]
                    if s:
                        pool.wait_ge(turned_back, s)
                    tt(b1[:, :], zr, cr, ALU.mult)
                    tt(b2[:, :], zi, ci, ALU.mult)
                    tt(b3[:, :], zr, ci, ALU.mult)
                    tt(b4[:, :], zi, cr, ALU.mult).then_inc(crossed, 1)
                    pool.wait_ge(crossed, s + 1)
                    if s >= 2:
                        pool.wait_ge(out_ready, s - 1)
                    tt(xre[:, s % 2, :], b1[:, :], b2[:, :], ALU.subtract)
                    tt(xim[:, s % 2, :], b3[:, :], b4[:, :], ALU.add).then_inc(turned_back, 1)

        with stage() as (block, (skipped, gelued, *_)):
            @block.vector
            def _(dve):
                for j in range(4):
                    nc.vector.scalar_tensor_tensor(oz[:, 4 + j, :], oz[:, 4 + j, :], vec("s5_d", j), ps[:, 2 + j, 0:S],
                                                   ALU.mult, ALU.add).then_inc(skipped, 1)

            @block.scalar
            def _(act):
                act.wait_ge(skipped, 4)
                nc.scalar.activation(oz[:, 4:8, :], oz[:, 4:8, :], ACT.Gelu_apprx_tanh)
        s5.close()

        with ExitStack() as tmp, stage() as (block, (src_high, src_low, sig_done, multiplied, *_)):
            sg = sb("sg", [P, 2, S], where=tmp)
            first = take(T_GLU)

            @block.sync
            def _(sp):
                refill(sp, first, T_GLU)

            @block.tensor
            def _(pe):
                for i in range(T_GLU):
                    pe.wait_ge(tiles_freed, first + i + 1)
                    for q in range(2):
                        for k in range(4):
                            if i == 0 and q == 0:
                                pe.wait_ge(src_low, k + 1)
                            last = product(ps[:, i, q * S:(q + 1) * S], first + i, 4 * q + k,
                                           (srch[:, k, :], srcl[:, k, :]), k == 0, k == 3)
                    last.then_inc(tiles_used, 1)

            @block.scalar
            def _(act):
                for k in range(4):
                    nc.scalar.activation(srch[:, k, :], oz[:, 4 + k, :], ACT.Copy).then_inc(src_high, 1)
                for i in range(T_GLU):
                    high(act, first + AHEAD + i)
                    act.wait_ge(tiles_used, first + i - T_ADA + 1)
                    if i >= 2:
                        act.wait_ge(multiplied, i - 1)
                    nc.scalar.activation(sg[:, i % 2, :], ps[:, i, S:2 * S], ACT.Sigmoid).then_inc(sig_done, 1)

            @block.vector
            def _(dve):
                for k in range(4):
                    dve.wait_ge(src_high, k + 1)
                    nc.vector.tensor_tensor(srcl[:, k, :], oz[:, 4 + k, :], srch[:, k, :].bitcast(F32), ALU.subtract
                                            ).then_inc(src_low, 1)
                for i in range(T_GLU):
                    low(dve, first + AHEAD + i)
                    dve.wait_ge(sig_done, i + 1)
                    nc.vector.tensor_tensor(mix[:, 4 + i, :], ps[:, i, 0:S], sg[:, i % 2, :], ALU.mult
                                            ).then_inc(multiplied, 1)
        odd.close()
        project(KT, mix, lambda i, src: nc.vector.tensor_tensor(one(xT, i), src, one(xT, i), ALU.add))
        swiglu(norm_w(1, 2))
        rms_norm(lambda k: vec("final", k), None)
        assert stream[0] == TOTAL, (stream[0], TOTAL)
        with stage() as (block, _):
            @block.sync
            def _(sp):
                sp.dma_start(A["out"].rearrange("(k p) t -> p k t", p=P), hT[:, :, :]).then_inc(stored, 16)
                sp.wait_ge(stored, 16)


def tiles_of(w, order=None):
    k, n = w.shape
    t = w.reshape(k // P, P, n // P, P).transpose(2, 1, 0, 3).reshape(n // P, P, -1)
    return t if order is None else t[order]


def token_tiles_of(w):
    k, n = w.shape
    return w.reshape(2, KT // 2, P, n // S, S).transpose(3, 0, 2, 1, 4).reshape(2 * n // S, P, D)


def layout(a):
    f = {k: np.asarray(v) for k, v in a.items()}
    parts = [f["ada_w"][0].reshape(KT, P, 6, D).transpose(0, 2, 1, 3).reshape(T_ADA, P, D),
             token_tiles_of(f["w_in"][0][:, 1024:1536]),
             tiles_of(f["w_in"][0], list(range(0, 8)) + list(range(12, 26))),
             tiles_of(f["w_out"][0]), tiles_of(f["peer_w_query"][0])]

    def ffn(layer, which):
        g, u = tiles_of(f["ffn_w_gate_2"][layer, which]), tiles_of(f["ffn_w_up_2"][layer, which])
        d = f["ffn_w_down_2"][layer, which].reshape(FJ, P, D)
        seq = [g[0], u[0]]
        for j in range(1, FJ):
            seq += [g[j], u[j], d[j - 1]]
        return np.stack(seq + [d[FJ - 1]])
    parts.append(ffn(0, 0))
    w = f["ev_w_in_2"][0]
    q = w[:, 1024:1536].reshape(D, 2, 4, HD).transpose(0, 2, 1, 3).reshape(D, 512)
    kc, vc, ks, vs, kw, vw = (w[:, 1536 + P * i:1536 + P * i + P] for i in range(6))
    gl = np.zeros((D, 2 * P), np.float32)
    gl[:, :24] = w[:, 2304:2328]
    parts.append(token_tiles_of(np.concatenate([w[:, 512:1024], vs, vw, gl], axis=1)))
    parts.append(tiles_of(np.concatenate([w[:, 0:512], q, kc, vc, ks, kw], axis=1)))
    wo = f["ev_w_out_2"][0]
    parts.append(tiles_of(np.concatenate([wo[:512], wo[512:].reshape(2, 4, HD, D).transpose(1, 0, 2, 3)
                                          .reshape(512, D)], axis=0)))
    parts += [ffn(0, 1), ffn(1, 0), tiles_of(f["od_w_in_2"][0])]
    glu = f["s5_w_glu_2"][0]
    ab = np.stack([tiles_of(glu[:, :512]), tiles_of(glu[:, 512:])], axis=2)
    parts += [ab.reshape(4, P, D), tiles_of(f["od_w_out_2"][0]), ffn(1, 1)]
    out = {"stream": np.concatenate(parts, axis=0)}

    def cols(v):
        return np.asarray(v).reshape(-1, P).T
    vectors = {"c": cols(f["c"]), "ada_b": cols(f["ada_b"]), "norm1_g": cols(f["norm1_g"]), "mu_prev": cols(f["mu_prev"]),
               "mu_next": cols(f["mu_next"]), "w_decay0": cols(f["w_decay0"]), "a_gate0": cols(f["a_gate0"]),
               "k_k": cols(f["k_k"]), "k_a": cols(f["k_a"]), "r_k": cols(f["r_k"]), "lnx_g": cols(f["lnx_g"]),
               "lnx_b": cols(f["lnx_b"]), "norm2_g": cols(f["norm2_g"]), "q_norm_g": cols(np.tile(f["q_norm_g"][0], 2)),
               "k_norm_g": cols(np.tile(f["k_norm_g"][0], 2)), "norm_w": cols(f["norm_w_2"]),
               "final": cols(f["final_norm_w_2"]), "pool_scale": cols(f["pool_scale_2"]), "s5_d": cols(f["s5_d_2"]),
               "lam_re": cols(f["s5_lam_re_2"]), "lam_im": cols(f["s5_lam_im_2"]),
               "log_dt": cols(np.repeat(f["s5_log_dt_2"][0], 64))}
    out["vecs"] = np.concatenate([vectors[n] for n in VEC], axis=1)
    out["xT"] = f["x"][0].T
    out["mats"] = constant_matrices()
    out["lora_up"] = np.concatenate([f["w_decay_up"][0].transpose(1, 0, 2), f["a_gate_up"][0].transpose(1, 0, 2)], 0)
    out["g_up"] = f["g_up"][0]
    out["subkeys"] = np.stack([f["peer_sub_keys1"][0].T, f["peer_sub_keys2"][0].T], axis=1)
    out["peer_u"], out["peer_v"] = f["peer_u"][0], f["peer_v"][0]
    out["gm_w"] = f["gm_w_s_2"][0].transpose(2, 0, 1)
    out["gm_b"] = np.repeat(f["gm_b_2"][0].reshape(4, 2, P), HD, axis=1).transpose(1, 0, 2)
    out["cmp_w1"] = np.tile(f["nsa_cmp_w1_2"][0].reshape(2, 32, HD, HD).transpose(2, 0, 1, 3), (2, 1, 1, 1))
    out["cmp_w2"] = np.tile(f["nsa_cmp_w2_2"][0].transpose(1, 0, 2), (2, 1, 1))
    out["pe_cmp"] = np.tile(f["nsa_cmp_pe_2"][0].transpose(2, 0, 1), (2, 1, 1))
    out["pool_w"] = f["pool_w_2"][0]
    b = np.zeros((4, 4, 2, 16, 2, 2, 64), np.float32)
    c = np.zeros((2, 64, 2, S5T, 2, 16), np.float32)
    for i, (bb, cc) in enumerate(((f["s5_b_re_2"][0], f["s5_c_re_2"][0]), (f["s5_b_im_2"][0], f["s5_c_im_2"][0]))):
        bb = bb.reshape(4, 4, 2, 64, 16)
        cc = cc.reshape(S5T, 2, 16, 64)
        for g in range(2):
            b[:, :, g, :, i, g, :] = bb[:, :, g].transpose(0, 1, 3, 2)
            c[g, :, i, :, g, :] = cc[:, g].transpose(2, 0, 1)
    out["s5_b"] = b.reshape(4, P, 2, P).transpose(1, 0, 2, 3)
    out["s5_c"] = c.reshape(P, 2, S5T, 32)

    t = np.arange(S)
    dist = np.abs(t[:, None] - t[None, :])
    patterns = ((128, 1), (512, 4), (2048, 16))
    seen = sum(((dist % d == 0) & (dist <= w // 2)).astype(np.float32) for w, d in patterns)
    slopes = np.exp2(-8.0 * (np.arange(NH, dtype=np.float32) + 1) / NH).astype(np.float32)
    logs = np.where(seen > 0, np.log(np.maximum(seen, 1)), NEG).astype(np.float32)
    out["attn_bias"] = (logs[None] - slopes[:, None, None] * dist[None].astype(np.float32)).astype(np.float32)
    out["causal"] = np.where(t[None, :] <= t[:, None], 0, NEG).astype(np.float32).reshape(TT, P, S).transpose(1, 0, 2)
    end = np.arange(NC_CMP) * 16 + 31
    valid = end[None, :] <= t[:, None]
    out["cmp_mask"] = np.where(valid, 0, NEG).astype(np.float32).reshape(TT, P, NC_CMP).transpose(1, 0, 2)
    out["any_cmp"] = valid.any(axis=1).astype(np.float32).reshape(TT, P).T
    half = HD // 2
    inv = np.float32(10000.0) ** (-np.arange(half, dtype=np.float32) / half)
    for pos, tag in ((t, ""), (end, "c")):
        ang = pos.astype(np.float32)[None, :] * np.tile(inv, 4)[:, None]
        out["cos" + tag], out["sin" + tag] = np.cos(ang).astype(np.float32), np.sin(ang).astype(np.float32)
    counts = np.minimum(t[None, :] + 1, np.array([2, 4, 8, 16])[:, None]).astype(np.float32)
    out["inv_count"] = np.broadcast_to((1 / counts).astype(np.float32), (P, 4, S))
    return {k: np.ascontiguousarray(v) for k, v in out.items()}


def kernel(**inputs):
    import concourse.bacc as bacc
    from concourse.bass_utils import run_bass_kernel_spmd

    nc = bacc.Bacc("TRN2", target_bir_lowering=False, num_devices=1)
    arrays = {"in_" + k: v for k, v in layout(inputs).items()}
    aps = {k[3:]: nc.dram_tensor(k, v.shape, F32, kind="ExternalInput").ap() for k, v in arrays.items()}
    aps["out"] = nc.dram_tensor("out_xT", (D, S), F32, kind="ExternalOutput").ap()
    build(nc, aps)
    result = run_bass_kernel_spmd(nc, [arrays], core_ids=[0]).results[0]["out_xT"]
    return np.ascontiguousarray(np.asarray(result).T).reshape(1, S, D)
```

```python
from contextlib import ExitStack, contextmanager

import numpy as np

import concourse.bass as bass
from concourse import mybir

F32 = mybir.dt.float32
F32R = mybir.dt.float32r
U32 = mybir.dt.uint32
ACT = mybir.ActivationFunctionType
ALU = mybir.AluOpType
AXX = mybir.AxisListType.X

P = 128
S = 256
TT = S // P
D = 1024
KT = D // P
HD = 64
NH = 8
RING = 6
PAIRS = 3
AHEAD = 2
FFN = 2816
FJ = FFN // P
NE = 128
TOPK = 16
SLOTS = NH * TOPK
NEG = -1e30
NC_CMP = (S - 32) // 16 + 1
S5T = 16
NORM_EPS = 1e-6

T_ADA, T_IN_TOK, T_IN, T_OUT, T_QUERY = 48, 4, 22, 8, 16
T_FFN = 3 * FJ
T_EV_TOK, T_EV, T_GLU = 8, 12, 4
TOTAL = (T_ADA + T_IN_TOK + T_IN + T_OUT + T_QUERY + 4 * T_FFN + T_EV_TOK + T_EV + T_OUT + KT + T_GLU + KT)

VEC = {}
_at = 0
for _name, _n in (("c", 8), ("ada_b", 48), ("norm1_g", 8), ("mu_prev", 14), ("mu_next", 14), ("w_decay0", 8), ("a_gate0", 8),
                  ("k_k", 4), ("k_a", 4), ("r_k", 4), ("lnx_g", 4), ("lnx_b", 4), ("norm2_g", 8), ("q_norm_g", 1),
                  ("k_norm_g", 1), ("norm_w", 48), ("final", 8), ("pool_scale", 4), ("s5_d", 4), ("lam_re", S5T),
                  ("lam_im", S5T), ("log_dt", S5T)):
    VEC[_name] = (_at, _at + _n)
    _at += _n
NVEC = _at

MATS = ["ident", "ones", "blockones", "rotate"]
for _d in range(2):
    MATS += [f"strict{_d}", f"upto{_d}"] + [f"level{_d}_{b}" for b in (1, 2, 4, 8, 16, 32, 64)]
MATS += ["level_row0", "level_row1"]
MAT = {n: i for i, n in enumerate(MATS)}


def constant_matrices():
    t = np.arange(P)
    a, b = t[:, None], t[None, :]
    out = np.zeros((len(MATS), P, P), np.float32)
    out[MAT["ident"]] = a == b
    out[MAT["ones"]] = 1
    out[MAT["blockones"]] = a // HD == b // HD
    half = HD // 2
    rot = np.zeros((P, P), np.float32)
    for m in range(P):
        rot[(m + half, m) if m % HD < half else (m - half, m)] = -1 if m % HD < half else 1
    out[MAT["rotate"]] = rot
    for d in range(2):
        later = (b > a) if d == 0 else (b < a)
        out[MAT[f"strict{d}"]] = later
        out[MAT[f"upto{d}"]] = later | (a == b)
        for n in (1, 2, 4, 8, 16, 32, 64):
            out[MAT[f"level{d}_{n}"]] = later & (a // (2 * n) == b // (2 * n)) & (a // n != b // n)
        out[MAT[f"level_row{d}"]] = out[MAT[f"level{d}_1"]].T
    return out


class counter:
    def __init__(self):
        self.now = 0

    def __call__(self):
        self.now += 1
        return self.now

    def one(self):
        self.now += 1
        return 1


def over_tiles(eng, first, count, body):
    turns = count // RING if count >= 2 * RING else 0
    if turns:
        with eng.Fori(0, turns) as g:
            for u in range(RING):
                body(g * RING + u, (first + u) % RING, g + (first + u) // RING)
    for i in range(turns * RING, count):
        body(i, (first + i) % RING, (first + i) // RING)


def build(nc, A):
    with ExitStack() as ctx:
        def sb(name, shape, dt=F32, where=ctx):
            return where.enter_context(nc.sbuf_tensor(name, shape, dt))

        def sem(name):
            return ctx.enter_context(nc.semaphore(name))

        ring = sb("ring", [P, RING, D])
        xT = sb("xT", [P, KT, S])
        hT = sb("hT", [P, KT, S])
        srch, srcl = sb("srch", [P, KT, S], F32R), sb("srcl", [P, KT, S], F32R)
        wh, wl = sb("wh", [P, PAIRS, D], F32R), sb("wl", [P, PAIRS, D], F32R)
        mix = sb("mix", [P, KT, S])
        sq = sb("sq", [P, KT, S])
        rstd = sb("rstd", [P, S])
        vecs = sb("vecs", [P, NVEC])
        mats = sb("mats", [P, len(MATS), P])
        mod = sb("mod", [P, 48])
        gs = sb("gs", [P, 2, KT])
        ps = ctx.enter_context(nc.psum_tensor("ps", [P, 8, 512], F32))

        loaded = [sem(f"tile_loaded{i}") for i in range(RING)]
        high_done = sem("high_done")
        tiles_freed = sem("tiles_freed")
        tiles_used = sem("tiles_used")
        consts_in = sem("consts_in")
        table_in = sem("table_in")
        stored = sem("stored")
        tables = counter()
        sets = [[sem(f"stage{j}_{i}") for i in range(14)] for j in range(2)]
        stages = [0]
        stream = [0]

        def vec(name, i=0):
            return vecs[:, VEC[name][0] + i:VEC[name][0] + i + 1]

        def vec_all(name):
            return vecs[:, VEC[name][0]:VEC[name][1]]

        def mat(name):
            return mats[:, MAT[name], :]

        @contextmanager
        def stage():
            mine, other = sets[stages[0] % 2], sets[1 - stages[0] % 2]
            again = stages[0] > 0
            stages[0] += 1
            with nc.Block() as block:
                if again:
                    @block.gpsimd
                    def _(pool):
                        pool.sem_clear(range(other[0].num, other[0].num + len(other)))
                yield block, mine

        def take(count):
            stream[0] += count
            return stream[0] - count

        def refill(sp, first, count):
            def load(i, slot, turn):
                sp.wait_ge(tiles_freed, i + (first + 1))
                sp.dma_start(ring[:, slot, :], A["stream"][bass.ds(i + (first + RING), 1)]
                             .rearrange("a p n -> (a p) n")).then_inc(loaded[slot], 16)
            over_tiles(sp, first, min(count, TOTAL - RING - first), load)

        with stage() as (block, _):
            @block.sync
            def _(sp):
                for i in range(RING):
                    sp.dma_start(ring[:, i, :], A["stream"][i]).then_inc(loaded[i], 16)

            @block.scalar
            def _(act):
                act.dma_start(vecs[:, :], A["vecs"]).then_inc(consts_in, 16)
                act.dma_start(xT[:, :, :], A["xT"].rearrange("(k p) t -> p k t", p=P)).then_inc(consts_in, 16)
                act.dma_start(mats[:, :, :], A["mats"].rearrange("m p n -> p m n")).then_inc(consts_in, 16)
                act.wait_ge(consts_in, 48)

        def high(act, tile, turns=0):
            n = tile - T_ADA
            act.wait_ge(loaded[tile % RING], turns * 16 + 16 * (tile // RING + 1))
            if n >= PAIRS:
                act.wait_ge(tiles_used, turns * RING + (n - PAIRS + 1))
            nc.scalar.activation(wh[:, n % PAIRS, :], ring[:, tile % RING, :], ACT.Copy).then_inc(high_done, 1)

        def low(dve, tile, turns=0):
            n = tile - T_ADA
            dve.wait_ge(high_done, turns * RING + (n + 1))
            nc.vector.tensor_tensor(wl[:, n % PAIRS, :], ring[:, tile % RING, :],
                                    wh[:, n % PAIRS, :].bitcast(F32), ALU.subtract).then_inc(tiles_freed, 1)

        def product(out, tile, k, source, start, stop, turns=0, token_major=False, src=None):
            n = (tile - T_ADA) % PAIRS
            cols = slice(k * S, (k + 1) * S) if token_major else slice(k * P, (k + 1) * P)
            w = wh[:, n, cols], wl[:, n, cols]
            for p, (a, b) in enumerate(((0, 0), (0, 1), (1, 0))):
                left, right = (source[b], w[a]) if token_major else (w[a], source[b])
                last = nc.tensor.matmul(out, left, right, start=(start and p == 0), stop=(stop and p == 2),
                                        skip_group_check=True)
            return last

        def split_high(act, src, gain, done):
            for k in range(KT):
                nc.scalar.activation(srch[:, k, :], src[:, k, :], ACT.Copy, scale=gain(k) if gain else 1.0
                                     ).then_inc(done, 1)

        def split_low(dve, src, gain, high_part, done):
            for k in range(KT):
                dve.wait_ge(high_part, k + 1)
                nc.vector.scalar_tensor_tensor(srcl[:, k, :], src[:, k, :], gain(k) if gain else 1.0,
                                               srch[:, k, :].bitcast(F32), ALU.mult, ALU.subtract).then_inc(done, 1)

        CHUNKS = 6 * D // D
        with ExitStack() as tmp, stage() as (block, (c_ready, columns, v, *_)):
            cs = sb("cs", [P, KT], where=tmp)
            acc = sb("acc", [P, CHUNKS, D], where=tmp)
            first = take(T_ADA)

            @block.sync
            def _(sp):
                refill(sp, first, T_ADA)

            @block.scalar
            def _(act):
                nc.scalar.activation(cs[:, :], vec_all("c"), ACT.Silu).then_inc(c_ready, 1)
                for n in range(AHEAD):
                    high(act, T_ADA + n)

            @block.vector
            def _(dve):
                dve.wait_ge(c_ready, 1)
                HALF = CHUNKS // 2
                tiles = HALF * KT
                assert tiles % RING == 0
                with dve.Fori(0, 2) as g:
                    for i in range(tiles):
                        chunk, k, slot = i // KT, i % KT, i % RING
                        total = acc[:, bass.ds(g * HALF + chunk, 1), :].rearrange("p a n -> p (a n)")
                        dve.wait_ge(loaded[slot], g * (16 * tiles // RING) + 16 * (i // RING + 1))
                        if k == 0:
                            nc.vector.tensor_scalar(total, ring[:, slot, :], cs[:, 0:1], None, ALU.mult
                                                    ).then_inc(tiles_freed, 1)
                        else:
                            dve.wait_ge(tiles_freed, g * tiles + i)
                            nc.vector.scalar_tensor_tensor(total, ring[:, slot, :], cs[:, k:k + 1], total, ALU.mult,
                                                           ALU.add).then_inc(tiles_freed, 1)
                for n in range(AHEAD):
                    low(dve, T_ADA + n)
                dve.wait_ge(columns, 1)
                nc.vector.tensor_tensor(mod[:, :], ps[:, 0, 0:48], vec_all("ada_b"), ALU.add).then_inc(v, 1)
                dve.wait_ge(v, 1)
                for n, name in ((0, "norm1_g"), (1, "norm2_g")):
                    nc.vector.scalar_tensor_tensor(gs[:, n, :], mod[:, 24 * n + 8:24 * n + 16], 1.0, vec_all(name),
                                                   ALU.add, ALU.mult)

            @block.tensor
            def _(pe):
                for u in range(CHUNKS):
                    pe.wait_ge(tiles_freed, first + KT * (u + 1))
                    for j in range(KT):
                        last = nc.tensor.matmul(ps[:, 0, u * KT + j:u * KT + j + 1], acc[:, u, j * P:(j + 1) * P],
                                                mat("ones")[:, 0:1], start=True, stop=True)
                last.then_inc(columns, 1)

        def rms_norm(gain, shift):
            with stage() as (block, (squared, summed, scaled, root, v, *_)):
                @block.scalar
                def _(act):
                    for k in range(KT):
                        nc.scalar.activation(sq[:, k, :], xT[:, k, :], ACT.Square).then_inc(squared, 1)
                    act.wait_ge(scaled, 1)
                    nc.scalar.activation(rstd[:, :], rstd[:, :], ACT.Sqrt).then_inc(root, 1)

                @block.tensor
                def _(pe):
                    for k in range(KT):
                        pe.wait_ge(squared, k + 1)
                        last = nc.tensor.matmul(ps[:, 0, 0:S], mat("ones"), sq[:, k, :], start=(k == 0),
                                                stop=(k == KT - 1))
                    last.then_inc(summed, 1)

                @block.vector
                def _(dve):
                    n = counter()
                    dve.wait_ge(summed, 1)
                    nc.vector.tensor_scalar(rstd[:, :], ps[:, 0, 0:S], 1.0 / D, NORM_EPS, ALU.mult,
                                            ALU.add).then_inc(scaled, 1)
                    dve.wait_ge(root, 1)
                    nc.vector.reciprocal(rstd[:, :], rstd[:, :]).then_inc(v, 1)
                    dve.wait_ge(v, n())
                    for k in range(KT):
                        nc.vector.scalar_tensor_tensor(hT[:, k, :], xT[:, k, :], gain(k), rstd[:, :], ALU.mult,
                                                       ALU.mult).then_inc(v, n.one())
                    if shift:
                        for k in range(KT):
                            dve.wait_ge(v, k + 2)
                            nc.vector.tensor_scalar(hT[:, k, :], hT[:, k, :], shift(k), None, ALU.add)

        def mean_square(pe, squared, summed):
            for k in range(KT):
                pe.wait_ge(squared, k + 1)
                last = nc.tensor.matmul(ps[:, 3, 0:S], mat("ones"), sq[:, k, :], start=(k == 0), stop=(k == KT - 1))
            last.then_inc(summed, 1)

        def take_rstd(dve, summed, scaled, root, inverted):
            dve.wait_ge(summed, 1)
            nc.vector.tensor_scalar(rstd[:, :], ps[:, 3, 0:S], 1.0 / D, NORM_EPS, ALU.mult, ALU.add).then_inc(scaled, 1)
            dve.wait_ge(root, 1)
            nc.vector.reciprocal(rstd[:, :], rstd[:, :]).then_inc(inverted, 1)
            dve.wait_ge(inverted, 1)

        def project(count, src, evacuate, tok_count=0, tok_evacuate=None, gain=None):
            with stage() as (block, (bank_free, src_high, src_low, squared, summed, scaled, root, inverted, *_)):
                first = take(tok_count + count)
                total = tok_count + count
                splits = min(total, TOTAL - AHEAD - first)

                def bank(i):
                    return i - tok_count + tok_count // 2

                @block.sync
                def _(sp):
                    refill(sp, first, total)

                @block.scalar
                def _(act):
                    split_high(act, src, gain, src_high)
                    if gain:
                        for k in range(KT):
                            nc.scalar.activation(sq[:, k, :], src[:, k, :], ACT.Square).then_inc(squared, 1)
                        high(act, first + AHEAD)
                        act.wait_ge(scaled, 1)
                        nc.scalar.activation(rstd[:, :], rstd[:, :], ACT.Sqrt).then_inc(root, 1)
                    else:
                        high(act, first + AHEAD)
                    begin = 1
                    turns = (splits - begin) // RING
                    if turns >= 2:
                        with act.Fori(0, turns) as g:
                            for u in range(RING):
                                high(act, first + AHEAD + begin + u, g)
                    else:
                        turns = 0
                    for i in range(begin + turns * RING, splits):
                        high(act, first + AHEAD + i)

                @block.tensor
                def _(pe):
                    for i in range(tok_count):
                        pe.wait_ge(tiles_freed, first + i + 1)
                        if i % 2 == 0:
                            pe.wait_ge(bank_free, i // 2 + 1)
                        for k in range(KT // 2):
                            src_k = i % 2 * (KT // 2) + k
                            if i < 2:
                                pe.wait_ge(src_low, src_k + 1)
                            for t in range(TT):
                                begins, ends = i % 2 == 0 and k == 0, i % 2 == 1 and k == KT // 2 - 1
                                cols = slice(t * P, (t + 1) * P)
                                last = product(ps[:, i // 2 % 2, t * S:(t + 1) * S], first + i, k,
                                               (srch[:, src_k, cols], srcl[:, src_k, cols]), begins and t == 0, ends,
                                               token_major=True)
                        last.then_inc(tiles_used, 1)

                    def tile(i, turns=0):
                        b = bank(i)
                        pe.wait_ge(tiles_freed, turns * RING + (first + i + 1))
                        pe.wait_ge(bank_free, turns * RING + (b + 1))
                        for k in range(KT):
                            if i == 0:
                                pe.wait_ge(src_low, k + 1)
                            last = product(ps[:, b % 2, 0:S], first + i, k, (srch[:, k, :], srcl[:, k, :]), k == 0,
                                           k == KT - 1)
                        last.then_inc(tiles_used, 1)
                    begin = tok_count
                    if gain:
                        tile(0)
                        mean_square(pe, squared, summed)
                        begin = 1
                    turns = (total - begin) // RING
                    if turns >= 2:
                        with pe.Fori(0, turns) as g:
                            for u in range(RING):
                                tile(begin + u, g)
                    else:
                        turns = 0
                    for i in range(begin + turns * RING, total):
                        tile(i)

                @block.vector
                def _(dve):
                    dve.sem_inc(bank_free, 2)
                    split_low(dve, src, gain, src_high, src_low)
                    if gain:
                        low(dve, first + AHEAD)
                        take_rstd(dve, summed, scaled, root, inverted)

                    def out(i, turns=0, at=None):
                        dve.wait_ge(tiles_used, turns * RING + (first + i - T_ADA + 1))
                        evacuate((i if at is None else at) - tok_count, ps[:, bank(i) % 2, 0:S]).then_inc(bank_free, 1)
                    for i in range(tok_count):
                        low(dve, first + AHEAD + i)
                        if i % 2:
                            dve.wait_ge(tiles_used, first + i - T_ADA + 1)
                            tok_evacuate(i // 2, ps[:, i // 2 % 2, :].rearrange("p (t f) -> p t f", t=TT)
                                         ).then_inc(bank_free, 1)
                    begin = tok_count
                    if gain:
                        out(0)
                        begin = 1
                    turns = (splits - begin) // RING
                    if turns >= 2:
                        with dve.Fori(0, turns) as g:
                            for u in range(RING):
                                low(dve, first + AHEAD + begin + u, g)
                                out(begin + u, g, g * RING + (begin + u))
                    else:
                        turns = 0
                    for i in range(begin + turns * RING, total):
                        if i < splits:
                            low(dve, first + AHEAD + i)
                        out(i)

        def one(tensor, i):
            return tensor[:, bass.ds(i, 1), :].rearrange("p a t -> p (a t)")

        def swiglu(gain, aside=None):
            with ExitStack() as tmp, stage() as (block, (src_high, src_low, squared, summed, scaled, root, inverted,
                                                         gate_ready, silu_done, up_ready, hid_ready, hid_high, act_ready,
                                                         *_)):
                tag = stream[0]
                gt, up, hid = (sb(f"{n}{tag}", [P, 2, S], where=tmp) for n in ("gt", "up", "hid"))
                hidh, hidl = (sb(f"{n}{tag}", [P, 2, S], F32R, where=tmp) for n in ("hidh", "hidl"))
                first = take(T_FFN)
                ACC = 4
                splits = min(T_FFN, TOTAL - AHEAD - first) + AHEAD

                def used(at):
                    return first - T_ADA + at + 1

                @block.sync
                def _(sp):
                    refill(sp, first, T_FFN)
                    if aside:
                        aside["sync"](sp)

                if aside:
                    @block.gpsimd
                    def _(pool):
                        aside["gpsimd"](pool)

                @block.tensor
                def _(pe):
                    def gate_up(j, at, turns=0):
                        if j >= 2:
                            pe.wait_ge(up_ready, turns * 2 + (j - 1))
                        for q in range(2):
                            pe.wait_ge(tiles_freed, turns * RING + (first + at + q + 1))
                            for k in range(KT):
                                if j == 0 and q == 0:
                                    pe.wait_ge(src_low, k + 1)
                                last = product(ps[:, j % 2, q * S:(q + 1) * S], first + at + q, k,
                                               (srch[:, k, :], srcl[:, k, :]), k == 0, k == KT - 1)
                            last.then_inc(tiles_used, 1)

                    def down(j, at, turns=0, begin=False, end=False):
                        pe.wait_ge(act_ready, turns * 2 + (j + 1))
                        pe.wait_ge(tiles_freed, turns * RING + (first + at + 1))
                        for d in range(KT):
                            last = product(ps[:, ACC + d // 2, d % 2 * S:(d % 2 + 1) * S], first + at, d,
                                           (hidh[:, j % 2, :], hidl[:, j % 2, :]), begin and d % 2 == 0, end)
                        last.then_inc(tiles_used, 1)

                    gate_up(0, 0)
                    mean_square(pe, squared, summed)
                    gate_up(1, 2)
                    down(0, 4, begin=True)
                    gate_up(2, 5)
                    down(1, 7)
                    with pe.Fori(0, FJ // 2 - 2) as g:
                        gate_up(3, 8, g)
                        down(2, 10, g)
                        gate_up(4, 11, g)
                        down(3, 13, g)
                    gate_up(FJ - 1, T_FFN - 4)
                    down(FJ - 2, T_FFN - 2)
                    down(FJ - 1, T_FFN - 1, end=True)

                def hidden_tiles(eng, step):
                    step(0)
                    step(1)
                    with eng.Fori(0, FJ // 2 - 2) as g:
                        step(2, g)
                        step(3, g)
                    step(FJ - 2)
                    step(FJ - 1)

                @block.scalar
                def _(act):
                    split_high(act, xT, gain, src_high)
                    for k in range(KT):
                        nc.scalar.activation(sq[:, k, :], xT[:, k, :], ACT.Square).then_inc(squared, 1)
                    high(act, first + AHEAD)
                    if aside:
                        aside["scalar_first"](act)
                    act.wait_ge(scaled, 1)
                    nc.scalar.activation(rstd[:, :], rstd[:, :], ACT.Sqrt).then_inc(root, 1)

                    def step(j, turns=0):
                        def weight(at):
                            if at < splits:
                                high(act, first + at, turns)
                        weight(3 * j + 3)
                        act.wait_ge(gate_ready, turns * 2 + (j + 1))
                        nc.scalar.activation(gt[:, j % 2, :], gt[:, j % 2, :], ACT.Silu).then_inc(silu_done, 1)
                        act.wait_ge(hid_ready, turns * 2 + (j + 1))
                        if j >= 2:
                            act.wait_ge(tiles_used, turns * RING + used(3 * (j - 2) + 4))
                        nc.scalar.activation(hidh[:, j % 2, :], hid[:, j % 2, :], ACT.Copy).then_inc(hid_high, 1)
                        weight(3 * j + 4)
                        weight(3 * j + 5)
                    hidden_tiles(act, step)
                    if aside:
                        aside["scalar"](act)

                @block.vector
                def _(dve):
                    split_low(dve, xT, gain, src_high, src_low)
                    low(dve, first + AHEAD)
                    take_rstd(dve, summed, scaled, root, inverted)

                    def step(j, turns=0):
                        def weight(at):
                            if at < splits:
                                low(dve, first + at, turns)
                        dve.wait_ge(tiles_used, turns * RING + used(1 if j == 0 else 3 * j))
                        nc.vector.tensor_tensor(gt[:, j % 2, :], ps[:, j % 2, 0:S], rstd[:, :], ALU.mult
                                                ).then_inc(gate_ready, 1)
                        nc.vector.tensor_tensor(up[:, j % 2, :], ps[:, j % 2, S:2 * S], rstd[:, :], ALU.mult
                                                ).then_inc(up_ready, 1)
                        weight(3 * j + 3)
                        dve.wait_ge(silu_done, turns * 2 + (j + 1))
                        dve.wait_ge(up_ready, turns * 2 + (j + 1))
                        nc.vector.tensor_tensor(hid[:, j % 2, :], up[:, j % 2, :], gt[:, j % 2, :], ALU.mult
                                                ).then_inc(hid_ready, 1)
                        dve.wait_ge(hid_high, turns * 2 + (j + 1))
                        nc.vector.tensor_tensor(hidl[:, j % 2, :], hid[:, j % 2, :], hidh[:, j % 2, :].bitcast(F32),
                                                ALU.subtract).then_inc(act_ready, 1)
                        weight(3 * j + 4)
                        weight(3 * j + 5)
                    hidden_tiles(dve, step)
                    if aside:
                        aside["vector"](dve)
                    dve.wait_ge(tiles_used, used(T_FFN - 1))
                    for b in range(4):
                        pair = xT[:, 2 * b:2 * b + 2, :].rearrange("p a t -> p (a t)")
                        nc.vector.scalar_tensor_tensor(pair, ps[:, ACC + b, :], 0.5, pair, ALU.mult, ALU.add)

        def attention(units, out, tag):
            U = len(units)
            WIDE = max(u["n"] for u in units)
            with ExitStack() as tmp, stage() as (block, (scored, shifted, maxed, exped, probs_ready, turned, turned_back,
                                                         out_ready, out_copied, v, a, *_)):
                DEEP = 3
                score_banks = (0, 1, 6)
                sc = sb(f"sc_{tag}", [P, DEEP, TT, WIDE], where=tmp)
                pT = sb(f"pT_{tag}", [P, 2, TT, S], where=tmp)
                stat = sb(f"stat_{tag}", [P, U, 6], where=tmp)

                done = [u for u in range(U) if u == U - 1 or units[u + 1]["j"] != units[u]["j"]]

                @block.tensor
                def _(pe):
                    for step in range(U + 3):
                        if step < U:
                            u = units[step]
                            if step >= DEEP:
                                pe.wait_ge(shifted, step - DEEP + 1)
                            for t in range(TT):
                                last = nc.tensor.matmul(ps[:, score_banks[step % DEEP], t * u["n"]:(t + 1) * u["n"]],
                                                        u["q"][:, t * P:(t + 1) * P], u["k"], start=True, stop=True)
                            last.then_inc(scored, 1)
                        if 2 <= step <= U + 1:
                            i = step - 2
                            u = units[i]
                            pe.wait_ge(probs_ready, i + 1)
                            if i >= 2:
                                pe.wait_ge(turned_back, i - 1)
                            for kt in range(len(u["v"])):
                                n = min(P, u["n"] - kt * P)
                                for t in range(TT):
                                    dst = ps[0:n, 2 + i % 2, kt * S + t * P:kt * S + (t + 1) * P]
                                    src = sc[:, i % DEEP, t, kt * P:kt * P + n]
                                    if n == P:
                                        last = nc.tensor.transpose(dst, src, mat("ident"))
                                    else:
                                        last = nc.tensor.matmul(dst, src, mat("ident"), start=True, stop=True)
                            last.then_inc(turned, 1)
                        if step >= 3:
                            i = step - 3
                            u = units[i]
                            pe.wait_ge(turned_back, i + 1)
                            fresh = i == 0 or (units[i - 1]["j"], units[i - 1]["po"]) != (u["j"], u["po"])
                            ends = i == U - 1 or (units[i + 1]["j"], units[i + 1]["po"]) != (u["j"], u["po"])
                            tiles = sum(x < i for x in done)
                            if tiles >= 2:
                                pe.wait_ge(out_copied, tiles - 1)
                            for kt, vv in enumerate(u["v"]):
                                n = min(P, u["n"] - kt * P)
                                last = nc.tensor.matmul(ps[u["po"]:u["po"] + HD, 4 + tiles % 2, 0:S], vv,
                                                        pT[0:n, i % 2, kt, :], start=(fresh and kt == 0),
                                                        stop=(ends and kt == len(u["v"]) - 1), skip_group_check=True)
                            if i in done:
                                last.then_inc(out_ready, 1)
                            else:
                                last.then_inc(a, 1)

                @block.vector
                def _(dve):
                    n = counter()
                    for i in range(U + 1):
                        if i < U:
                            u = units[i]
                            dve.wait_ge(scored, i + 1)
                            if i >= DEEP:
                                dve.wait_ge(turned, i - DEEP + 1)
                            w = u["n"]
                            nc.vector.scalar_tensor_tensor(sc[:, i % DEEP, :, 0:w],
                                                           ps[:, score_banks[i % DEEP], 0:TT * w].rearrange("p (t n) -> p t n", t=TT),
                                                           HD ** -0.5, u["bias"], ALU.mult, ALU.add).then_inc(shifted, 1)
                            dve.wait_ge(shifted, i + 1)
                            nc.vector.tensor_reduce(stat[:, i, 0:2], sc[:, i % DEEP, :, 0:w], AXX, ALU.max,
                                                    negate=True).then_inc(maxed, 1)
                        if i >= 1:
                            g = i - 1
                            dve.wait_ge(exped, TT * (g + 1))
                            nc.vector.reciprocal(stat[:, g, 4:6], stat[:, g, 2:4]).then_inc(v, 1)
                            dve.wait_ge(v, n())
                            if units[g].get("gate") is not None:
                                nc.vector.tensor_tensor(stat[:, g, 4:6], stat[:, g, 4:6], units[g]["gate"],
                                                        ALU.mult).then_inc(v, 1)
                                dve.wait_ge(v, n())
                            w = units[g]["n"]
                            nc.vector.tensor_tensor(sc[:, g % DEEP, :, 0:w], sc[:, g % DEEP, :, 0:w],
                                                    stat[:, g, 4:6].unsqueeze(2).broadcast_to([P, TT, w]),
                                                    ALU.mult).then_inc(probs_ready, 1)

                @block.scalar
                def _(act):
                    outs = 0
                    for i in range(U + 3):
                        if i < U:
                            act.wait_ge(maxed, i + 1)
                            for t in range(TT):
                                x = sc[:, i % DEEP, t, 0:units[i]["n"]]
                                nc.scalar.activation(x, x, ACT.Exp, bias=stat[:, i, t:t + 1],
                                                     accum_out=stat[:, i, 2 + t:3 + t]).then_inc(exped, 1)
                        if 2 <= i <= U + 1:
                            g = i - 2
                            act.wait_ge(turned, g + 1)
                            n = min(P, units[g]["n"])
                            w = len(units[g]["v"]) * S
                            if g >= 2:
                                ends = sum(x <= g - 2 for x in done)
                                act.wait_ge(out_ready, ends) if ends else None
                                act.wait_ge(a, g - 1 - ends) if g - 1 - ends else None
                            nc.scalar.activation(pT[0:n, g % 2, 0:len(units[g]["v"]), :].rearrange("p a b -> p (a b)"),
                                                 ps[0:n, 2 + g % 2, 0:w], ACT.Copy).then_inc(turned_back, 1)
                        if i >= 3 and i - 3 in done:
                            act.wait_ge(out_ready, outs + 1)
                            nc.scalar.activation(out[:, units[i - 3]["j"], :], ps[:, 4 + outs % 2, 0:S],
                                                 ACT.Copy).then_inc(out_copied, 1)
                            outs += 1

        mixer = ExitStack()
        zT = sb("zT", [P, T_IN, S], where=mixer)
        vtok = sb("vtok", [P, TT, 512], where=mixer)

        rms_norm(lambda k: gs[:, 0, k:k + 1], lambda k: mod[:, k:k + 1])

        def copy_in(i, src):
            return nc.vector.tensor_scalar(one(zT, i), src, 1.0, None, ALU.mult)

        project(T_IN, hT, copy_in, T_IN_TOK,
                lambda i, src: nc.vector.tensor_copy(vtok[:, :, i * S:(i + 1) * S], src))

        attn = ExitStack()
        bias = sb("bias", [P, NH, TT, S], where=attn)
        with ExitStack() as tmp, stage() as (block, (squared, summed, scaled, root, v, c0_ready, weighted, before_in,
                                                     both_in, *_)):
            root_qk = sb("root_qk", [P, NH * S], where=tmp)
            c0 = sb("c0", [P, 14], where=tmp)
            shiftd = sb("shiftd", [P, 14, S], where=tmp)
            qk = zT[:, 0:8, :].rearrange("p a t -> p (a t)")
            zr = zT[:, 8:22, :]

            @block.sync
            def _(sp):
                for h in range(NH):
                    sp.dma_start(bias[:, h, :, :], A["attn_bias"][h].rearrange("(t p) k -> p t k", p=P)
                                 ).then_inc(table_in, 16)
                    tables()
                sp.wait_ge(table_in, 16 * NH)

            @block.scalar
            def _(act):
                nc.scalar.activation(sq[:, :, :].rearrange("p a t -> p (a t)"), qk, ACT.Square).then_inc(squared, 1)
                act.wait_ge(c0_ready, 2)
                for i in range(14):
                    nc.scalar.activation(shiftd[:, i, :], zr[:, i, :], ACT.Copy, scale=c0[:, i:i + 1]
                                         ).then_inc(weighted, 1)
                act.wait_ge(scaled, 4)
                nc.scalar.activation(root_qk[:, :], root_qk[:, :], ACT.Sqrt).then_inc(root, 1)

            @block.tensor
            def _(pe):
                pe.wait_ge(squared, 1)
                for b in range(4):
                    nc.tensor.matmul(ps[:, b, :], mat("blockones"),
                                     sq[:, 2 * b:2 * b + 2, :].rearrange("p a t -> p (a t)"),
                                     start=True, stop=True).then_inc(summed, 1)

            @block.vector
            def _(dve):
                n = counter()
                nc.vector.tensor_tensor(c0[:, :], vec_all("mu_prev"), vec_all("mu_next"), ALU.add).then_inc(c0_ready, 1)
                dve.wait_ge(c0_ready, 1)
                nc.vector.tensor_scalar(c0[:, :], c0[:, :], -1.0, 1.0, ALU.mult, ALU.add).then_inc(c0_ready, 1)
                for i in range(14 + 2):
                    if i < 14:
                        dve.wait_ge(weighted, i + 1)
                        nc.vector.scalar_tensor_tensor(shiftd[:, i, 1:S], zr[:, i, 0:S - 1], vec("mu_prev", i),
                                                       shiftd[:, i, 1:S], ALU.mult, ALU.add).then_inc(before_in, 1)
                    if i >= 2:
                        k = i - 2
                        dve.wait_ge(before_in, k + 1)
                        nc.vector.scalar_tensor_tensor(shiftd[:, k, 0:S - 1], zr[:, k, 1:S], vec("mu_next", k),
                                                       shiftd[:, k, 0:S - 1], ALU.mult, ALU.add).then_inc(both_in, 1)
                for b in range(4):
                    dve.wait_ge(summed, b + 1)
                    nc.vector.tensor_scalar(root_qk[:, 512 * b:512 * b + 512], ps[:, b, :], 1.0 / HD, NORM_EPS,
                                            ALU.mult, ALU.add).then_inc(scaled, 1)
                dve.wait_ge(root, 1)
                nc.vector.reciprocal(root_qk[:, :], root_qk[:, :]).then_inc(v, 1)
                dve.wait_ge(v, n())
                for b, name in enumerate(("q_norm_g", "k_norm_g")):
                    cols = slice(1024 * b, 1024 * b + 1024)
                    nc.vector.scalar_tensor_tensor(qk[:, cols], qk[:, cols], vec(name), root_qk[:, cols], ALU.mult,
                                                   ALU.mult)

            @block.gpsimd
            def _(pool):
                for i in range(14):
                    pool.wait_ge(both_in, i + 1)
                    nc.gpsimd.tensor_copy(zr[:, i, :], shiftd[:, i, :])

        attention([dict(po=HD * (h % 2), j=h // 2, n=S, q=zT[HD * (h % 2):HD * (h % 2) + HD, h // 2, :],
                        k=zT[HD * (h % 2):HD * (h % 2) + HD, 4 + h // 2, :], bias=bias[:, h, :, :],
                        v=[vtok[:, t, h * HD:(h + 1) * HD] for t in range(TT)]) for h in range(NH)], mix, "dilated")
        attn.close()

        wkv = ExitStack()
        rT, kT, vT = zT[:, 8:12, :], zT[:, 12:16, :], zT[:, 16:20, :]
        flat = "p a t -> p (a t)"
        alpha, beta, kappa, rho = (sb(n, [P, 2, 4, S], where=wkv) for n in ("alpha", "beta", "kappa", "rho"))
        gT = sb("gT", [P, 4, S], where=wkv)
        bonus = sb("bonus", [P, 4, S], where=wkv)
        ysum = sb("ysum", [P, 2, 512], where=wkv)
        carry = sb("carry", [P, 2, 4], where=wkv)
        feat = ExitStack()
        lora = sb("lora", [P, 2, 512], where=feat)
        g_up = sb("g_up", [P, 512], where=feat)
        logw = sb("logw", [P, 2, 4, S], where=feat)
        aa = sb("aa", [P, 2, 4, S], where=feat)
        kk = sb("kk", [P, 4, S], where=feat)
        omka = sb("omka", [P, 4], where=feat)
        with stage() as (block, (ups_in, squashed, raised, sig_done, v, kk_scaled, summed, *_)):
            @block.sync
            def _(sp):
                sp.dma_start(lora[:, :, :], A["lora_up"]).then_inc(ups_in, 16)
                sp.dma_start(g_up[:, :], A["g_up"]).then_inc(ups_in, 16)

            @block.scalar
            def _(act):
                nc.scalar.activation(zT[0:64, 20, :], zT[0:64, 20, :], ACT.Tanh).then_inc(squashed, 1)
                nc.scalar.activation(zT[:, 21, :], zT[:, 21, :], ACT.Sigmoid).then_inc(squashed, 1)
                for d in range(2):
                    act.wait_ge(raised, 8 * d + 8)
                    for j in range(4):
                        bank, col = 4 * d + j // 2, j % 2 * S
                        nc.scalar.activation(logw[:, d, j, :], ps[:, bank, col:col + S], ACT.Sigmoid,
                                             bias=vec("w_decay0", 4 * d + j)).then_inc(sig_done, 1)
                        nc.scalar.activation(aa[:, d, j, :], ps[:, bank + 2, col:col + S], ACT.Sigmoid,
                                             bias=vec("a_gate0", 4 * d + j)).then_inc(sig_done, 1)

            @block.tensor
            def _(pe):
                pe.wait_ge(ups_in, 32)
                pe.wait_ge(squashed, 2)
                for d in range(2):
                    for j in range(4):
                        bank, col = 4 * d + j // 2, j % 2 * S
                        nc.tensor.matmul(ps[:, bank, col:col + S], lora[0:64, d, j * P:(j + 1) * P], zT[0:64, 20, :],
                                         start=True, stop=True).then_inc(raised, 1)
                        nc.tensor.matmul(ps[:, bank + 2, col:col + S], lora[64:128, d, j * P:(j + 1) * P],
                                         zT[64:128, 20, :], start=True, stop=True).then_inc(raised, 1)

            @block.vector
            def _(dve):
                for j in range(4):
                    nc.vector.tensor_scalar(kk[:, j, :], kT[:, j, :], vec("k_k", j), None, ALU.mult).then_inc(v, 1)
                nc.vector.tensor_scalar(omka[:, :], vec_all("k_a"), -1.0, 1.0, ALU.mult, ALU.add)
                dve.wait_ge(v, 4)
                nc.vector.tensor_tensor(sq[:, 0:4, :], kk[:, :, :], kk[:, :, :], ALU.mult)
                dve.wait_ge(sig_done, 16)
                nc.vector.tensor_scalar(logw[:, :, :, :].rearrange("p d a t -> p (d a t)"),
                                        logw[:, :, :, :].rearrange("p d a t -> p (d a t)"),
                                        -float(np.exp(-0.5)), None, ALU.mult)

        with ExitStack() as tmp, stage() as (block, (summed, gated, kk_ready, exp_in, exps, v, w, kb_ready, bonus_sum,
                                                     g_done, kk_root, carry_in, *_)):
            cum = zT[:, 0:8, :].rearrange("p (d a) t -> p d a t", d=2)
            inv2 = hT[:, :, :].rearrange("p (d a) t -> p d a t", d=2)
            inv = sq[:, 0:4, :]
            kd = vtok[:, :, :].rearrange("p a (b t) -> p (a b) t", t=S)
            off = logw[:, :, :, :]
            mid = sb("mid", [P, 2, 8], where=tmp)

            @block.tensor
            def _(pe):
                for b in range(2):
                    nc.tensor.matmul(ps[:, b, :], mat("blockones"), sq[:, 2 * b:2 * b + 2, :].rearrange(flat),
                                     start=True, stop=True).then_inc(summed, 1)
                for j in range(4):
                    nc.tensor.matmul(ps[:, 2 + j // 2, j % 2 * S:j % 2 * S + S], g_up[:, j * P:(j + 1) * P],
                                     zT[:, 21, :], start=True, stop=True).then_inc(gated, 1)
                pe.wait_ge(kb_ready, 1)
                for b in range(2):
                    nc.tensor.matmul(ps[:, 4 + b, :], mat("blockones"), sq[:, 4 + 2 * b:6 + 2 * b, :].rearrange(flat),
                                     start=True, stop=True).then_inc(bonus_sum, 1)

            @block.scalar
            def _(act):
                act.wait_ge(kk_ready, 2)
                nc.scalar.activation(inv[:, :, :], inv[:, :, :], ACT.Sqrt).then_inc(kk_root, 1)
                act.wait_ge(gated, 4)
                nc.scalar.activation(gT[:, :, :].rearrange(flat), ps[:, 2:4, :].rearrange("p b n -> p (b n)"),
                                     ACT.Copy).then_inc(g_done, 1)
                for d in range(2):
                    act.wait_ge(exp_in, d + 1)
                    upto, sign = (cum, 1.0) if d == 0 else (off, -1.0)
                    before = off if d == 0 else cum
                    nc.scalar.activation(rho[:, d], upto[:, d], ACT.Exp).then_inc(exps, 1)
                    nc.scalar.activation(inv2[:, d], upto[:, d], ACT.Exp, scale=-1.0).then_inc(exps, 1)
                    nc.scalar.activation(alpha[:, d], before[:, d], ACT.Exp, scale=sign).then_inc(exps, 1)
                act.wait_ge(carry_in, 2)
                nc.scalar.activation(carry[:, :, :], carry[:, :, :], ACT.Exp)

            @block.vector
            def _(dve):
                n = counter()
                for b in range(2):
                    dve.wait_ge(summed, b + 1)
                    nc.vector.tensor_scalar(inv[:, 2 * b:2 * b + 2, :].rearrange(flat), ps[:, b, :], 1e-12, None,
                                            ALU.max).then_inc(kk_ready, 1)
                for d in range(2):
                    for j in range(4):
                        for c in range(2):
                            cols = slice(c * P, c * P + P)
                            nc.vector.tensor_tensor_scan(cum[:, d, j, cols], mat("ones"), logw[:, d, j, cols], 0.0,
                                                         ALU.mult, ALU.add).then_inc(v, n.one())
                    dve.wait_ge(v, n.now)
                    chunks = cum[:, d].rearrange("p a (c t) -> p (a c) t", t=P)
                    nc.vector.tensor_copy(mid[:, d, :], chunks[:, :, P // 2 - 1:P // 2].rearrange("p a b -> p (a b)")
                                          ).then_inc(v, n.one())
                    dve.wait_ge(v, n.now)
                    nc.vector.tensor_tensor(chunks, chunks, mid[:, d, :].unsqueeze(2).broadcast_to([P, 8, P]),
                                            ALU.subtract).then_inc(v, n.one())
                    dve.wait_ge(v, n.now)
                    pair = (cum[:, d], logw[:, d]) if d == 0 else (logw[:, d], cum[:, d])
                    nc.vector.tensor_tensor(off[:, d], pair[0], pair[1], ALU.subtract).then_inc(exp_in, 1)
                    dve.wait_ge(exp_in, d + 1)
                    nc.vector.tensor_tensor(carry[:, d, :], cum[:, d, :, P - 1:P].rearrange("p a b -> p (a b)"),
                                            off[:, d, :, P:P + 1].rearrange("p a b -> p (a b)"),
                                            ALU.subtract if d == 0 else ALU.add).then_inc(carry_in, 1)
                dve.wait_ge(kk_root, 1)
                nc.vector.reciprocal(inv[:, :, :], inv[:, :, :]).then_inc(v, n.one())
                dve.wait_ge(v, n.now)
                nc.vector.tensor_tensor(kk[:, :, :], kk[:, :, :], inv[:, :, :], ALU.mult).then_inc(v, n.one())
                dve.wait_ge(v, n.now)
                nc.vector.tensor_tensor(inv[:, :, :], aa[:, 0], aa[:, 1], ALU.add).then_inc(v, n.one())
                dve.wait_ge(v, n.now)
                nc.vector.tensor_scalar(inv[:, :, :].rearrange(flat), inv[:, :, :].rearrange(flat), 0.5, None,
                                        ALU.mult).then_inc(v, n.one())
                dve.wait_ge(v, n.now)
                for j in range(4):
                    nc.vector.tensor_scalar(inv[:, j, :], inv[:, j, :], vec("k_a", j), omka[:, j:j + 1], ALU.mult,
                                            ALU.add).then_inc(v, n.one())
                dve.wait_ge(v, n.now)
                nc.vector.tensor_tensor(inv[:, :, :], inv[:, :, :], kT, ALU.mult).then_inc(v, n.one())
                dve.wait_ge(v, n.now)
                for j in range(4):
                    nc.vector.scalar_tensor_tensor(sq[:, 4 + j, :], inv[:, j, :], vec("r_k", j), rT[:, j, :],
                                                   ALU.mult, ALU.mult).then_inc(kb_ready if j == 3 else w, 1)
                dve.wait_ge(kb_ready, 1)
                dve.wait_ge(w, 3)
                for d in range(2):
                    dve.wait_ge(v, n.now)
                    for j in range(4):
                        nc.vector.tensor_scalar(kd[:, j, :], aa[:, d, j, :], vec("k_a", j), omka[:, j:j + 1],
                                                ALU.mult, ALU.add).then_inc(v, n.one())
                    nc.vector.tensor_tensor(beta[:, d], kk[:, :, :], aa[:, d], ALU.mult).then_inc(v, n.one())
                    dve.wait_ge(v, n.now)
                    nc.vector.tensor_tensor(kd[:, :, :], kd[:, :, :], kT, ALU.mult).then_inc(v, n.one())
                    dve.wait_ge(exps, 3 * d + 3)
                    dve.wait_ge(v, n.now)
                    nc.vector.tensor_tensor(kappa[:, d], kd[:, :, :], inv2[:, d], ALU.mult).then_inc(v, n.one())
                    nc.vector.tensor_tensor(beta[:, d], beta[:, d], inv2[:, d], ALU.mult).then_inc(v, n.one())
                    nc.vector.tensor_tensor(alpha[:, d], alpha[:, d], kk[:, :, :], ALU.mult).then_inc(v, n.one())
                    nc.vector.tensor_tensor(rho[:, d], rho[:, d], rT, ALU.mult).then_inc(v, n.one())
                dve.wait_ge(bonus_sum, 2)
                for b in range(2):
                    nc.vector.tensor_tensor(bonus[:, 2 * b:2 * b + 2, :].rearrange(flat), ps[:, 4 + b, :],
                                            vT[:, 2 * b:2 * b + 2, :].rearrange(flat), ALU.mult)
        feat.close()

        solve = ExitStack()
        v_tok = vtok
        bk_tok = sb("bk_tok", [P, 2, 2, 512], where=solve)
        with stage() as (block, (turned, *_)):
            jobs = [(v_tok[:, c, :], vT, c) for c in range(2)]
            jobs += [(bk_tok[:, d, i, :], (beta, kappa)[i][:, d], d) for d in range(2) for i in range(2)]

            @block.tensor
            def _(pe):
                for n, (_, src, c) in enumerate(jobs):
                    for j in range(4):
                        last = nc.tensor.transpose(ps[:, n, j * P:(j + 1) * P], src[:, j, c * P:(c + 1) * P],
                                                   mat("ident"))
                    last.then_inc(turned, 1)

            @block.vector
            def _(dve):
                for n, (dst, _, _) in enumerate(jobs):
                    if n % 2 == 0:
                        dve.wait_ge(turned, n + 1)
                        nc.vector.tensor_copy(dst, ps[:, n, :])

            @block.scalar
            def _(act):
                for n, (dst, _, _) in enumerate(jobs):
                    if n % 2:
                        act.wait_ge(turned, n + 1)
                        nc.scalar.activation(dst, ps[:, n, :], ACT.Copy)

        states = [sb(f"state{d}", [P, 4, HD], where=solve) for d in range(2)]
        def matrices(tensor, n):
            return tensor[:, 4 * n:4 * n + 4, :].rearrange("p a (b t) -> p (a b) t", t=P)
        LT, X, XT, Y = matrices(hT, 0), matrices(hT, 1), matrices(zT, 0), matrices(zT, 1)
        LmT, MT, N1, N2 = matrices(zT, 2), matrices(zT, 3), matrices(sq, 0), matrices(sq, 1)
        G, SA = mix[:, 4:6, :].rearrange("p a t -> p (a t)"), mix[:, 6:8, :].rearrange("p a t -> p (a t)")
        heads = "p h t -> p (h t)"

        def all_heads(m):
            return mat(m).unsqueeze(1).broadcast_to([P, NH, P])

        def banks(b):
            return ps[:, b:b + 2, :].rearrange("p b (h t) -> p (b h) t", t=P)

        def place_of(h):
            return h % 2 * 4 + h // 2

        def rows(h):
            return slice(HD * (h % 2), HD * (h % 2) + HD)

        for first_chunk in (True, False):
            for d in range(2):
                c = d if first_chunk else 1 - d
                cols = slice(c * P, c * P + P)
                with stage() as (block, (products, masked, y_done, x_done, xt_done, x_ready, xt_ready, level_in,
                                         y_copied, g_ready, v, sa_ready, y_ready, state_ready)):
                    LEVELS = (2, 4, 8, 16, 32, 64)
                    half_of = [slice(0, 4), slice(4, 8)]

                    def updated(lv, half):
                        return max(1, 2 * lv + half)

                    @block.tensor
                    def _(pe):
                        def outer(bank, left, right, counted):
                            for h in range(NH):
                                last = nc.tensor.matmul(ps[:, bank + h % 2, h // 2 * P:h // 2 * P + P],
                                                        left[rows(h), d, h // 2, cols],
                                                        right[rows(h), d, h // 2, cols], start=True, stop=True)
                            last.then_inc(counted, 1)

                        def doubling(bank, half, left, right, counted):
                            for i in range(4):
                                last = nc.tensor.matmul(ps[:, bank + half, i * P:i * P + P], left[:, 4 * half + i, :],
                                                        right[:, 4 * half + i, :], start=True, stop=True)
                            last.then_inc(counted, 1)

                        outer(0, beta, alpha, products)
                        outer(2, alpha, beta, products)
                        outer(4, kappa, alpha, products)
                        outer(6, beta, rho, products)
                        for lv in range(6):
                            for half in range(2):
                                pe.wait_ge(level_in, 2 * lv + half + 1)
                                pe.wait_ge(x_ready, updated(lv, half))
                                doubling(0, half, LmT, X, y_done)
                            for half in range(2):
                                pe.wait_ge(y_copied, 2 * lv + half + 1)
                                pe.wait_ge(xt_ready, updated(lv, half))
                                if lv < 5:
                                    doubling(2, half, XT, Y, x_done)
                                if lv == 0:
                                    pe.wait_ge(masked, 3)
                                doubling(4, half, Y, XT, xt_done)
                            if lv == 0:
                                pe.wait_ge(masked, 4)
                                outer(6, kappa, rho, products)
                            if lv == 1:
                                pe.wait_ge(masked, 5)
                                for h in range(NH):
                                    dst = ps[:, 6 + h % 2, h // 2 * HD:(h // 2 + 1) * HD]
                                    if not first_chunk:
                                        nc.tensor.matmul(dst, alpha[rows(h), d, h // 2, cols],
                                                         states[d][rows(h), h // 2, :], start=True, stop=False)
                                    last = nc.tensor.matmul(dst, MT[:, place_of(h), :],
                                                            v_tok[:, c, h * HD:(h + 1) * HD], start=first_chunk,
                                                            stop=True)
                                last.then_inc(g_ready, 1)
                            if lv == 3:
                                pe.wait_ge(g_ready, 2)
                                for h in range(NH):
                                    dst = ps[:, 6 + h % 2, h // 2 * HD:(h // 2 + 1) * HD]
                                    begins = h // 2 == 0
                                    if not first_chunk:
                                        nc.tensor.matmul(dst, rho[rows(h), d, h // 2, cols],
                                                         states[d][rows(h), h // 2, :], start=begins, stop=False,
                                                         skip_group_check=True)
                                    nc.tensor.matmul(dst, N2[:, place_of(h), :], v_tok[:, c, h * HD:(h + 1) * HD],
                                                     start=begins and first_chunk, stop=False, skip_group_check=True)
                        for half in range(2):
                            pe.wait_ge(xt_ready, updated(6, half))
                            for i in range(4):
                                at = 4 * half + i
                                last = nc.tensor.matmul(ps[:, 2 + half, i * HD:(i + 1) * HD], XT[:, at, :],
                                                        G[:, at * HD:(at + 1) * HD], start=True, stop=True)
                            last.then_inc(products, 1)
                        for half in range(2):
                            pe.wait_ge(sa_ready, half + 1)
                            for i in range(4):
                                at = 4 * half + i
                                last = nc.tensor.matmul(ps[:, 6 + half, i * HD:(i + 1) * HD], N1[:, at, :],
                                                        SA[:, at * HD:(at + 1) * HD], start=False, stop=True,
                                                        skip_group_check=True)
                            last.then_inc(y_ready, 1)
                        if first_chunk:
                            for h in range(NH):
                                hv = slice(h * HD, (h + 1) * HD)
                                at = place_of(h)
                                dst = ps[rows(h), 1, h // 2 * HD:(h // 2 + 1) * HD]
                                nc.tensor.matmul(dst, bk_tok[:, d, 0, hv], SA[:, at * HD:(at + 1) * HD], start=True,
                                                 stop=False)
                                last = nc.tensor.matmul(dst, bk_tok[:, d, 1, hv], v_tok[:, c, hv], start=False,
                                                        stop=True)
                            last.then_inc(state_ready, 1)

                    @block.scalar
                    def _(act):
                        for lv in range(6):
                            for half in range(2):
                                act.wait_ge(y_done, 2 * lv + half + 1)
                                if lv:
                                    act.wait_ge(xt_done, 2 * (lv - 1) + half + 1)
                                nc.scalar.activation(Y[:, half_of[half], :],
                                                     ps[:, half, :].rearrange("p (h t) -> p h t", t=P),
                                                     ACT.Copy).then_inc(y_copied, 1)
                            if lv == 2:
                                act.wait_ge(g_ready, 1)
                                nc.scalar.activation(G[:, :].rearrange("p (a n) -> p a n", a=2), ps[:, 6:8, 0:S],
                                                     ACT.Copy).then_inc(g_ready, 1)

                    @block.gpsimd
                    def _(pool):
                        pool.wait_ge(masked, 1)
                        for lv, b in enumerate(LEVELS):
                            for half in range(2):
                                if lv:
                                    pool.wait_ge(y_done, 2 * (lv - 1) + half + 1)
                                nc.gpsimd.tensor_tensor(LmT[:, half_of[half], :], LT[:, half_of[half], :],
                                                        mat(f"level{d}_{b}").unsqueeze(1).broadcast_to([P, 4, P]),
                                                        ALU.mult).then_inc(level_in, 1)

                    @block.vector
                    def _(dve):
                        n = counter()

                        def masked_product(dst, bank, mask, count):
                            dve.wait_ge(products, count)
                            nc.vector.tensor_tensor(dst[:, :, :], banks(bank), all_heads(mask), ALU.mult
                                                    ).then_inc(masked, 1)
                        masked_product(LT, 0, f"strict{d}", 1)
                        masked_product(X, 2, f"level_row{d}", 2)
                        dve.wait_ge(masked, 1)
                        nc.vector.tensor_tensor(XT[:, :, :], LT[:, :, :], all_heads(f"level{d}_1"),
                                                ALU.mult).then_inc(v, n.one())
                        dve.wait_ge(masked, 2)
                        nc.vector.tensor_tensor(X[:, :, :], all_heads("ident"), X[:, :, :],
                                                ALU.subtract).then_inc(x_ready, 1)
                        dve.wait_ge(v, n.now)
                        nc.vector.tensor_tensor(XT[:, :, :], all_heads("ident"), XT[:, :, :],
                                                ALU.subtract).then_inc(xt_ready, 1)
                        masked_product(MT, 4, f"strict{d}", 3)
                        for lv in range(6):
                            for half in range(2):
                                for matrix, bank, done, ready in ((X, 2, x_done, x_ready), (XT, 4, xt_done, xt_ready)):
                                    if matrix is X and lv == 5:
                                        continue
                                    dve.wait_ge(done, 2 * lv + half + 1)
                                    dve.wait_ge(ready, updated(lv, half))
                                    nc.vector.tensor_tensor(matrix[:, half_of[half], :], matrix[:, half_of[half], :],
                                                            ps[:, bank + half, :].rearrange("p (h t) -> p h t", t=P),
                                                            ALU.subtract).then_inc(ready, 1)
                            if lv == 0:
                                masked_product(N1, 6, f"upto{d}", 4)
                            if lv == 1:
                                masked_product(N2, 6, f"upto{d}", 5)
                        for half in range(2):
                            dve.wait_ge(products, 6 + half)
                            nc.vector.tensor_scalar(SA[:, half * S:(half + 1) * S], ps[:, 2 + half, 0:S], -1.0, None,
                                                    ALU.mult).then_inc(sa_ready, 1)
                        for odd in range(2):
                            dve.wait_ge(y_ready, odd + 1)
                            mine = ysum[:, c, :].rearrange("p (j q e) -> p j q e", q=2, e=HD)[:, :, odd, :]
                            new = ps[:, 6 + odd, 0:S].rearrange("p (j e) -> p j e", e=HD)
                            if first_chunk:
                                nc.vector.tensor_copy(mine, new)
                            else:
                                nc.vector.tensor_tensor(mine, mine, new, ALU.add)
                        if first_chunk:
                            dve.wait_ge(state_ready, 1)
                            for j in range(4):
                                nc.vector.tensor_scalar(states[d][:, j, :], ps[:, 1, j * HD:(j + 1) * HD],
                                                        carry[:, d, j:j + 1], None, ALU.mult)
        solve.close()

        with ExitStack() as tmp, stage() as (block, (v, centred, squared, root, normed, turned, root_in, *_)):
            st = sb("st", [P, 2, 16], where=tmp)
            y = ysum[:, :, :].rearrange("p c (h e) -> p (c h) e", e=HD)
            ysq = sq[:, 0:4, :].rearrange("p a t -> p (a t)").rearrange("p (h e) -> p h e", e=HD)

            @block.scalar
            def _(act):
                act.wait_ge(centred, 1)
                nc.scalar.activation(ysq, y, ACT.Square).then_inc(squared, 1)
                act.wait_ge(root_in, 1)
                nc.scalar.activation(st[:, 1, :], st[:, 1, :], ACT.Sqrt).then_inc(root, 1)

            @block.vector
            def _(dve):
                n = counter()
                nc.vector.tensor_reduce(st[:, 0, :], y, AXX, ALU.add).then_inc(v, n.one())
                dve.wait_ge(v, n.now)
                nc.vector.tensor_scalar(st[:, 0, :], st[:, 0, :], 1.0 / HD, None, ALU.mult).then_inc(v, n.one())
                dve.wait_ge(v, n.now)
                nc.vector.tensor_tensor(y, y, st[:, 0, :].unsqueeze(2).broadcast_to([P, 16, HD]),
                                        ALU.subtract).then_inc(centred, 1)
                dve.wait_ge(squared, 1)
                nc.vector.tensor_reduce(st[:, 1, :], ysq, AXX, ALU.add).then_inc(v, n.one())
                dve.wait_ge(v, n.now)
                nc.vector.tensor_scalar(st[:, 1, :], st[:, 1, :], 1.0 / HD, 64e-5, ALU.mult,
                                        ALU.add).then_inc(root_in, 1)
                dve.wait_ge(root, 1)
                nc.vector.reciprocal(st[:, 1, :], st[:, 1, :]).then_inc(v, n.one())
                dve.wait_ge(v, n.now)
                nc.vector.tensor_tensor(y, y, st[:, 1, :].unsqueeze(2).broadcast_to([P, 16, HD]),
                                        ALU.mult).then_inc(normed, 1)
                for j in range(4):
                    dve.wait_ge(turned, j + 1)
                    nc.vector.tensor_scalar(mix[:, 4 + j, :], ps[:, j, 0:S], vec("lnx_g", j), vec("lnx_b", j),
                                            ALU.mult, ALU.add).then_inc(v, n.one())
                dve.wait_ge(v, n.now)
                nc.vector.tensor_tensor(mix[:, 4:8, :], mix[:, 4:8, :], bonus[:, :, :], ALU.add).then_inc(v, n.one())
                dve.wait_ge(v, n.now)
                nc.vector.tensor_tensor(mix[:, 4:8, :], mix[:, 4:8, :], gT[:, :, :], ALU.mult)

            @block.tensor
            def _(pe):
                pe.wait_ge(normed, 1)
                for j in range(4):
                    for c in range(2):
                        last = nc.tensor.transpose(ps[:, j, c * P:(c + 1) * P], ysum[:, c, j * P:(j + 1) * P],
                                                   mat("ident"))
                    last.then_inc(turned, 1)
        wkv.close()
        mixer.close()

        def add_gated(col):
            return lambda i, src: nc.vector.scalar_tensor_tensor(one(xT, i), src, mod[:, col:col + 8][:, bass.ds(i, 1)],
                                                                 one(xT, i), ALU.mult, ALU.add)

        project(T_OUT, mix, add_gated(16))
        rms_norm(lambda k: gs[:, 1, k:k + 1], lambda k: mod[:, 24 + k:25 + k])

        peer = ExitStack()
        h_tok = sb("h_tok", [P, TT, D], where=peer)
        experts = sb("experts", [P, TT, SLOTS], U32, where=peer)
        gates = sb("gates", [P, TT, SLOTS], where=peer)
        best = sb("best", [P, TT, NH, TOPK], where=peer)
        digits = sb("digits", [P, TOPK], where=peer)
        scores = [free[:, :, :].rearrange("p k t -> p (k t)").rearrange("p (s h n) -> p s h n", s=2, h=NH)
                  for free in (mix, sq)]
        with ExitStack() as tmp:
            queries = sb("queries", [P, T_QUERY, S], where=tmp)
            subkeys = sb("subkeys", [P, 2, NE], where=tmp)
            project(T_QUERY, hT, lambda i, src: nc.vector.tensor_scalar(one(queries, i), src, 1.0, None, ALU.mult))
            with stage() as (block, (keys_in, scored, turned, bank_free, *_)):
                @block.sync
                def _(sp):
                    sp.dma_start(subkeys[:, :, :], A["subkeys"]).then_inc(keys_in, 16)

                @block.tensor
                def _(pe):
                    pe.wait_ge(keys_in, 16)
                    for t in range(TT):
                        for half in range(2):
                            if t:
                                pe.wait_ge(bank_free, half + 1)
                            for h in range(NH):
                                last = nc.tensor.matmul(ps[:, 2 * half + h // 4, h % 4 * P:h % 4 * P + P],
                                                        queries[:, 2 * h + half, t * P:(t + 1) * P],
                                                        subkeys[:, half, :], start=True, stop=True)
                            last.then_inc(scored, 1)
                    for t in range(TT):
                        for k in range(KT):
                            last = nc.tensor.transpose(ps[:, 4 + 2 * t + k // 4, k % 4 * P:k % 4 * P + P],
                                                       hT[:, k, t * P:(t + 1) * P], mat("ident"))
                        last.then_inc(turned, 1)

                @block.vector
                def _(dve):
                    for n in range(2 * TT):
                        dve.wait_ge(scored, n + 1)
                        b = n % 2 * 2
                        nc.vector.tensor_copy(scores[n // 2][:, n % 2, :, :].rearrange(heads),
                                              ps[:, b:b + 2, :].rearrange("p b n -> p (b n)")).then_inc(bank_free, 1)

                @block.scalar
                def _(act):
                    for t in range(TT):
                        act.wait_ge(turned, t + 1)
                        nc.scalar.activation(h_tok[:, t, :], ps[:, 4 + 2 * t:6 + 2 * t, :].rearrange("p b n -> p (b n)"),
                                             ACT.Copy)

        def choice_buffers(tag, heads, where):
            b = {n: sb(f"{n}_{tag}", shape, dt, where=where) for n, shape, dt in (
                ("top", [P, 2, heads, TOPK], F32), ("at", [P, 2, heads, TOPK], U32), ("atf", [P, 2, heads, TOPK], F32),
                ("sums", [P, heads, TOPK, TOPK], F32), ("hot", [P, 2, heads, TOPK, TOPK], F32),
                ("place", [P, heads, TOPK], U32), ("half", [P, 2, heads, TOPK], U32),
                ("halff", [P, 2, heads, TOPK], F32), ("found", [P, 2, heads, TOPK], F32))}
            b["heads"] = heads
            return b

        def choice_steps(heads):
            return 5 * 2 * heads + 1 + 5 * heads + 12

        def top16(done, n, units, hold):
            def step(first, op):
                for u in range(len(units)):
                    hold(n.now - u if first else n.now - len(units) + 1)
                    op(*units[u]).then_inc(done, n.one())
            step(True, lambda values, out, places: nc.vector.max(out[:, 0:8], values))
            step(False, lambda values, out, places: nc.vector.max_index(places[:, 0:8], out[:, 0:8], values))
            step(False, lambda values, out, places: nc.vector.match_replace(values, out[:, 0:8], values, -3e38))
            step(False, lambda values, out, places: nc.vector.max(out[:, 8:16], values))
            step(False, lambda values, out, places: nc.vector.max_index(places[:, 8:16], out[:, 8:16], values))

        def choose(dve, done, n, before, b, scores_of, best_of, expert_slots, hold, meanwhile):
            H = b["heads"]
            four = [P, H, TOPK, TOPK]
            top16(done, n, [(scores_of(half, h), b["top"][:, half, h, :], b["at"][:, half, h, :])
                            for half in range(2) for h in range(H)], hold)
            dve.wait_ge(done, before + n.now)
            nc.vector.tensor_tensor(b["sums"][:, :, :, :], b["top"][:, 0].unsqueeze(3).broadcast_to(four),
                                    b["top"][:, 1].unsqueeze(2).broadcast_to(four), ALU.add).then_inc(done, n.one())
            top16(done, n, [(b["sums"][:, h].rearrange("p a b -> p (a b)"), best_of(h), b["place"][:, h, :])
                            for h in range(H)], hold)
            nc.vector.tensor_copy(b["atf"][:, :, :, :], b["at"][:, :, :, :]).then_inc(done, n.one())
            meanwhile()
            dve.wait_ge(done, before + (n.now - 1))
            nc.vector.tensor_scalar(b["half"][:, 0], b["place"][:, :, :], 4, None, ALU.logical_shift_right
                                    ).then_inc(done, n.one())
            nc.vector.tensor_scalar(b["half"][:, 1], b["place"][:, :, :], 15, None, ALU.bitwise_and
                                    ).then_inc(done, n.one())
            meanwhile()
            for half in range(2):
                dve.wait_ge(done, before + (n.now - 1))
                nc.vector.tensor_copy(b["halff"][:, half], b["half"][:, half]).then_inc(done, n.one())
            meanwhile()
            for half in range(2):
                dve.wait_ge(done, before + (n.now - 1))
                nc.vector.tensor_tensor(b["hot"][:, half], digits[:, :].unsqueeze(1).unsqueeze(1).broadcast_to(four),
                                        b["halff"][:, half].unsqueeze(3).broadcast_to(four), ALU.is_equal
                                        ).then_inc(done, n.one())
                meanwhile()
            for half in range(2):
                dve.wait_ge(done, before + (n.now - 1))
                nc.vector.tensor_tensor(b["hot"][:, half], b["hot"][:, half],
                                        b["atf"][:, half].unsqueeze(2).broadcast_to(four), ALU.mult
                                        ).then_inc(done, n.one())
                meanwhile()
            for half in range(2):
                dve.wait_ge(done, before + (n.now - 1))
                nc.vector.tensor_reduce(b["found"][:, half], b["hot"][:, half], AXX, ALU.add).then_inc(done, n.one())
                meanwhile()
            dve.wait_ge(done, before + n.now)
            nc.vector.scalar_tensor_tensor(expert_slots, b["found"][:, 0], float(NE), b["found"][:, 1], ALU.mult,
                                           ALU.add).then_inc(done, n.one())

        def gate_softmax(dve, t, den, exp_in, exped, v):
            g3 = gates[:, t, :].rearrange("p (h k) -> p h k", k=TOPK)
            n = counter()
            n.now = 3 * t
            nc.vector.tensor_tensor(g3, best[:, t], best[:, t, :, 0:1].broadcast_to([P, NH, TOPK]),
                                    ALU.subtract).then_inc(exp_in, 1)
            dve.wait_ge(exped, t + 1)
            nc.vector.tensor_reduce(den[:, :], g3, AXX, ALU.add).then_inc(v, n.one())
            dve.wait_ge(v, n.now)
            nc.vector.reciprocal(den[:, :], den[:, :]).then_inc(v, n.one())
            dve.wait_ge(v, n.now)
            nc.vector.tensor_tensor(g3, g3, den[:, :].unsqueeze(2).broadcast_to([P, NH, TOPK]), ALU.mult
                                    ).then_inc(v, n.one())

        def gate_exp(act, t, exp_in, exped):
            act.wait_ge(exp_in, t + 1)
            nc.scalar.activation(gates[:, t, :], gates[:, t, :], ACT.Exp).then_inc(exped, 1)

        with ExitStack() as tmp, stage() as (block, (chosen, counted, *_)):
            buffers = choice_buffers("first", NH, tmp)

            @block.gpsimd
            def _(pool):
                nc.gpsimd.iota(digits[:, :], [[1, TOPK]], base=0, channel_multiplier=0,
                               allow_small_or_imprecise_dtypes=True).then_inc(counted, 1)

            @block.vector
            def _(dve):
                n = counter()
                dve.wait_ge(counted, 1)
                dve.sem_inc(chosen, n.one())
                choose(dve, chosen, n, 0, buffers, lambda half, h: scores[0][:, half, h, :], lambda h: best[:, 0, h, :],
                       experts[:, 0, :].rearrange("p (h k) -> p h k", k=TOPK), lambda c: dve.wait_ge(chosen, c),
                       lambda: None)
                assert n.now == choice_steps(NH) + 1

        BATCH = TOPK // 2
        TURNS = NH
        y_tok = sb("y_tok", [P, TT, D], where=peer)
        weights = sb("weights", [P, TT, SLOTS], where=peer)
        row_in = [[sem(f"row_in{s}_{i}") for i in range(BATCH)] for s in range(2)]
        row_used = sem("row_used")
        with ExitStack() as tmp:
            index = sb("index", [P, 2, BATCH], U32, where=tmp)
            row = sb("row", [P, 2, BATCH, D], where=tmp)
            dots = sb("dots", [P, TOPK], where=tmp)
            idle = sb("idle", [P, 2], where=tmp)
            buffers = choice_buffers("head", 1, tmp)
            den = sb("den", [P, NH], where=tmp)
            head_scores = sb("head_scores", [P, 2, NE], where=tmp)
            head_best = sb("head_best", [P, TOPK], where=tmp)
            STEPS = choice_steps(1) + 2
            with stage() as (block, (index_ready, index_read, gelu_in, gelued, weighted, v, idle_set, chosen, exp_in,
                                     exped, gate_steps, *_)):
                @block.gpsimd
                def _(pool):
                    nc.gpsimd.memset(idle[:, :], 0.0).then_inc(idle_set, 1)
                    pool.wait_ge(idle_set, 1)
                    for p in range(2 * TT):
                        t, table = p // 2, ("peer_u", "peer_v")[p % 2]

                        def batch(g, s, again):
                            before = g * TOPK + (2 * p * TURNS + s - 1) * BATCH
                            if again:
                                pool.wait_ge(index_read, before)
                                pool.wait_ge(row_used, before)
                            if p == 2 and s == 0:
                                pool.wait_ge(chosen, g * STEPS + (STEPS + 1))
                            nc.gpsimd.tensor_copy(index[:, s, :], experts[:, t, bass.ds(g * TOPK + s * BATCH, BATCH)]
                                                  ).then_inc(index_ready, 1)
                            pool.wait_ge(index_ready, g * 2 + (2 * p * TURNS + s + 1))
                            nc.gpsimd.tensor_tensor(idle[:, 0:1], idle[:, 1:2], idle[:, 1:2], ALU.add)
                            for i in range(BATCH):
                                pool.indirect_dma_start(
                                    out=row[:, s, i, :], out_offset=None, in_=A[table],
                                    in_offset=bass.IndirectOffsetOnAxis(ap=index[:, s, i:i + 1], axis=0),
                                    engine_sem=index_read).then_inc(row_in[s][i], 16)
                        if p == 0:
                            batch(0, 0, False)
                            batch(0, 1, False)
                        with pool.Fori(1 if p == 0 else 0, TURNS) as g:
                            batch(g, 0, True)
                            batch(g, 1, True)

                @block.scalar
                def _(act):
                    for t in range(TT):
                        gate_exp(act, t, exp_in, exped)
                        act.wait_ge(gelu_in, t + 1)
                        nc.scalar.activation(weights[:, t, :], weights[:, t, :], ACT.Gelu).then_inc(gelued, 1)

                @block.vector
                def _(dve):
                    def dot(p, g, e):
                        dve.wait_ge(row_in[e // BATCH][e % BATCH], g * 16 + 16 * (p * TURNS + 1))
                        u_row = row[:, e // BATCH, e % BATCH, :]
                        nc.vector.tensor_tensor_reduce(u_row, u_row, h_tok[:, p // 2, :], 1.0, 0.0, ALU.mult, ALU.add,
                                                       dots[:, e:e + 1]).then_inc(row_used, 1)

                    def dots_out(p, g):
                        dve.wait_ge(row_used, g * TOPK + (p * TURNS + 1) * TOPK)
                        nc.vector.tensor_scalar(weights[:, p // 2, bass.ds(g * TOPK, TOPK)], dots[:, :], 1.0, None,
                                                ALU.mult).then_inc(v, 1)

                    def sum_up(p, g, e):
                        t = p // 2
                        dve.wait_ge(row_in[e // BATCH][e % BATCH], g * 16 + 16 * (p * TURNS + 1))
                        dve.wait_ge(row_used, g * TOPK + (p * TURNS * TOPK + e))
                        nc.vector.scalar_tensor_tensor(y_tok[:, t, :], row[:, e // BATCH, e % BATCH, :],
                                                       weights[:, t, bass.ds(g * TOPK + e, 1)], y_tok[:, t, :],
                                                       ALU.mult, ALU.add).then_inc(row_used, 1)

                    def choose_head(h, work):
                        steps, slot, before = counter(), counter(), h * STEPS
                        steps.one()

                        def meanwhile():
                            if slot.now < TOPK:
                                work(slot.now)
                                slot.one()

                        def hold(c):
                            assert slot.now < TOPK
                            dve.wait_ge(chosen, before + c)
                            meanwhile()
                        dve.wait_ge(chosen, before + 1)
                        nc.vector.tensor_copy(head_scores[:, :, :],
                                              scores[1][:, :, bass.ds(h, 1), :].rearrange("p s a n -> p s (a n)")
                                              ).then_inc(chosen, steps.one())
                        choose(dve, chosen, steps, before, buffers, lambda half, i: head_scores[:, half, :],
                               lambda i: head_best[:, :], experts[:, 1, bass.ds(h * TOPK, TOPK)].unsqueeze(1), hold,
                               meanwhile)
                        nc.vector.tensor_copy(best[:, 1, bass.ds(h, 1), :].rearrange("p a n -> p (a n)"),
                                              head_best[:, :]).then_inc(chosen, steps.one())
                        assert steps.now == STEPS + 1
                        for e in range(slot.now, TOPK):
                            work(e)

                    def weigh(t):
                        if t == 1:
                            dve.wait_ge(chosen, NH * STEPS + 1)
                        gate_softmax(dve, t, den, exp_in, exped, gate_steps)
                        dve.wait_ge(gate_steps, 3 * (t + 1))
                        dve.wait_ge(gelued, t + 1)
                        nc.vector.tensor_tensor(weights[:, t, :], weights[:, t, :], gates[:, t, :],
                                                ALU.mult).then_inc(weighted, 1)
                        dve.wait_ge(weighted, t + 1)

                    for t in range(TT):
                        nc.vector.memset(y_tok[:, t, :], 0.0).then_inc(v, 1)
                    dve.wait_ge(v, TT)
                    dve.sem_inc(chosen, 1)
                    with dve.Fori(0, TURNS // 2) as g:
                        for odd in range(2):
                            turn = g * 2 + odd
                            dve.wait_ge(v, turn + TT)
                            if odd == 0:
                                choose_head(g, lambda e: dot(0, turn, e))
                            else:
                                for e in range(TOPK):
                                    dot(0, turn, e)
                            dots_out(0, turn)
                    dve.wait_ge(v, TT + TURNS)
                    dve.sem_inc(gelu_in, 1)
                    weigh(0)
                    with dve.Fori(0, TURNS // 2) as g:
                        choose_head(g + NH // 2, lambda e: sum_up(1, g * 2, e))
                        for e in range(TOPK):
                            sum_up(1, g * 2 + 1, e)
                    with dve.Fori(0, TURNS) as g:
                        dve.wait_ge(v, g + (TT + TURNS))
                        for e in range(TOPK):
                            dot(2, g, e)
                        dots_out(2, g)
                    dve.wait_ge(v, TT + 2 * TURNS)
                    dve.sem_inc(gelu_in, 1)
                    weigh(1)
                    with dve.Fori(0, TURNS) as g:
                        for e in range(TOPK):
                            sum_up(3, g, e)

        with stage() as (block, (turned, *_)):
            @block.tensor
            def _(pe):
                for k in range(KT):
                    for t in range(TT):
                        last = nc.tensor.transpose(ps[:, k, t * P:(t + 1) * P], y_tok[:, t, k * P:(k + 1) * P],
                                                   mat("ident"))
                    last.then_inc(turned, 1)

            @block.vector
            def _(dve):
                for k in range(KT):
                    dve.wait_ge(turned, k + 1)
                    nc.vector.scalar_tensor_tensor(xT[:, k, :], ps[:, k, 0:S], mod[:, 40 + k:41 + k], xT[:, k, :],
                                                   ALU.mult, ALU.add)
        peer.close()

        def norm_w(layer, which):
            return lambda k: vec("norm_w", (layer * 3 + which) * KT + k)

        swiglu(norm_w(0, 0))
        rms_norm(norm_w(0, 1), None)

        even = ExitStack()
        ez = sb("ez", [P, T_EV, S], where=even)
        et = sb("et", [P, TT, T_EV_TOK * P], where=even)
        project(T_EV, hT, lambda i, src: nc.vector.tensor_scalar(one(ez, i), src, 1.0, None, ALU.mult),
                T_EV_TOK, lambda i, src: nc.vector.tensor_copy(et[:, :, i * S:(i + 1) * S], src))
        with ExitStack() as tmp, stage() as (block, (tables_in, gelu_u, gelu_v, root_in, root, centred, v, normed,
                                                     w_masked, gated, sq_done, sig, *_)):
            ws = sb("ws", [P, NH, P], where=tmp)
            gb = sb("gb", [P, 4, P], where=tmp)
            st2 = sb("st2", [P, 2, 16], where=tmp)
            vg = et[:, :, 0:512].rearrange("p t (h e) -> p t h e", e=HD)
            mean4 = st2[:, 0, :].rearrange("p (t h) -> p t h", t=TT).unsqueeze(3).broadcast_to([P, TT, NH, HD])
            var4 = st2[:, 1, :].rearrange("p (t h) -> p t h", t=TT).unsqueeze(3).broadcast_to([P, TT, NH, HD])
            sq4 = sq[:, 0:4, :].rearrange("p (t a) (h e) -> p t (a h) e", t=TT, e=HD)

            @block.sync
            def _(sp):
                sp.dma_start(ws[:, :, :], A["gm_w"]).then_inc(tables_in, 16)
                sp.dma_start(gb[:, :, :], A["gm_b"]).then_inc(tables_in, 16)

            @block.scalar
            def _(act):
                nc.scalar.activation(et[:, :, 0:512], et[:, :, 0:512], ACT.Gelu_apprx_tanh).then_inc(gelu_v, 1)
                nc.scalar.activation(ez[:, 0:4, :], ez[:, 0:4, :], ACT.Gelu_apprx_tanh).then_inc(gelu_u, 1)
                act.wait_ge(root_in, 1)
                nc.scalar.activation(st2[:, 1, :], st2[:, 1, :], ACT.Sqrt).then_inc(root, 1)
                nc.scalar.activation(et[:, :, 768:792], et[:, :, 768:792], ACT.Sigmoid)

            @block.vector
            def _(dve):
                n = counter()
                dve.wait_ge(tables_in, 32)
                causal = mat("upto0").unsqueeze(1).broadcast_to([P, NH, P])
                nc.vector.tensor_tensor(ws[:, :, :], ws[:, :, :], causal, ALU.mult).then_inc(w_masked, 1)
                dve.wait_ge(gelu_v, 1)
                nc.vector.tensor_reduce(st2[:, 0, :].rearrange("p (t h) -> p t h", t=TT), vg, AXX,
                                        ALU.add).then_inc(v, n.one())
                dve.wait_ge(v, n.now)
                nc.vector.tensor_scalar(st2[:, 0, :], st2[:, 0, :], 1.0 / HD, None, ALU.mult).then_inc(v, n.one())
                dve.wait_ge(v, n.now)
                nc.vector.tensor_tensor(vg, vg, mean4, ALU.subtract).then_inc(v, n.one())
                dve.wait_ge(v, n.now)
                nc.vector.tensor_tensor(sq4, vg, vg, ALU.mult).then_inc(v, n.one())
                dve.wait_ge(v, n.now)
                nc.vector.tensor_reduce(st2[:, 1, :].rearrange("p (t h) -> p t h", t=TT), sq4, AXX,
                                        ALU.add).then_inc(v, n.one())
                dve.wait_ge(v, n.now)
                nc.vector.tensor_scalar(st2[:, 1, :], st2[:, 1, :], 1.0 / HD, 1e-5, ALU.mult,
                                        ALU.add).then_inc(root_in, 1)
                dve.wait_ge(root, 1)
                nc.vector.reciprocal(st2[:, 1, :], st2[:, 1, :]).then_inc(v, n.one())
                dve.wait_ge(v, n.now)
                nc.vector.tensor_tensor(vg, vg, var4, ALU.mult).then_inc(normed, 1)
                dve.wait_ge(gelu_u, 1)
                for j in range(4):
                    dve.wait_ge(gated, j + 1)
                    m2 = mix[:, j, :].rearrange("p (c t) -> p c t", c=TT)
                    nc.vector.tensor_tensor(m2, ps[:, j, 0:S].rearrange("p (c t) -> p c t", c=TT),
                                            gb[:, j, :].unsqueeze(1).broadcast_to([P, TT, P]), ALU.add
                                            ).then_inc(v, n.one())
                    dve.wait_ge(v, n.now)
                    nc.vector.tensor_tensor(mix[:, j, :], mix[:, j, :], ez[:, j, :], ALU.mult)

            @block.tensor
            def _(pe):
                pe.wait_ge(w_masked, 1)
                pe.wait_ge(normed, 1)
                for j in range(4):
                    for h in (2 * j, 2 * j + 1):
                        for c in range(TT):
                            last = nc.tensor.matmul(ps[rows(h), j, c * P:(c + 1) * P], et[:, c, h * HD:(h + 1) * HD],
                                                    ws[:, h, :], start=True, stop=True)
                    last.then_inc(gated, 1)

        nsa = ExitStack()
        kcmp = sb("kcmp", [P, NC_CMP], where=nsa)
        vcmp = sb("vcmp", [NC_CMP, P], where=nsa)
        cmp_mask = sb("cmp_mask", [P, TT, NC_CMP], where=nsa)
        causal = sb("causal", [P, TT, S], where=nsa)
        any_cmp = sb("any_cmp", [P, TT], where=nsa)
        cmp_gate = sb("cmp_gate", [P, TT, NH], where=nsa)
        with ExitStack() as tmp, stage() as (block, (rope_in, w_in, rotated, v, pooled, hidden, hidden_ready, keys,
                                                     keys_copied, keys_rot, small_in, *_)):
            cos, sin = sb("cos", [P, S], where=tmp), sb("sin", [P, S], where=tmp)
            cosc, sinc = sb("cosc", [P, NC_CMP], where=tmp), sb("sinc", [P, NC_CMP], where=tmp)
            pe_cmp = sb("pe_cmp", [P, 2, 32], where=tmp)
            w1 = sb("w1", [P, 2, 32, HD], where=tmp)
            w2 = sb("w2", [P, 2, HD], where=tmp)
            blocks = sb("blocks", [P, 2, 32, NC_CMP], where=tmp)
            hc = sb("hc", [P, 2, NC_CMP], where=tmp)
            kraw = sb("kraw", [P, NC_CMP], where=tmp)
            krot = sb("krot", [P, NC_CMP], where=tmp)
            turned_qk = sb("turned_qk", [P, 6, S], where=tmp)
            roped = [4, 5, 6, 7, 10, 11]

            @block.sync
            def _(sp):
                for dst, name in ((cos[:, :], "cos"), (sin[:, :], "sin")):
                    sp.dma_start(dst, A[name]).then_inc(rope_in, 16)
                for dst, name in ((cosc[:, :], "cosc"), (sinc[:, :], "sinc"), (pe_cmp[:, :, :], "pe_cmp"),
                                  (cmp_mask[:, :, :], "cmp_mask"), (causal[:, :, :], "causal"),
                                  (any_cmp[:, :], "any_cmp")):
                    sp.dma_start(dst, A[name]).then_inc(small_in, 16)
                sp.dma_start(w1[:, :, :, :], A["cmp_w1"]).then_inc(w_in, 16)
                sp.dma_start(w2[:, :, :], A["cmp_w2"]).then_inc(w_in, 16)

            @block.tensor
            def _(pe):
                for n, i in enumerate(roped):
                    nc.tensor.matmul(ps[:, n // 2, n % 2 * S:n % 2 * S + S], mat("rotate"), ez[:, i, :], start=True,
                                     stop=True).then_inc(rotated, 1)
                pe.wait_ge(w_in, 32)
                pe.wait_ge(pooled, 2)
                for kv in range(2):
                    for g in range(2):
                        r = slice(g * HD, (g + 1) * HD)
                        for pos in range(32):
                            last = nc.tensor.matmul(ps[r, 3 + kv, 0:NC_CMP], w1[r, kv, pos, :],
                                                    blocks[r, kv, pos, :], start=(pos == 0), stop=(pos == 31))
                    last.then_inc(hidden, 1)
                pe.wait_ge(hidden_ready, 2)
                for g in range(2):
                    r = slice(g * HD, (g + 1) * HD)
                    nc.tensor.matmul(ps[r, 5, 0:NC_CMP], w2[r, 0, :], hc[r, 0, :], start=True, stop=True
                                     ).then_inc(keys, 1)
                    nc.tensor.matmul(ps[0:NC_CMP, 3 + g, r], hc[r, 1, :], w2[r, 1, :], start=True, stop=True
                                     ).then_inc(keys, 1)
                pe.wait_ge(keys_copied, 1)
                nc.tensor.matmul(ps[:, 7, 0:NC_CMP], mat("rotate"), kraw[:, :], start=True, stop=True
                                 ).then_inc(keys_rot, 1)

            @block.scalar
            def _(act):
                for kv in range(2):
                    act.wait_ge(hidden, kv + 1)
                    nc.scalar.activation(hc[:, kv, :], ps[:, 3 + kv, 0:NC_CMP], ACT.Gelu_apprx_tanh
                                         ).then_inc(hidden_ready, 1)
                act.wait_ge(keys, 4)
                for g in range(2):
                    r = slice(g * HD, (g + 1) * HD)
                    nc.scalar.activation(vcmp[:, r], ps[0:NC_CMP, 3 + g, r], ACT.Copy)

            @block.vector
            def _(dve):
                n = counter()
                dve.wait_ge(small_in, 16 * 6)
                for kv in range(2):
                    for part in range(2):
                        src = ez[:, 8 + kv, 16 * part:16 * part + 16 * NC_CMP].rearrange("p (n l) -> p l n", l=16)
                        nc.vector.tensor_tensor(blocks[:, kv, 16 * part:16 * part + 16, :], src,
                                                pe_cmp[:, kv, 16 * part:16 * part + 16].unsqueeze(2)
                                                .broadcast_to([P, 16, NC_CMP]), ALU.add).then_inc(v, n.one())
                dve.wait_ge(v, n.now)
                dve.sem_inc(pooled, 2)
                dve.wait_ge(rope_in, 32)
                dve.wait_ge(rotated, 6)
                nc.vector.tensor_tensor(turned_qk[:, :, :], ps[:, 0:3, :].rearrange("p b (c t) -> p (b c) t", t=S),
                                        sin[:, :].unsqueeze(1).broadcast_to([P, 6, S]), ALU.mult).then_inc(v, n.one())
                for a, b in ((4, 8), (10, 12)):
                    nc.vector.tensor_tensor(ez[:, a:b, :], ez[:, a:b, :],
                                            cos[:, :].unsqueeze(1).broadcast_to([P, b - a, S]),
                                            ALU.mult).then_inc(v, n.one())
                dve.wait_ge(v, n.now)
                nc.vector.tensor_tensor(ez[:, 4:8, :], ez[:, 4:8, :], turned_qk[:, 0:4, :], ALU.add)
                nc.vector.tensor_tensor(ez[:, 10:12, :], ez[:, 10:12, :], turned_qk[:, 4:6, :], ALU.add)
                gl = et[:, :, 768:792].rearrange("p t (h b) -> p t h b", b=3)
                nc.vector.tensor_tensor(cmp_gate[:, :, :], gl[:, :, :, 0:1].rearrange("p t h b -> p t (h b)"),
                                        any_cmp[:, :].unsqueeze(2).broadcast_to([P, TT, NH]), ALU.mult)
                dve.wait_ge(keys, 4)
                nc.vector.tensor_copy(kraw[:, :], ps[:, 5, 0:NC_CMP]).then_inc(keys_copied, 1)
                dve.wait_ge(keys_rot, 1)
                nc.vector.tensor_tensor(krot[:, :], ps[:, 7, 0:NC_CMP], sinc[:, :], ALU.mult).then_inc(v, n.one())
                dve.wait_ge(keys_copied, 1)
                nc.vector.tensor_tensor(kraw[:, :], kraw[:, :], cosc[:, :], ALU.mult).then_inc(v, n.one())
                dve.wait_ge(v, n.now)
                nc.vector.tensor_tensor(kcmp[:, :], kraw[:, :], krot[:, :], ALU.add)

        gl = et[:, :, 768:792].rearrange("p t (h b) -> p t h b", b=3)
        units = []
        for j in range(4):
            for g in range(2):
                h, r = j + 4 * g, slice(g * HD, (g + 1) * HD)
                base = dict(po=g * HD, j=4 + j, q=ez[r, 4 + j, :])
                units.append(dict(base, n=NC_CMP, k=kcmp[r, :], bias=cmp_mask[:, :, :], v=[vcmp[:, r]],
                                  gate=cmp_gate[:, :, h]))
                for b, keys_at, v_at in ((1, 10, 512), (2, 11, 640)):
                    units.append(dict(base, n=S, k=ez[r, keys_at, :], bias=causal[:, :, :],
                                      v=[et[:, t, v_at + g * HD:v_at + (g + 1) * HD] for t in range(TT)],
                                      gate=gl[:, :, h, b]))
        attention(units, mix, "nsa")
        nsa.close()
        even.close()
        project(T_OUT, mix, lambda i, src: nc.vector.tensor_tensor(one(xT, i), src, one(xT, i), ALU.add))

        s5 = ExitStack()
        decay = sb("decay", [P, S5T], where=s5)
        fre, fim = sb("fre", [P, S5T], where=s5), sb("fim", [P, S5T], where=s5)
        wre, wim = sb("wre", [P, S5T, S], where=s5), sb("wim", [P, S5T, S], where=s5)
        s5_b = sb("s5_b", [P, 4, 2, P], where=s5)
        s5_c = sb("s5_c", [P, 2, S5T, 32], where=s5)
        dt, theta, turns_of, part_of = (sb(n, [P, S5T], where=s5) for n in ("dt", "theta", "turns_of", "part_of"))
        sine, cosine, lre_bar, lim_bar = (sb(n, [P, S5T], where=s5) for n in ("sine", "cosine", "lre_bar", "lim_bar"))
        t1, t2, t3 = (sb(f"t{i}", [P, S5T], where=s5) for i in range(3))
        cre = sb("cre", [P, S5T, 32], where=s5)
        big1, big2 = sb("big1", [P, S5T, P], where=s5), sb("big2", [P, S5T, P], where=s5)
        step_re, step_im = sb("step_re", [P, S5T], where=s5), sb("step_im", [P, S5T], where=s5)
        dt_ready, args, trig, table_steps = sem("dt_ready"), sem("args"), sem("trig"), sem("table_steps")
        s5_in, norm_ready, norm_inverted = sem("s5_in"), sem("norm_ready"), sem("norm_inverted")
        table_n = counter()
        tt, ts = nc.gpsimd.tensor_tensor, nc.gpsimd.tensor_scalar

        def inc(ins):
            ins.then_inc(table_steps, table_n.one())

        def step_aside(pool, ins):
            inc(ins)
            pool.wait_ge(table_steps, table_n.now)

        def angles_gpsimd(pool):
            pool.wait_ge(dt_ready, 1)
            tt(decay[:, :], vec_all("lam_re"), dt[:, :], ALU.mult).then_inc(args, 1)
            step_aside(pool, tt(theta[:, :], vec_all("lam_im"), dt[:, :], ALU.mult))
            step_aside(pool, ts(turns_of[:, :], theta[:, :], 1.0 / (2 * np.pi), None, ALU.mult))
            step_aside(pool, ts(turns_of[:, :], turns_of[:, :], 12582912.0, None, ALU.add))
            step_aside(pool, ts(turns_of[:, :], turns_of[:, :], -12582912.0, None, ALU.add))
            for part in (6.28125, 0.0019350051879882812, float(2 * np.pi - 6.28125 - 0.0019350051879882812)):
                step_aside(pool, ts(part_of[:, :], turns_of[:, :], -part, None, ALU.mult))
                step_aside(pool, tt(theta[:, :], theta[:, :], part_of[:, :], ALU.add))
            ts(theta[:, :], theta[:, :], 3.1415925, -3.1415925, ALU.min, ALU.max).then_inc(args, 1)

        def angles_scalar(act):
            act.wait_ge(args, 1)
            nc.scalar.activation(decay[:, :], decay[:, :], ACT.Exp).then_inc(trig, 1)
            act.wait_ge(args, 2)
            nc.scalar.activation(sine[:, :], theta[:, :], ACT.Sin).then_inc(trig, 1)
            nc.scalar.activation(cosine[:, :], theta[:, :], ACT.Sin, scale=0.5).then_inc(trig, 1)

        def load_s5(sp):
            sp.dma_start(s5_b[:, :, :, :], A["s5_b"]).then_inc(s5_in, 16)
            sp.dma_start(s5_c[:, :, :, :], A["s5_c"]).then_inc(s5_in, 16)

        def tables_gpsimd(pool):
            def step(ins):
                step_aside(pool, ins)
            lre, lim = vec_all("lam_re"), vec_all("lam_im")
            pool.wait_ge(trig, 3)
            inc(tt(dt[:, :], lre, lre, ALU.mult))
            step(tt(t3[:, :], lim, lim, ALU.mult))
            tt(dt[:, :], dt[:, :], t3[:, :], ALU.add).then_inc(norm_ready, 1)
            step(tt(cosine[:, :], cosine[:, :], cosine[:, :], ALU.mult))
            step(ts(cosine[:, :], cosine[:, :], -2.0, 1.0, ALU.mult, ALU.add))
            inc(tt(lim_bar[:, :], decay[:, :], sine[:, :], ALU.mult))
            step(tt(lre_bar[:, :], decay[:, :], cosine[:, :], ALU.mult))
            step(ts(lre_bar[:, :], lre_bar[:, :], -1.0, None, ALU.add))
            inc(tt(fre[:, :], lre_bar[:, :], lre, ALU.mult))
            inc(tt(fim[:, :], lim_bar[:, :], lre, ALU.mult))
            inc(tt(t1[:, :], lim_bar[:, :], lim, ALU.mult))
            step(tt(t2[:, :], lre_bar[:, :], lim, ALU.mult))
            inc(tt(fre[:, :], fre[:, :], t1[:, :], ALU.add))
            inc(tt(fim[:, :], fim[:, :], t2[:, :], ALU.subtract))
            inc(nc.gpsimd.memset(wre[:, :, 0:1], 1.0))
            inc(nc.gpsimd.memset(wim[:, :, 0:1], 0.0))
            inc(nc.gpsimd.tensor_copy(step_re[:, :], cosine[:, :]))
            step(nc.gpsimd.tensor_copy(step_im[:, :], sine[:, :]))
            size = 1
            while size < S:
                low, high = slice(0, size), slice(size, 2 * size)
                shape = [P, S5T, size]
                sr = step_re[:, :].unsqueeze(2).broadcast_to(shape)
                si = step_im[:, :].unsqueeze(2).broadcast_to(shape)
                inc(tt(wre[:, :, high], wre[:, :, low], sr, ALU.mult))
                inc(tt(wim[:, :, high], wre[:, :, low], si, ALU.mult))
                inc(tt(big1[:, :, low], wim[:, :, low], si, ALU.mult))
                step(tt(big2[:, :, low], wim[:, :, low], sr, ALU.mult))
                inc(tt(wre[:, :, high], wre[:, :, high], big1[:, :, low], ALU.subtract))
                inc(tt(wim[:, :, high], wim[:, :, high], big2[:, :, low], ALU.add))
                inc(tt(t1[:, :], step_re[:, :], step_re[:, :], ALU.mult))
                inc(tt(t2[:, :], step_im[:, :], step_im[:, :], ALU.mult))
                step(tt(t3[:, :], step_re[:, :], step_im[:, :], ALU.mult))
                inc(tt(step_re[:, :], t1[:, :], t2[:, :], ALU.subtract))
                step(ts(step_im[:, :], t3[:, :], 2.0, None, ALU.mult))
                size *= 2
            pool.wait_ge(norm_inverted, 1)
            inc(tt(fre[:, :], fre[:, :], dt[:, :], ALU.mult))
            step(tt(fim[:, :], fim[:, :], dt[:, :], ALU.mult))
            pool.wait_ge(s5_in, 32)
            wide = [P, S5T, 32]
            fr, fi = fre[:, :].unsqueeze(2).broadcast_to(wide), fim[:, :].unsqueeze(2).broadcast_to(wide)
            inc(tt(cre[:, :, :], s5_c[:, 0], fi, ALU.mult))
            step(tt(big1[:, :, 0:32], s5_c[:, 1], fi, ALU.mult))
            inc(tt(s5_c[:, 0], s5_c[:, 0], fr, ALU.mult))
            step(tt(s5_c[:, 1], s5_c[:, 1], fr, ALU.mult))
            inc(tt(s5_c[:, 0], s5_c[:, 0], big1[:, :, 0:32], ALU.subtract))
            step(tt(s5_c[:, 1], s5_c[:, 1], cre[:, :, :], ALU.add))
            step(ts(s5_c[:, 1].rearrange("p a b -> p (a b)"), s5_c[:, 1].rearrange("p a b -> p (a b)"), -1.0, None,
                    ALU.mult))

        def tables_vector(dve):
            dve.wait_ge(norm_ready, 1)
            nc.vector.reciprocal(dt[:, :], dt[:, :]).then_inc(norm_inverted, 1)

        swiglu(norm_w(0, 2), dict(sync=load_s5, gpsimd=angles_gpsimd, scalar=angles_scalar,
                                  scalar_first=lambda act: nc.scalar.activation(dt[:, :], vec_all("log_dt"), ACT.Exp)
                                  .then_inc(dt_ready, 1), vector=lambda dve: None))

        swiglu(norm_w(1, 0), dict(sync=lambda sp: None, gpsimd=tables_gpsimd, scalar=lambda act: None,
                                  scalar_first=lambda act: None,
                                  vector=tables_vector))
        odd = ExitStack()
        oz = sb("oz", [P, KT, S], where=odd)
        project(KT, xT, lambda i, src: nc.vector.tensor_tensor(one(oz, i), src, rstd[:, :], ALU.mult),
                gain=norm_w(1, 1))

        with ExitStack() as tmp, stage() as (block, (pool_in, v, pooled, mapped, *_)):
            pw = sb("pw", [P, 4, P], where=tmp)
            inv_count = sb("inv_count", [P, 4, S], where=tmp)
            sums_a = sb("sums_a", [P, 4, S], where=tmp)
            sums_b = sb("sums_b", [P, 4, S], where=tmp)

            @block.sync
            def _(sp):
                sp.dma_start(pw[:, :, :], A["pool_w"].rearrange("g c d -> c g d")).then_inc(pool_in, 16)
                sp.dma_start(inv_count[:, :, :], A["inv_count"]).then_inc(pool_in, 16)

            @block.vector
            def _(dve):
                n = counter()
                cur, nxt = oz[:, 0:4, :], sums_a[:, :, :]
                bufs = [sums_a[:, :, :], sums_b[:, :, :]]
                for lv in range(4):
                    shift = 1 << lv
                    nxt = bufs[lv % 2]
                    if lv:
                        nc.vector.tensor_copy(nxt[:, 0:lv, :], cur[:, 0:lv, :]).then_inc(v, n.one())
                    nc.vector.tensor_copy(nxt[:, lv:4, 0:shift], cur[:, lv:4, 0:shift]).then_inc(v, n.one())
                    nc.vector.tensor_tensor(nxt[:, lv:4, shift:S], cur[:, lv:4, shift:S], cur[:, lv:4, 0:S - shift],
                                            ALU.add).then_inc(v, n.one())
                    dve.wait_ge(v, n.now)
                    cur = nxt
                dve.wait_ge(pool_in, 32)
                nc.vector.tensor_tensor(sums_a[:, :, :], cur, inv_count[:, :, :], ALU.mult).then_inc(v, n.one())
                dve.wait_ge(v, n.now)
                nc.vector.tensor_tensor(sums_a[:, :, :], sums_a[:, :, :], oz[:, 0:4, :], ALU.subtract
                                        ).then_inc(pooled, 1)
                for g in range(4):
                    dve.wait_ge(mapped, g + 1)
                    nc.vector.tensor_scalar(mix[:, g, :], ps[:, g, 0:S], vec("pool_scale", g), None, ALU.mult)

            @block.tensor
            def _(pe):
                pe.wait_ge(pooled, 1)
                for g in range(4):
                    nc.tensor.matmul(ps[:, g, 0:S], pw[:, g, :], sums_a[:, g, :], start=True, stop=True
                                     ).then_inc(mapped, 1)

        with ExitStack() as tmp, stage() as (block, (fed, v, scanned, w, turned_back, out_ready, crossed, halfway, *_)):
            a1, a2, a3, a4 = (sb(f"a{i}", [P, S], where=tmp) for i in range(4))
            zre, zim = sb("zre", [P, 2, S], where=tmp), sb("zim", [P, 2, S], where=tmp)
            b1, b2 = (sb(f"b{i}", [P, 2, S], where=tmp) for i in range(2))
            b3, b4 = (sb(f"b{i}", [P, S], where=tmp) for i in range(2, 4))
            xre, xim = sb("xre", [P, 2, S], where=tmp), sb("xim", [P, 2, S], where=tmp)

            @block.tensor
            def _(pe):
                for s in range(S5T + 2):
                    if s < S5T:
                        if s >= 2:
                            pe.wait_ge(v, s - 1)
                        r = slice(32 * (s % 4), 32 * (s % 4) + 32)
                        for c in range(2):
                            last = nc.tensor.matmul(ps[:, s % 2, c * S:(c + 1) * S], s5_b[r, s // 4, c, :],
                                                    oz[r, 4 + s // 4, :], start=True, stop=True)
                        last.then_inc(fed, 1)
                    if s >= 2:
                        i = s - 2
                        pe.wait_ge(turned_back, i + 1)
                        r = slice(32 * (i % 4), 32 * (i % 4) + 32)
                        nc.tensor.matmul(ps[r, 2 + i // 4, 0:S], s5_c[:, 0, i, :], xre[:, i % 2, :], start=True,
                                         stop=False)
                        nc.tensor.matmul(ps[r, 2 + i // 4, 0:S], s5_c[:, 1, i, :], xim[:, i % 2, :], start=False,
                                         stop=True).then_inc(out_ready, 1)

            @block.vector
            def _(dve):
                tt = nc.vector.tensor_tensor
                n = counter()

                def turn_back(i):
                    dve.wait_ge(scanned, 2 * i + 2)
                    if i >= 2:
                        dve.wait_ge(turned_back, i - 1)
                    tt(b1[:, i % 2, :], zre[:, i % 2, :], wre[:, i, :], ALU.mult)
                    tt(b2[:, i % 2, :], zim[:, i % 2, :], wim[:, i, :], ALU.mult).then_inc(halfway, 1)
                for s in range(S5T):
                    dve.wait_ge(fed, s + 1)
                    bre, bim = ps[:, s % 2, 0:S], ps[:, s % 2, S:2 * S]
                    if s:
                        dve.wait_ge(scanned, 2 * s)
                    tt(a1[:, :], bre, wre[:, s, :], ALU.mult).then_inc(w, n.one())
                    tt(a2[:, :], bim, wim[:, s, :], ALU.mult).then_inc(w, n.one())
                    tt(a3[:, :], bim, wre[:, s, :], ALU.mult).then_inc(w, n.one())
                    tt(a4[:, :], bre, wim[:, s, :], ALU.mult).then_inc(v, 1)
                    if s:
                        turn_back(s - 1)
                    dve.wait_ge(w, n.now)
                    tt(a1[:, :], a1[:, :], a2[:, :], ALU.add).then_inc(w, n.one())
                    dve.wait_ge(v, s + 1)
                    tt(a3[:, :], a3[:, :], a4[:, :], ALU.subtract).then_inc(w, n.one())
                    dve.wait_ge(w, n.now)
                    if s >= 2:
                        dve.wait_ge(turned_back, s - 1)
                        dve.wait_ge(halfway, s - 1)
                    nc.vector.tensor_tensor_scan(zre[:, s % 2, :], decay[:, s:s + 1].broadcast_to([P, S]), a1[:, :], 0.0, ALU.mult,
                                                 ALU.add).then_inc(scanned, 1)
                    nc.vector.tensor_tensor_scan(zim[:, s % 2, :], decay[:, s:s + 1].broadcast_to([P, S]), a3[:, :], 0.0, ALU.mult,
                                                 ALU.add).then_inc(scanned, 1)
                turn_back(S5T - 1)

            @block.gpsimd
            def _(pool):
                tt = nc.gpsimd.tensor_tensor
                for s in range(S5T):
                    pool.wait_ge(scanned, 2 * s + 2)
                    zr, zi, cr, ci = zre[:, s % 2, :], zim[:, s % 2, :], wre[:, s, :], wim[:, s, :]
                    if s:
                        pool.wait_ge(turned_back, s)
                    tt(b3[:, :], zr, ci, ALU.mult)
                    tt(b4[:, :], zi, cr, ALU.mult).then_inc(crossed, 1)
                    pool.wait_ge(crossed, s + 1)
                    if s >= 2:
                        pool.wait_ge(out_ready, s - 1)
                    tt(xim[:, s % 2, :], b3[:, :], b4[:, :], ALU.add)
                    pool.wait_ge(halfway, s + 1)
                    tt(xre[:, s % 2, :], b1[:, s % 2, :], b2[:, s % 2, :], ALU.subtract).then_inc(turned_back, 1)

        with stage() as (block, (skipped, gelued, *_)):
            @block.vector
            def _(dve):
                for j in range(4):
                    nc.vector.scalar_tensor_tensor(oz[:, 4 + j, :], oz[:, 4 + j, :], vec("s5_d", j), ps[:, 2 + j, 0:S],
                                                   ALU.mult, ALU.add).then_inc(skipped, 1)

            @block.scalar
            def _(act):
                act.wait_ge(skipped, 4)
                nc.scalar.activation(oz[:, 4:8, :], oz[:, 4:8, :], ACT.Gelu_apprx_tanh)

        with ExitStack() as tmp, stage() as (block, (src_high, src_low, sig_done, multiplied, *_)):
            sg = sb("sg", [P, 2, S], where=tmp)
            first = take(T_GLU)

            @block.sync
            def _(sp):
                refill(sp, first, T_GLU)

            @block.tensor
            def _(pe):
                for i in range(T_GLU):
                    pe.wait_ge(tiles_freed, first + i + 1)
                    for q in range(2):
                        for k in range(4):
                            if i == 0 and q == 0:
                                pe.wait_ge(src_low, k + 1)
                            last = product(ps[:, i, q * S:(q + 1) * S], first + i, 4 * q + k,
                                           (srch[:, k, :], srcl[:, k, :]), k == 0, k == 3)
                    last.then_inc(tiles_used, 1)

            @block.scalar
            def _(act):
                for k in range(4):
                    nc.scalar.activation(srch[:, k, :], oz[:, 4 + k, :], ACT.Copy).then_inc(src_high, 1)
                for i in range(T_GLU):
                    high(act, first + AHEAD + i)
                    act.wait_ge(tiles_used, first + i - T_ADA + 1)
                    if i >= 2:
                        act.wait_ge(multiplied, i - 1)
                    nc.scalar.activation(sg[:, i % 2, :], ps[:, i, S:2 * S], ACT.Sigmoid).then_inc(sig_done, 1)

            @block.vector
            def _(dve):
                for k in range(4):
                    dve.wait_ge(src_high, k + 1)
                    nc.vector.tensor_tensor(srcl[:, k, :], oz[:, 4 + k, :], srch[:, k, :].bitcast(F32), ALU.subtract
                                            ).then_inc(src_low, 1)
                for i in range(T_GLU):
                    low(dve, first + AHEAD + i)
                    dve.wait_ge(sig_done, i + 1)
                    nc.vector.tensor_tensor(mix[:, 4 + i, :], ps[:, i, 0:S], sg[:, i % 2, :], ALU.mult
                                            ).then_inc(multiplied, 1)
        odd.close()
        s5.close()
        project(KT, mix, lambda i, src: nc.vector.tensor_tensor(one(xT, i), src, one(xT, i), ALU.add))
        swiglu(norm_w(1, 2))
        rms_norm(lambda k: vec("final", k), None)
        assert stream[0] == TOTAL, (stream[0], TOTAL)
        with stage() as (block, _):
            @block.sync
            def _(sp):
                sp.dma_start(A["out"].rearrange("(k p) t -> p k t", p=P), hT[:, :, :]).then_inc(stored, 16)
                sp.wait_ge(stored, 16)


def tiles_of(w, order=None):
    k, n = w.shape
    t = w.reshape(k // P, P, n // P, P).transpose(2, 1, 0, 3).reshape(n // P, P, -1)
    return t if order is None else t[order]


def token_tiles_of(w):
    k, n = w.shape
    return w.reshape(2, KT // 2, P, n // S, S).transpose(3, 0, 2, 1, 4).reshape(2 * n // S, P, D)


def layout(a):
    f = {k: np.asarray(v) for k, v in a.items()}
    parts = [f["ada_w"][0].reshape(KT, P, 6, D).transpose(2, 0, 1, 3).reshape(T_ADA, P, D),
             token_tiles_of(f["w_in"][0][:, 1024:1536]),
             tiles_of(f["w_in"][0], list(range(0, 8)) + list(range(12, 26))),
             tiles_of(f["w_out"][0]), tiles_of(f["peer_w_query"][0])]

    def ffn(layer, which):
        g, u = tiles_of(f["ffn_w_gate_2"][layer, which]), tiles_of(f["ffn_w_up_2"][layer, which])
        d = f["ffn_w_down_2"][layer, which].reshape(FJ, P, D)
        seq = [g[0], u[0]]
        for j in range(1, FJ):
            seq += [g[j], u[j], d[j - 1]]
        return np.stack(seq + [d[FJ - 1]])
    parts.append(ffn(0, 0))
    w = f["ev_w_in_2"][0]
    q = w[:, 1024:1536].reshape(D, 2, 4, HD).transpose(0, 2, 1, 3).reshape(D, 512)
    kc, vc, ks, vs, kw, vw = (w[:, 1536 + P * i:1536 + P * i + P] for i in range(6))
    gl = np.zeros((D, 2 * P), np.float32)
    gl[:, :24] = w[:, 2304:2328]
    parts.append(token_tiles_of(np.concatenate([w[:, 512:1024], vs, vw, gl], axis=1)))
    parts.append(tiles_of(np.concatenate([w[:, 0:512], q, kc, vc, ks, kw], axis=1)))
    wo = f["ev_w_out_2"][0]
    parts.append(tiles_of(np.concatenate([wo[:512], wo[512:].reshape(2, 4, HD, D).transpose(1, 0, 2, 3)
                                          .reshape(512, D)], axis=0)))
    parts += [ffn(0, 1), ffn(1, 0), tiles_of(f["od_w_in_2"][0])]
    glu = f["s5_w_glu_2"][0]
    ab = np.stack([tiles_of(glu[:, :512]), tiles_of(glu[:, 512:])], axis=2)
    parts += [ab.reshape(4, P, D), tiles_of(f["od_w_out_2"][0]), ffn(1, 1)]
    out = {"stream": np.concatenate(parts, axis=0)}

    def cols(v):
        return np.asarray(v).reshape(-1, P).T
    vectors = {"c": cols(f["c"]), "ada_b": cols(f["ada_b"]), "norm1_g": cols(f["norm1_g"]), "mu_prev": cols(f["mu_prev"]),
               "mu_next": cols(f["mu_next"]), "w_decay0": cols(f["w_decay0"]), "a_gate0": cols(f["a_gate0"]),
               "k_k": cols(f["k_k"]), "k_a": cols(f["k_a"]), "r_k": cols(f["r_k"]), "lnx_g": cols(f["lnx_g"]),
               "lnx_b": cols(f["lnx_b"]), "norm2_g": cols(f["norm2_g"]), "q_norm_g": cols(np.tile(f["q_norm_g"][0], 2)),
               "k_norm_g": cols(np.tile(f["k_norm_g"][0], 2)), "norm_w": cols(f["norm_w_2"]),
               "final": cols(f["final_norm_w_2"]), "pool_scale": cols(f["pool_scale_2"]), "s5_d": cols(f["s5_d_2"]),
               "lam_re": cols(f["s5_lam_re_2"]), "lam_im": cols(f["s5_lam_im_2"]),
               "log_dt": cols(np.repeat(f["s5_log_dt_2"][0], 64))}
    out["vecs"] = np.concatenate([vectors[n] for n in VEC], axis=1)
    out["xT"] = f["x"][0].T
    out["mats"] = constant_matrices()
    out["lora_up"] = np.concatenate([f["w_decay_up"][0].transpose(1, 0, 2), f["a_gate_up"][0].transpose(1, 0, 2)], 0)
    out["g_up"] = f["g_up"][0]
    out["subkeys"] = np.stack([f["peer_sub_keys1"][0].T, f["peer_sub_keys2"][0].T], axis=1)
    out["peer_u"], out["peer_v"] = f["peer_u"][0], f["peer_v"][0]
    out["gm_w"] = f["gm_w_s_2"][0].transpose(2, 0, 1)
    out["gm_b"] = np.repeat(f["gm_b_2"][0].reshape(4, 2, P), HD, axis=1).transpose(1, 0, 2)
    out["cmp_w1"] = np.tile(f["nsa_cmp_w1_2"][0].reshape(2, 32, HD, HD).transpose(2, 0, 1, 3), (2, 1, 1, 1))
    out["cmp_w2"] = np.tile(f["nsa_cmp_w2_2"][0].transpose(1, 0, 2), (2, 1, 1))
    out["pe_cmp"] = np.tile(f["nsa_cmp_pe_2"][0].transpose(2, 0, 1), (2, 1, 1))
    out["pool_w"] = f["pool_w_2"][0]
    b = np.zeros((4, 4, 2, 16, 2, 2, 64), np.float32)
    c = np.zeros((2, 64, 2, S5T, 2, 16), np.float32)
    for i, (bb, cc) in enumerate(((f["s5_b_re_2"][0], f["s5_c_re_2"][0]), (f["s5_b_im_2"][0], f["s5_c_im_2"][0]))):
        bb = bb.reshape(4, 4, 2, 64, 16)
        cc = cc.reshape(S5T, 2, 16, 64)
        for g in range(2):
            b[:, :, g, :, i, g, :] = bb[:, :, g].transpose(0, 1, 3, 2)
            c[g, :, i, :, g, :] = cc[:, g].transpose(2, 0, 1)
    out["s5_b"] = b.reshape(4, P, 2, P).transpose(1, 0, 2, 3)
    out["s5_c"] = c.reshape(P, 2, S5T, 32)

    t = np.arange(S)
    dist = np.abs(t[:, None] - t[None, :])
    patterns = ((128, 1), (512, 4), (2048, 16))
    seen = sum(((dist % d == 0) & (dist <= w // 2)).astype(np.float32) for w, d in patterns)
    slopes = np.exp2(-8.0 * (np.arange(NH, dtype=np.float32) + 1) / NH).astype(np.float32)
    logs = np.where(seen > 0, np.log(np.maximum(seen, 1)), NEG).astype(np.float32)
    out["attn_bias"] = (logs[None] - slopes[:, None, None] * dist[None].astype(np.float32)).astype(np.float32)
    out["causal"] = np.where(t[None, :] <= t[:, None], 0, NEG).astype(np.float32).reshape(TT, P, S).transpose(1, 0, 2)
    end = np.arange(NC_CMP) * 16 + 31
    valid = end[None, :] <= t[:, None]
    out["cmp_mask"] = np.where(valid, 0, NEG).astype(np.float32).reshape(TT, P, NC_CMP).transpose(1, 0, 2)
    out["any_cmp"] = valid.any(axis=1).astype(np.float32).reshape(TT, P).T
    half = HD // 2
    inv = np.float32(10000.0) ** (-np.arange(half, dtype=np.float32) / half)
    for pos, tag in ((t, ""), (end, "c")):
        ang = pos.astype(np.float32)[None, :] * np.tile(inv, 4)[:, None]
        out["cos" + tag], out["sin" + tag] = np.cos(ang).astype(np.float32), np.sin(ang).astype(np.float32)
    counts = np.minimum(t[None, :] + 1, np.array([2, 4, 8, 16])[:, None]).astype(np.float32)
    out["inv_count"] = np.broadcast_to((1 / counts).astype(np.float32), (P, 4, S))
    return {k: np.ascontiguousarray(v) for k, v in out.items()}


def kernel(**inputs):
    import concourse.bacc as bacc
    from concourse.bass_utils import run_bass_kernel_spmd

    nc = bacc.Bacc("TRN2", target_bir_lowering=False, num_devices=1)
    arrays = {"in_" + k: v for k, v in layout(inputs).items()}
    aps = {k[3:]: nc.dram_tensor(k, v.shape, F32, kind="ExternalInput").ap() for k, v in arrays.items()}
    aps["out"] = nc.dram_tensor("out_xT", (D, S), F32, kind="ExternalOutput").ap()
    build(nc, aps)
    result = run_bass_kernel_spmd(nc, [arrays], core_ids=[0]).results[0]["out_xT"]
    return np.ascontiguousarray(np.asarray(result).T).reshape(1, S, D)
```
